# Optimizing a Trainium2 kernel written in Bass

```python
import jax, jax.numpy as jnp
from jax import lax
import numpy as np

D_MODEL = 1024
BATCH = 1
SEQ = 256
DEPTH = 2

CHUNK = 64
N_A_LAYERS = DEPTH // 2
N_B_LAYERS = DEPTH - N_A_LAYERS
EPS = 1e-6

MA_HEADS = 8
MA_QK = 64
MA_V = D_MODEL // MA_HEADS
MA_CONV = 4
MA_QK_COLS = 2 * MA_HEADS * MA_QK
MA_PROJ = MA_QK_COLS + 2 * D_MODEL + 2 * MA_HEADS

SB_HEADS = 16
SB_DIM = D_MODEL // SB_HEADS
SB_BLOCK = 128

PEER_HEADS = 8
PEER_NKEYS = 128
PEER_EXPERTS = PEER_NKEYS * PEER_NKEYS
PEER_QDIM = 256
PEER_TOPK = 16
PEER_BLOCK = 128


def rmsnorm(x, g):
    xf = x.astype(jnp.float32)
    y = xf * lax.rsqrt(jnp.mean(xf * xf, axis=-1, keepdims=True) + EPS)
    return (y * g.astype(jnp.float32)).astype(x.dtype)

def ada_mod(c, w, b):
    return jnp.einsum('bd,de->be', jax.nn.silu(c), w) + b

def modulate(h, shift, scale):
    return h * (1.0 + scale[:, None, :]) + shift[:, None, :]

def causal_conv(x, w):
    width, ch = w.shape
    return lax.conv_general_dilated(x, w[:, None, :], window_strides=(1,), padding=[(width - 1, 0)],
                                    dimension_numbers=('NWC', 'WIO', 'NWC'), feature_group_count=ch)

def mlstm_mixer(h, w_in, conv_w, b_if, hnorm_g, w_out):
    bsz, seq, _ = h.shape
    nc = seq // CHUNK
    proj = jnp.einsum('bsd,de->bse', h, w_in)
    qk, v, o, gates = jnp.split(proj, [MA_QK_COLS, MA_QK_COLS + D_MODEL, MA_QK_COLS + 2 * D_MODEL], axis=-1)
    qk = jax.nn.silu(causal_conv(qk, conv_w))
    q, k = jnp.split(qk, 2, axis=-1)
    gates = (gates + b_if).astype(jnp.float32)
    i_pre, f_pre = jnp.split(gates, 2, axis=-1)

    def to_chunks(t, d):
        return t.reshape(bsz, nc, CHUNK, MA_HEADS, d).transpose(0, 3, 1, 2, 4)

    q = to_chunks(q, MA_QK).astype(jnp.float32) * (MA_QK ** -0.5)
    k = to_chunks(k, MA_QK).astype(jnp.float32)
    v = to_chunks(v, MA_V).astype(jnp.float32)
    i_pre = i_pre.reshape(bsz, nc, CHUNK, MA_HEADS).transpose(0, 3, 1, 2)
    log_f = jax.nn.log_sigmoid(f_pre).reshape(bsz, nc, CHUNK, MA_HEADS).transpose(0, 3, 1, 2)
    b = jnp.cumsum(log_f, axis=-1)
    b_last = b[..., -1]

    w_state = b_last[..., None] - b + i_pre
    m_loc = jnp.max(w_state, axis=-1)
    e_state = jnp.exp(w_state - m_loc[..., None])
    c_loc = jnp.einsum('bhcl,bhclv,bhclk->bhcvk', e_state, v, k)
    n_loc = jnp.einsum('bhcl,bhclk->bhck', e_state, k)

    def step(carry, inp):
        c_st, n_st, m_st = carry
        cl, nl, ml, bl = inp
        m_new = jnp.maximum(bl + m_st, ml)
        a = jnp.exp(bl + m_st - m_new)
        r = jnp.exp(ml - m_new)
        c_new = a[..., None, None] * c_st + r[..., None, None] * cl
        n_new = a[..., None] * n_st + r[..., None] * nl
        return (c_new, n_new, m_new), (c_st, n_st, m_st)

    init = (jnp.zeros((bsz, MA_HEADS, MA_V, MA_QK), jnp.float32),
            jnp.zeros((bsz, MA_HEADS, MA_QK), jnp.float32),
            jnp.zeros((bsz, MA_HEADS), jnp.float32))
    xs = (c_loc.transpose(2, 0, 1, 3, 4), n_loc.transpose(2, 0, 1, 3),
          m_loc.transpose(2, 0, 1), b_last.transpose(2, 0, 1))
    _, (c_prev, n_prev, m_prev) = lax.scan(step, init, xs)
    c_prev = c_prev.transpose(1, 2, 0, 3, 4)
    n_prev = n_prev.transpose(1, 2, 0, 3)
    m_prev = m_prev.transpose(1, 2, 0)

    causal = jnp.tril(jnp.ones((CHUNK, CHUNK), dtype=bool))
    log_d = jnp.where(causal, b[..., :, None] - b[..., None, :] + i_pre[..., None, :], -jnp.inf)
    inter_log = b + m_prev[..., None]
    m_t = jnp.maximum(inter_log, jnp.max(log_d, axis=-1))
    inter_w = jnp.exp(inter_log - m_t)
    s_qk = jnp.einsum('bhcld,bhcsd->bhcls', q, k) * jnp.exp(log_d - m_t[..., None])
    num = jnp.einsum('bhcls,bhcsv->bhclv', s_qk, v) + inter_w[..., None] * jnp.einsum('bhcvk,bhclk->bhclv', c_prev, q)
    den = jnp.sum(s_qk, axis=-1) + inter_w * jnp.einsum('bhck,bhclk->bhcl', n_prev, q)
    hh = num / jnp.maximum(jnp.abs(den), jnp.exp(-m_t))[..., None]
    hh = hh.transpose(0, 2, 3, 1, 4).reshape(bsz, seq, MA_HEADS, MA_V)
    hh = rmsnorm(hh, hnorm_g) * jax.nn.sigmoid(o.astype(jnp.float32)).reshape(bsz, seq, MA_HEADS, MA_V)
    return jnp.einsum('bse,ed->bsd', hh.reshape(bsz, seq, D_MODEL).astype(h.dtype), w_out)

def shared_kv(x, c, kv_ada_w, kv_ada_b, kv_norm_g, kv_w, k_norm_g):
    bsz, seq, _ = x.shape
    shift, scale = jnp.split(ada_mod(c, kv_ada_w, kv_ada_b), 2, axis=-1)
    h = modulate(rmsnorm(x, kv_norm_g), shift, scale)
    kv = jnp.einsum('bsd,de->bse', h, kv_w)
    k, v = jnp.split(kv, 2, axis=-1)
    k = rmsnorm(k.reshape(bsz, seq, SB_HEADS, SB_DIM), k_norm_g).transpose(0, 2, 1, 3)
    v = v.reshape(bsz, seq, SB_HEADS, SB_DIM).transpose(0, 2, 1, 3)
    return k, v

def stick_breaking_mixer(h, k, v, w_q, q_norm_g, w_out):
    bsz, seq, _ = h.shape
    q = jnp.einsum('bsd,de->bse', h, w_q).reshape(bsz, seq, SB_HEADS, SB_DIM)
    q = (rmsnorm(q, q_norm_g) * (SB_DIM ** -0.5)).transpose(0, 2, 1, 3)
    outs = []
    for blk in range(seq // SB_BLOCK):
        t0 = blk * SB_BLOCK
        end = t0 + SB_BLOCK
        z = jnp.einsum('bhtd,bhsd->bhts', q[:, :, t0:end], k[:, :, :end]).astype(jnp.float32)
        strict = jnp.arange(end)[None, :] < (t0 + jnp.arange(SB_BLOCK))[:, None]
        log1m = jnp.where(strict, -jax.nn.softplus(z), 0.0)
        between = lax.cumsum(log1m, axis=3, reverse=True) - log1m
        a = jnp.where(strict, jnp.exp(jax.nn.log_sigmoid(z) + between), 0.0)
        outs.append(jnp.einsum('bhts,bhsd->bhtd', a, v[:, :, :end].astype(jnp.float32)))
    o = jnp.concatenate(outs, axis=2).transpose(0, 2, 1, 3).reshape(bsz, seq, D_MODEL)
    return jnp.einsum('bse,ed->bsd', o.astype(h.dtype), w_out)

def peer_ffn(h, w_q, sub_keys, peer_u, peer_v):
    bsz, seq, d = h.shape
    xt = h.reshape(bsz * seq // PEER_BLOCK, PEER_BLOCK, d)

    def block(xb):
        q = jnp.einsum('td,de->te', xb, w_q).reshape(PEER_BLOCK, PEER_HEADS, 2, PEER_QDIM // 2)
        s = jnp.einsum('thpk,pnk->thpn', q, sub_keys).astype(jnp.float32)
        s_top, i_top = lax.top_k(s, PEER_TOPK)
        cand = (s_top[:, :, 0, :, None] + s_top[:, :, 1, None, :]).reshape(PEER_BLOCK, PEER_HEADS, PEER_TOPK * PEER_TOPK)
        cand_idx = (i_top[:, :, 0, :, None] * PEER_NKEYS + i_top[:, :, 1, None, :]).reshape(PEER_BLOCK, PEER_HEADS, PEER_TOPK * PEER_TOPK)
        g_top, pos = lax.top_k(cand, PEER_TOPK)
        expert = jnp.take_along_axis(cand_idx, pos, axis=-1)
        g = jax.nn.softmax(g_top, axis=-1)
        u = jnp.take(peer_u, expert, axis=0)
        act = jax.nn.gelu(jnp.einsum('thkd,td->thk', u, xb).astype(jnp.float32), approximate=False)
        vv = jnp.take(peer_v, expert, axis=0)
        return jnp.einsum('thk,thkd->td', (g * act).astype(xb.dtype), vv)

    return lax.map(block, xt).reshape(bsz, seq, d)

def first_inputs(seed: int = 0) -> dict:
    key = jax.random.key(seed)
    ks = jax.random.split(key, 24)
    f32 = jnp.float32
    d = D_MODEL

    def nrm(k, shape, scale):
        return jax.random.normal(k, shape, f32) * scale

    def gain(k, shape):
        return 1.0 + 0.02 * jax.random.normal(k, shape, f32)

    if_base = jnp.concatenate([jnp.zeros((MA_HEADS,), f32), jnp.linspace(3.0, 6.0, MA_HEADS, dtype=f32)])
    return {
        'x': nrm(ks[0], (BATCH, SEQ, d), 1.0),
        'c': nrm(ks[1], (BATCH, d), 1.0),
        'ada_w': nrm(ks[2], (DEPTH, d, 6 * d), 0.5 * d ** -0.5),
        'ada_b': nrm(ks[3], (DEPTH, 6 * d), 0.01),
        'norm_mix_g': gain(ks[4], (DEPTH, d)),
        'norm_ffn_g': gain(ks[5], (DEPTH, d)),
        'ma_w_in': nrm(ks[6], (N_A_LAYERS, d, MA_PROJ), d ** -0.5),
        'ma_conv_w': nrm(ks[7], (N_A_LAYERS, MA_CONV, MA_QK_COLS), MA_CONV ** -0.5),
        'ma_b_if': if_base + nrm(ks[8], (N_A_LAYERS, 2 * MA_HEADS), 0.1),
        'ma_hnorm_g': gain(ks[9], (N_A_LAYERS, MA_HEADS, MA_V)),
        'ma_w_out': nrm(ks[10], (N_A_LAYERS, d, d), d ** -0.5),
        'kv_ada_w': nrm(ks[11], (d, 2 * d), 0.5 * d ** -0.5),
        'kv_ada_b': nrm(ks[12], (2 * d,), 0.01),
        'kv_norm_g': gain(ks[13], (d,)),
        'kv_w': nrm(ks[14], (d, 2 * d), d ** -0.5),
        'k_norm_g': gain(ks[15], (SB_DIM,)),
        'sb_w_q': nrm(ks[16], (N_B_LAYERS, d, d), d ** -0.5),
        'sb_q_norm_g': gain(ks[17], (N_B_LAYERS, SB_DIM)),
        'sb_w_out': nrm(ks[18], (N_B_LAYERS, d, d), d ** -0.5),
        'peer_w_q': nrm(ks[19], (DEPTH, d, PEER_HEADS * PEER_QDIM), d ** -0.5),
        'peer_sub_keys': nrm(ks[20], (DEPTH, 2, PEER_NKEYS, PEER_QDIM // 2), (PEER_QDIM // 2) ** -0.5),
        'peer_u': nrm(ks[21], (DEPTH, PEER_EXPERTS, d), d ** -0.5),
        'peer_v': nrm(ks[22], (DEPTH, PEER_EXPERTS, d), PEER_HEADS ** -0.5),
    }

def first_block(x, c, ada_w, ada_b, norm_mix_g, norm_ffn_g, ma_w_in, ma_conv_w, ma_b_if, ma_hnorm_g, ma_w_out,
              kv_ada_w, kv_ada_b, kv_norm_g, kv_w, k_norm_g, sb_w_q, sb_q_norm_g, sb_w_out,
              peer_w_q, peer_sub_keys, peer_u, peer_v):
    k_sh = None
    v_sh = None
    for layer in range(DEPTH):
        sh1, sc1, g1, sh2, sc2, g2 = jnp.split(ada_mod(c, ada_w[layer], ada_b[layer]), 6, axis=-1)
        h = modulate(rmsnorm(x, norm_mix_g[layer]), sh1, sc1)
        if layer < N_A_LAYERS:
            y = mlstm_mixer(h, ma_w_in[layer], ma_conv_w[layer], ma_b_if[layer], ma_hnorm_g[layer], ma_w_out[layer])
        else:
            if layer == N_A_LAYERS:
                k_sh, v_sh = shared_kv(x, c, kv_ada_w, kv_ada_b, kv_norm_g, kv_w, k_norm_g)
            j = layer - N_A_LAYERS
            y = stick_breaking_mixer(h, k_sh, v_sh, sb_w_q[j], sb_q_norm_g[j], sb_w_out[j])
        x = x + g1[:, None, :] * y
        h = modulate(rmsnorm(x, norm_ffn_g[layer]), sh2, sc2)
        x = x + g2[:, None, :] * peer_ffn(h, peer_w_q[layer], peer_sub_keys[layer], peer_u[layer], peer_v[layer])
    return x


PLE_DIM = 256
N_MIXERS = 2
D_FF = 2816
FFN_HALF = 0.5
MLA_HEADS = 16
MLA_Q_RANK = 512
MLA_KV_RANK = 256
MLA_NOPE = 64
MLA_ROPE = 32
MLA_V = 64
ROPE_THETA = 10000.0
FOX_HEADS = 16
FOX_HEAD_DIM = 64
Q_BLOCK = 128
N_MLA_LAYERS = (DEPTH + N_MIXERS - 1) // N_MIXERS
N_FOX_LAYERS = DEPTH // N_MIXERS


def rms_norm(x, g):
    xf = x.astype(jnp.float32)
    y = xf * lax.rsqrt(jnp.mean(xf * xf, axis=-1, keepdims=True) + EPS)
    return (y * g.astype(jnp.float32)).astype(x.dtype)

def swiglu(x, w_in, w_out):
    gate, up = jnp.split(x @ w_in, 2, axis=-1)
    return (jax.nn.silu(gate) * up) @ w_out

def rope(x, pos):
    r = x.shape[-1]
    inv_freq = ROPE_THETA ** (-jnp.arange(0, r, 2, dtype=jnp.float32) / r)
    ang = pos.astype(jnp.float32)[:, :, None, None] * inv_freq
    cos = jnp.cos(ang).astype(x.dtype)
    sin = jnp.sin(ang).astype(x.dtype)
    x1, x2 = jnp.split(x, 2, axis=-1)
    return jnp.concatenate([x1 * cos - x2 * sin, x1 * sin + x2 * cos], axis=-1)

def block_causal_attention(q, k, v, decay=None):
    b, s, h, dk = q.shape
    dv = v.shape[-1]
    nb = s // Q_BLOCK
    scale = dk ** -0.5
    qb = q.reshape(b, nb, Q_BLOCK, h, dk).transpose(1, 0, 2, 3, 4)
    blk = jnp.arange(nb)
    k_pos = jnp.arange(s)
    c_k = None if decay is None else decay.transpose(0, 2, 1)

    def attend(qi, i, c_qi):
        logits = jnp.einsum('bqhd,bkhd->bhqk', qi, k).astype(jnp.float32) * scale
        if c_qi is not None:
            logits = logits + c_qi[:, :, :, None] - c_k[:, :, None, :]
        q_pos = i * Q_BLOCK + jnp.arange(Q_BLOCK)
        mask = k_pos[None, :] <= q_pos[:, None]
        logits = jnp.where(mask[None, None], logits, -jnp.inf)
        probs = jax.nn.softmax(logits, axis=-1)
        return jnp.einsum('bhqk,bkhd->bqhd', probs.astype(v.dtype), v)

    if decay is None:
        out = lax.map(lambda a: attend(a[0], a[1], None), (qb, blk))
    else:
        c_qb = decay.reshape(b, nb, Q_BLOCK, h).transpose(1, 0, 3, 2)
        out = lax.map(lambda a: attend(a[0], a[1], a[2]), (qb, blk, c_qb))
    return out.transpose(1, 0, 2, 3, 4).reshape(b, s, h, dv)

def mla_mixer(hn, pos, w_in, g_q_lat, w_uq, g_kv_lat, w_ukv, g_qn, g_kn, w_o):
    b, s, _ = hn.shape
    z = hn @ w_in
    c_q = z[..., :MLA_Q_RANK]
    c_kv = z[..., MLA_Q_RANK:MLA_Q_RANK + MLA_KV_RANK]
    k_pe = z[..., MLA_Q_RANK + MLA_KV_RANK:]
    q = (rms_norm(c_q, g_q_lat) @ w_uq).reshape(b, s, MLA_HEADS, MLA_NOPE + MLA_ROPE)
    kv = (rms_norm(c_kv, g_kv_lat) @ w_ukv).reshape(b, s, MLA_HEADS, MLA_NOPE + MLA_V)
    k_nope, v = kv[..., :MLA_NOPE], kv[..., MLA_NOPE:]
    k_pe_h = jnp.broadcast_to(k_pe[:, :, None, :], (b, s, MLA_HEADS, MLA_ROPE))
    k = jnp.concatenate([k_nope, k_pe_h], axis=-1)
    q = rms_norm(q, g_qn)
    k = rms_norm(k, g_kn)
    q = jnp.concatenate([q[..., :MLA_NOPE], rope(q[..., MLA_NOPE:], pos)], axis=-1)
    k = jnp.concatenate([k[..., :MLA_NOPE], rope(k[..., MLA_NOPE:], pos)], axis=-1)
    o = block_causal_attention(q, k, v)
    return o.reshape(b, s, MLA_HEADS * MLA_V) @ w_o

def fox_mixer(hn, w_in, b_f, g_qn, g_kn, w_o):
    b, s, _ = hn.shape
    hd = FOX_HEADS * FOX_HEAD_DIM
    z = hn @ w_in
    q = z[..., :hd].reshape(b, s, FOX_HEADS, FOX_HEAD_DIM)
    k = z[..., hd:2 * hd].reshape(b, s, FOX_HEADS, FOX_HEAD_DIM)
    v = z[..., 2 * hd:3 * hd].reshape(b, s, FOX_HEADS, FOX_HEAD_DIM)
    f_logit = z[..., 3 * hd:].astype(jnp.float32) + b_f.astype(jnp.float32)
    log_f = jax.nn.log_sigmoid(f_logit)
    decay = jnp.cumsum(log_f, axis=1)
    q = rms_norm(q, g_qn)
    k = rms_norm(k, g_kn)
    o = block_causal_attention(q, k, v, decay)
    return o.reshape(b, s, hd) @ w_o

def second_inputs(seed: int = 0) -> dict:
    key = jax.random.key(seed)
    ks = iter(jax.random.split(key, 40))

    def dense(shape, fan_in):
        return jax.random.normal(next(ks), shape, jnp.float32) * (fan_in ** -0.5)

    def gain(shape):
        return 1.0 + 0.1 * jax.random.normal(next(ks), shape, jnp.float32)

    x = jax.random.normal(next(ks), (BATCH, SEQ, D_MODEL), jnp.float32)
    p = jax.random.normal(next(ks), (DEPTH, BATCH, SEQ, PLE_DIM), jnp.float32)
    positions = jnp.broadcast_to(jnp.arange(SEQ, dtype=jnp.int32), (BATCH, SEQ))
    na, nf = N_MLA_LAYERS, N_FOX_LAYERS
    fox_in = 3 * FOX_HEADS * FOX_HEAD_DIM + FOX_HEADS
    return {
        "x": x,
        "p": p,
        "positions": positions,
        "g_ffn1": gain((DEPTH, D_MODEL)),
        "g_mix": gain((DEPTH, D_MODEL)),
        "g_ffn2": gain((DEPTH, D_MODEL)),
        "g_ple": gain((DEPTH, D_MODEL)),
        "ffn1_w_in": dense((DEPTH, D_MODEL, 2 * D_FF), D_MODEL),
        "ffn1_w_out": dense((DEPTH, D_FF, D_MODEL), D_FF),
        "ffn2_w_in": dense((DEPTH, D_MODEL, 2 * D_FF), D_MODEL),
        "ffn2_w_out": dense((DEPTH, D_FF, D_MODEL), D_FF),
        "ple_w_proj": dense((DEPTH, PLE_DIM, D_MODEL), PLE_DIM),
        "ple_w_gate": dense((DEPTH, D_MODEL, D_MODEL), D_MODEL),
        "mla_w_in": dense((na, D_MODEL, MLA_Q_RANK + MLA_KV_RANK + MLA_ROPE), D_MODEL),
        "mla_g_q_lat": gain((na, MLA_Q_RANK)),
        "mla_w_uq": dense((na, MLA_Q_RANK, MLA_HEADS * (MLA_NOPE + MLA_ROPE)), MLA_Q_RANK),
        "mla_g_kv_lat": gain((na, MLA_KV_RANK)),
        "mla_w_ukv": dense((na, MLA_KV_RANK, MLA_HEADS * (MLA_NOPE + MLA_V)), MLA_KV_RANK),
        "mla_g_qn": gain((na, MLA_NOPE + MLA_ROPE)),
        "mla_g_kn": gain((na, MLA_NOPE + MLA_ROPE)),
        "mla_w_o": dense((na, MLA_HEADS * MLA_V, D_MODEL), MLA_HEADS * MLA_V),
        "fox_w_in": dense((nf, D_MODEL, fox_in), D_MODEL),
        "fox_b_f": jax.random.uniform(next(ks), (nf, FOX_HEADS), jnp.float32, 1.0, 4.0),
        "fox_g_qn": gain((nf, FOX_HEAD_DIM)),
        "fox_g_kn": gain((nf, FOX_HEAD_DIM)),
        "fox_w_o": dense((nf, FOX_HEADS * FOX_HEAD_DIM, D_MODEL), FOX_HEADS * FOX_HEAD_DIM),
    }

def second_block(x, p, positions, g_ffn1, g_mix, g_ffn2, g_ple,
              ffn1_w_in, ffn1_w_out, ffn2_w_in, ffn2_w_out, ple_w_proj, ple_w_gate,
              mla_w_in, mla_g_q_lat, mla_w_uq, mla_g_kv_lat, mla_w_ukv,
              mla_g_qn, mla_g_kn, mla_w_o,
              fox_w_in, fox_b_f, fox_g_qn, fox_g_kn, fox_w_o):
    h = x
    for i in range(DEPTH):
        h = h + FFN_HALF * swiglu(rms_norm(h, g_ffn1[i]), ffn1_w_in[i], ffn1_w_out[i])
        hn = rms_norm(h, g_mix[i])
        j = i // N_MIXERS
        if i % N_MIXERS == 0:
            h = h + mla_mixer(hn, positions, mla_w_in[j], mla_g_q_lat[j], mla_w_uq[j],
                              mla_g_kv_lat[j], mla_w_ukv[j], mla_g_qn[j], mla_g_kn[j],
                              mla_w_o[j])
        else:
            h = h + fox_mixer(hn, fox_w_in[j], fox_b_f[j], fox_g_qn[j], fox_g_kn[j],
                              fox_w_o[j])
        h = h + FFN_HALF * swiglu(rms_norm(h, g_ffn2[i]), ffn2_w_in[i], ffn2_w_out[i])
        gate = jax.nn.sigmoid(rms_norm(h, g_ple[i]) @ ple_w_gate[i])
        h = h + gate * (p[i] @ ple_w_proj[i])
    return h


def setup_inputs(seed=0):
    out = dict(first_inputs(seed))
    for name, value in second_inputs(seed + 1).items():
        if name != "x":
            out[name + "_2"] = value
    return out


def reference(
    x, c, ada_w, ada_b, norm_mix_g, norm_ffn_g, ma_w_in, ma_conv_w, ma_b_if, ma_hnorm_g,
    ma_w_out, kv_ada_w, kv_ada_b, kv_norm_g, kv_w, k_norm_g, sb_w_q, sb_q_norm_g, sb_w_out,
    peer_w_q, peer_sub_keys, peer_u, peer_v, p_2, positions_2, g_ffn1_2, g_mix_2, g_ffn2_2,
    g_ple_2, ffn1_w_in_2, ffn1_w_out_2, ffn2_w_in_2, ffn2_w_out_2, ple_w_proj_2, ple_w_gate_2,
    mla_w_in_2, mla_g_q_lat_2, mla_w_uq_2, mla_g_kv_lat_2, mla_w_ukv_2, mla_g_qn_2, mla_g_kn_2,
    mla_w_o_2, fox_w_in_2, fox_b_f_2, fox_g_qn_2, fox_g_kn_2, fox_w_o_2,
):
    x = first_block(
        x, c, ada_w, ada_b, norm_mix_g, norm_ffn_g, ma_w_in, ma_conv_w, ma_b_if, ma_hnorm_g,
        ma_w_out, kv_ada_w, kv_ada_b, kv_norm_g, kv_w, k_norm_g, sb_w_q, sb_q_norm_g, sb_w_out,
        peer_w_q, peer_sub_keys, peer_u, peer_v,
    )
    return second_block(
        x, p_2, positions_2, g_ffn1_2, g_mix_2, g_ffn2_2, g_ple_2, ffn1_w_in_2, ffn1_w_out_2,
        ffn2_w_in_2, ffn2_w_out_2, ple_w_proj_2, ple_w_gate_2, mla_w_in_2, mla_g_q_lat_2,
        mla_w_uq_2, mla_g_kv_lat_2, mla_w_ukv_2, mla_g_qn_2, mla_g_kn_2, mla_w_o_2, fox_w_in_2,
        fox_b_f_2, fox_g_qn_2, fox_g_kn_2, fox_w_o_2,
    )


_drawn_inputs = setup_inputs


def setup_inputs(seed=0):
    import zlib

    import numpy as np

    out = dict(_drawn_inputs(seed))
    spreads = {}
    factors = {'ada_b': 3.315,
     'norm_mix_g': 6.409,
     'norm_ffn_g': 4.495,
     'ma_hnorm_g': 7.991,
     'kv_ada_b': 8.0,
     'kv_norm_g': 8.0,
     'k_norm_g': 8.0,
     'sb_q_norm_g': 8.0,
     'mla_g_q_lat_2': 3.612,
     'mla_g_qn_2': 3.76,
     'mla_g_kn_2': 3.477,
     'fox_g_qn_2': 3.949,
     'fox_g_kn_2': 3.056,
     'g_ple_2': 5.648}
    for name, (base, spread) in spreads.items():
        noise = np.random.default_rng([zlib.crc32(name.encode()), seed]).standard_normal(out[name].shape)
        drawn = base * np.exp(spread * noise) if base else spread * noise
        out[name] = __import__('jax').numpy.asarray(drawn.astype(out[name].dtype))
    for name, factor in factors.items():
        out[name] = (out[name] * factor).astype(out[name].dtype)
    return out
```

```python
import math
from contextlib import ExitStack

import numpy as np

import concourse.bass as bass
from concourse import mybir

F32 = mybir.dt.float32
I32 = mybir.dt.int32
U32 = mybir.dt.uint32
ALU = mybir.AluOpType
ACT = mybir.ActivationFunctionType
AX = mybir.AxisListType

P = 128
S = 256
NT = S // P
D = 1024
KD = D // P
TW = 512
EPS = 1e-6
HUGE = 3.0e38

MH, MQK, MV = 8, 64, 128
SH, SD = 16, 64
PH, PK, PTOP = 8, 128, 16
PSLOTS = PH * PTOP
FF = 2816
FB = FF // P
AH = 16
MLA_Q, MLA_KV, NOPE, ROPE, AV = 512, 256, 64, 32, 64
MLA_D = NOPE + ROPE
FOX_D = 64
HG = 4
RING = 3
SLOT = KD * TW
BATCH = 8


def build(nc, d):
    ctx = ExitStack()
    with ctx:
        def sb(name, shape, dt=F32):
            return ctx.enter_context(nc.sbuf_tensor("sb_" + name, shape, dt))

        def sem(name):
            return ctx.enter_context(nc.semaphore(name))

        X = sb("x", [P, NT, D])
        H = sb("h", [P, NT, D])
        XT = sb("xT", [P, KD, S])
        MOD = sb("mod", [P, 6 * D])
        KVMOD = sb("kvmod", [P, 2 * D])
        GAIN = sb("gain", [P, 2, D])
        W = sb("w", [P, RING, SLOT])
        CB = sb("cb", [P, KD, P])
        ident = sb("ident", [P, P])
        ones = sb("ones", [P, P])
        after = sb("after", [P, P])
        before = sb("before", [P, P])
        upto = sb("upto", [P, P])
        causal = sb("causal", [P, S])
        zrow = sb("zrow", [P, TW])
        iota16 = sb("iota16", [P, 16])
        eps = sb("eps", [P, 1])
        ccol = sb("ccol", [P, KD])
        ss = sb("ss", [P, 32])
        rms = sb("rms", [P, 32])
        rs = sb("rs", [P, 32])
        small = sb("small", [P, 256])
        bias8 = sb("bias8", [16, 2])
        bias16 = sb("bias16", [16, 1])
        posi = sb("posi", [P, NT], I32)
        rope_int = sb("rope_int", [P, NT * ROPE // 2], I32)
        r_freq_own = sb("rope_freq", [P, ROPE // 2])
        ARENA = 20480
        A = sb("arena", [P, ARENA])
        PS = ctx.enter_context(nc.psum_tensor("ps", [P, 8, TW], F32))

        def part(start, *shape):
            n = int(np.prod(shape))
            assert start + n <= ARENA, (start, shape)
            v = A[:, start:start + n]
            if len(shape) == 2:
                v = v.rearrange("p (a b) -> p a b", b=shape[1])
            elif len(shape) == 3:
                v = v.rearrange("p (a b c) -> p a b c", b=shape[1], c=shape[2])
            elif len(shape) == 4:
                v = v.rearrange("p (a b c e) -> p a b c e", b=shape[1], c=shape[2], e=shape[3])
            return v

        def wslot(pos, kc, width):
            return W[:, pos % RING, 0:kc * width].rearrange("p (k n) -> p k n", n=width)

        STAGES = []

        def stage(kind, **kw):
            kw["kind"] = kind
            kw["n"] = len(STAGES)
            STAGES.append(kw)

        gains = []

        def norm(src, width, gain, shift=None, scale=None, dst=None):
            gains.append((gain, width))
            stage("norm", src=src, width=width, gain=len(gains) - 1, shift=shift, scale=scale,
                  dst=dst or (lambda t: H[:, t, 0:width]))

        def turn(jobs):
            stage("turn", jobs=jobs)

        def linear(name, kc, tiles, width, out):
            stage("linear", weights=name, kc=kc, tiles=tiles, width=width, out=out)

        def headnorm(src, heads, hd, gain, factor=1.0, times=None):
            gains.append((gain, heads * hd if times else hd))
            stage("headnorm", src=src, heads=heads, hd=hd, gain=len(gains) - 1, factor=factor, times=times)

        def model_norm(gain, shift=None, scale=None):
            norm(lambda t: X[:, t, :], D, gain, shift, scale)

        def mod(i):
            return MOD[:, i * D:(i + 1) * D]

        def copy_to(dst, width=TW):
            return lambda t, j: ("copy", dst[:, t, j * width:(j + 1) * width])

        def residual(gate):
            return lambda t, j: ("residual", X[:, t, j * TW:(j + 1) * TW],
                                 None if gate is None else gate[:, j * TW:(j + 1) * TW])

        def peer(layer):
            model_norm(f"norm_ffn_g{layer}", mod(3), mod(4))
            stage("linearT", weights=f"peer_w_q{layer}", tiles=4, dst=part(0, 16, S))
            stage("subkeys", layer=layer)
            stage("topk")
            stage("gather", layer=layer)
            stage("mix_in")

        def ffn(name, gain):
            model_norm(gain)
            stage("ffn", weights=name)

        stage("ada", weights="ada_w0", bias="ada_b0", tiles=12, dst=MOD, scales=(1, 4))
        model_norm("norm_mix_g0", mod(0), mod(1))
        m_qk, m_conv = part(0, 8, S), part(2048, 8, S)
        m_v = part(4096, NT, MH, MV + 1)
        m_o = part(6160, NT, D)
        m_h = part(8208, NT, D)
        stage("linearT", weights="ma_w_qk", tiles=2, dst=m_qk)
        stage("linear", weights="ma_w_vo", kc=KD, tiles=4, width=TW,
              out=lambda t, j: ("copy by ACT", m_v[:, t, 4 * j:4 * j + 4, 0:MV]) if j < 2
              else ("sigmoid", m_o[:, t, (j - 2) * TW:(j - 1) * TW]))
        stage("gates", weights="ma_w_g", groups=2, m=MH)
        stage("conv")
        stage("mlstm")
        headnorm(m_h, MH, MV, "ma_hnorm_g", times=m_o)
        turn([(lambda t, k: m_h[:, t, k * P:(k + 1) * P], KD, P, XT)])
        linear("ma_w_out", KD, 2, TW, residual(mod(2)))
        peer(0)

        stage("ada", weights="ada_w1", bias="ada_b1", tiles=12, dst=MOD, scales=(1, 4))
        stage("ada", weights="kv_ada_w", bias="kv_ada_b", tiles=4, dst=KVMOD, scales=(1,))
        s_kv = part(0, NT, 2 * D)
        s_q = part(4096, NT, D)
        s_qT, s_kT = part(6144, SH, S), part(10240, SH, S)
        model_norm("kv_norm_g", KVMOD[:, 0:D], KVMOD[:, D:2 * D])
        linear("kv_w", KD, 4, TW, copy_to(s_kv))
        model_norm("norm_mix_g1", mod(0), mod(1))
        linear("sb_w_q", KD, 2, TW, copy_to(s_q))
        headnorm(s_kv[:, :, 0:D], SH, SD, "k_norm_g")
        headnorm(s_q, SH, SD, "sb_q_norm_g", factor=SD ** -0.5)
        turn([(lambda t, h: s_q[:, t, h * SD:(h + 1) * SD], SH, SD, s_qT),
              (lambda t, h: s_kv[:, t, h * SD:(h + 1) * SD], SH, SD, s_kT)])
        stage("stick", qT=s_qT, kT=s_kT, v=lambda s, h: s_kv[:, s, D + h * SD:D + (h + 1) * SD])
        turn([(lambda t, k: H[:, t, k * P:(k + 1) * P], KD, P, XT)])
        linear("sb_w_out", KD, 2, TW, residual(mod(2)))
        peer(1)

        def embed(i):
            model_norm(f"g_ple{i}")
            e_g, e_p = part(0, NT, D), part(2048, NT, 256)
            linear(f"ple_gate{i}", KD, 2, TW, lambda t, j: ("sigmoid", e_g[:, t, j * TW:(j + 1) * TW]))
            stage("fetch", name=f"p{i}", dst=e_p)
            turn([(lambda t, k: e_p[:, t, k * P:(k + 1) * P], 2, P, XT)])
            linear(f"ple_proj{i}", 2, 2, TW,
                   lambda t, j: ("residual", X[:, t, j * TW:(j + 1) * TW], e_g[:, t, j * TW:(j + 1) * TW]))

        ffn("ffn1_0", "g_ffn1_0")
        model_norm("g_mix_0")
        a_z = part(0, NT, 800)
        a_kv = part(1600, NT, 2 * D)
        a_q = part(5696, NT, AH * MLA_D)
        a_k = part(8768, NT, AH * MLA_D)
        a_qT, a_kT = part(11840, AH, S), part(15936, AH, S)
        linear("mla_w_in", KD, 2, 400, copy_to(a_z, 400))
        norm(lambda t: a_z[:, t, 0:MLA_Q], MLA_Q, "mla_g_q_lat")
        linear("mla_w_uq", MLA_Q // P, 3, TW, copy_to(a_q))
        norm(lambda t: a_z[:, t, MLA_Q:MLA_Q + MLA_KV], MLA_KV, "mla_g_kv_lat")
        linear("mla_w_ukv", MLA_KV // P, 4, TW, copy_to(a_kv))
        stage("mla_keys", z=a_z, kv=a_kv, k=a_k)
        headnorm(a_q, AH, MLA_D, "mla_g_qn", factor=MLA_D ** -0.5)
        headnorm(a_k, AH, MLA_D, "mla_g_kn")
        stage("rope", parts=(a_q, a_k))
        turn([(lambda t, h: a_q[:, t, h * MLA_D:(h + 1) * MLA_D], AH, MLA_D, a_qT),
              (lambda t, h: a_k[:, t, h * MLA_D:(h + 1) * MLA_D], AH, MLA_D, a_kT)])
        stage("softmax", qT=a_qT, kT=a_kT, dk=MLA_D, decay=False, work=5696,
              v=lambda s, h: a_kv[:, s, h * 2 * AV + AV:(h + 1) * 2 * AV])
        turn([(lambda t, k: H[:, t, k * P:(k + 1) * P], KD, P, XT)])
        linear("mla_w_o", KD, 2, TW, residual(None))
        ffn("ffn2_0", "g_ffn2_0")
        embed(0)

        ffn("ffn1_1", "g_ffn1_1")
        model_norm("g_mix_1")
        f_z = part(0, NT, 3 * D)
        f_qT, f_kT = part(6144, AH, S), part(10240, AH, S)
        linear("fox_w_in", KD, 6, TW, copy_to(f_z))
        stage("gates", weights="fox_w_g", groups=1, m=AH)
        headnorm(f_z[:, :, 0:D], AH, FOX_D, "fox_g_qn", factor=FOX_D ** -0.5)
        headnorm(f_z[:, :, D:2 * D], AH, FOX_D, "fox_g_kn")
        turn([(lambda t, h: f_z[:, t, h * FOX_D:(h + 1) * FOX_D], AH, FOX_D, f_qT),
              (lambda t, h: f_z[:, t, D + h * FOX_D:D + (h + 1) * FOX_D], AH, FOX_D, f_kT)])
        stage("softmax", qT=f_qT, kT=f_kT, dk=FOX_D, decay=True, work=14336,
              v=lambda s, h: f_z[:, s, 2 * D + h * FOX_D:2 * D + (h + 1) * FOX_D])
        turn([(lambda t, k: H[:, t, k * P:(k + 1) * P], KD, P, XT)])
        linear("fox_w_o", KD, 2, TW, residual(None))
        ffn("ffn2_1", "g_ffn2_1")
        embed(1)

        stage_done = sem("stage_done")
        consts_ready = sem("consts_ready")
        inputs_loaded = sem("inputs_loaded")
        gain_loaded = [sem("gain_loaded0"), sem("gain_loaded1")]
        bias_loaded = sem("bias_loaded")
        fetched = sem("fetched")
        stored = sem("stored")
        w_loaded = [sem(f"w_loaded{q}") for q in range(RING)]
        tile_used = sem("tile_used")
        names = ["bank_ready", "bank_free0", "bank_free1", "rms_ready", "h_ready", "sq_ready", "sum_ready",
                 "turned", "turned_taken0", "turned_taken1",
                 "gates_in", "log_in", "log_out", "scan_ready", "rowsT_ready", "rows_taken", "floor_ready",
                 "decay_spread", "exponent_ready", "exp_ready", "scores_ready", "probs_ready", "pv_ready",
                 "pv_taken", "soft_ready", "between_ready", "max_ready", "probsT_ready",
                 "probsT_taken0", "probsT_taken1", "conv_ready",
                 "hidden_silu", "hidden_ready", "gu_ready",
                 "angles_ready", "sines_ready", "top_shifted", "top_exp",
                 "expert_free", "mix_free", "dots_ready", "gelu_ready", "weights_ready", "diag_ready",
                 "claimed", "indices_staged", "mixed"]
        SEM = {n: sem(n) for n in names}
        u_loaded = [sem(f"u_loaded{q}") for q in range(BATCH)]
        v_loaded = [sem(f"v_loaded{q}") for q in range(BATCH)]

        BANK_PAIRS = 3

        def counts(st):
            k = st["kind"]
            c = {}
            if k == "ada":
                c = dict(bank_free0=st["tiles"])
            elif k == "linear":
                c = dict(bank_ready=st["tiles"], bank_free0=st["tiles"], bank_free1=st["tiles"])
            elif k == "linearT":
                c = dict(bank_ready=3 * st["tiles"], turned_taken0=2 * st["tiles"], turned_taken1=2 * st["tiles"])
            elif k == "gates":
                c = dict(gates_in=1, log_in=1, log_out=1)
                if st["groups"] == 2:
                    c.update(scan_ready=1, rowsT_ready=1, rows_taken=1, floor_ready=1)
            elif k == "norm":
                g = NT * -(-st["width"] // (4 * P))
                c = dict(rms_ready=1, h_ready=NT, turned=g, turned_taken0=g // 2, turned_taken1=g // 2)
            elif k == "turn":
                g = sum(NT * -(-j[1] // 4) for j in st["jobs"])
                c = dict(turned=g, turned_taken0=g // 2, turned_taken1=g // 2)
            elif k == "headnorm":
                c = dict(sq_ready=1, sum_ready=1, rms_ready=1)
            elif k == "conv":
                c = dict(conv_ready=8)
            elif k == "mlstm":
                c = dict(decay_spread=MH, exponent_ready=MH, exp_ready=MH, scores_ready=MH, probs_ready=MH,
                         pv_ready=MH, pv_taken=MH)
            elif k == "subkeys":
                c = dict(bank_ready=7)
            elif k == "topk":
                c = dict(top_shifted=1, top_exp=1)
            elif k == "gather":
                n = NT * PSLOTS
                c = dict(expert_free=n, mix_free=n, dots_ready=n // BATCH, gelu_ready=n // BATCH,
                         weights_ready=n // BATCH, diag_ready=n, indices_staged=NT * PH, mixed=1)
            elif k == "stick":
                n = SH // HG
                c = dict(scores_ready=n, soft_ready=n, log_in=n, between_ready=n, exponent_ready=n, exp_ready=n,
                         probs_ready=n, pv_ready=n, pv_taken=n)
            elif k == "softmax":
                n = AH // HG
                c = dict(scores_ready=n, max_ready=n, exp_ready=n, probsT_ready=3 * n, probsT_taken0=2 * n,
                         probsT_taken1=n, pv_ready=n, pv_taken=n)
            elif k == "ffn":
                c = dict(gu_ready=FB, hidden_silu=FB, hidden_ready=FB, mixed=1)
            elif k == "rope":
                c = dict(angles_ready=1, sines_ready=1)
            return c

        base = []
        running = {n: 0 for n in names}
        running.update(sines_ready=1, angles_ready=1, diag_ready=1)
        tiles_before = 0
        gathers_before = 0
        norms_before = 0
        ada_before = fetch_before = 0
        for st in STAGES:
            base.append(dict(running))
            for n_, v_ in counts(st).items():
                running[n_] += v_
            st["tile0"] = tiles_before
            tiles_before += {"ada": st.get("tiles", 0), "linear": st.get("tiles", 0),
                             "linearT": st.get("tiles", 0), "gates": 1, "subkeys": 1,
                             "ffn": FB}.get(st["kind"], 0)
            st["gather0"] = gathers_before
            gathers_before += st["kind"] == "gather"
            st["ada0"] = ada_before
            ada_before += st["kind"] == "ada"
            st["fetch0"] = fetch_before
            fetch_before += st["kind"] == "fetch"

        def at(st, name, n=0):
            return base[st["n"]][name] + n

        def enter(eng, st):
            if st["n"]:
                eng.wait_ge(stage_done, 4 * st["n"])

        def leave(eng):
            eng.drain().then_inc(stage_done, 1)

        def w_wait(eng, pos, lap=0):
            eng.wait_ge(w_loaded[pos % RING], (lap + pos // RING + 1) * 16)

        QUERY = part(0, 16, S)
        SCORE = part(4096, NT, 16, PK)
        CAND = part(8192, NT, PH, PTOP * PTOP)
        TOPV = part(12288, NT, PH, 2, PTOP)
        TOPI = part(12800, NT, PH, 2, PTOP).bitcast(U32)
        TOPIF = part(13312, NT, PH, 2, PTOP)
        BESTV = part(13824, NT, PH, PTOP)
        BESTI = part(14080, NT, PH * PTOP).bitcast(U32)
        BROW = part(14336, NT, PH * PTOP).bitcast(U32)
        BCOL = part(14592, NT, PH * PTOP).bitcast(U32)
        BROWF = part(14848, NT, PH * PTOP)
        BCOLF = part(15104, NT, PH * PTOP)
        HOT = part(0, PH, PTOP, PTOP)
        EXPROW = part(15360, NT, PH * PTOP)
        EXPCOL = part(15616, NT, PH * PTOP)
        PSUMS = part(15872, NT * PH)
        GATE = part(20224, NT, PSLOTS)
        EXPERT = part(19968, NT, PSLOTS).bitcast(I32)
        UROWS = part(0, BATCH, D)
        VROWS = part(8192, BATCH, D)
        DIAG = part(16384, BATCH, P)
        PEER_SMALL = part(18432, 256)
        DOTS = PEER_SMALL[:, 0:16].rearrange("p (a b) -> p a b", a=2)
        GELU = PEER_SMALL[:, 16:32].rearrange("p (a b) -> p a b", a=2)
        WEIGHTS = PEER_SMALL[:, 32:48].rearrange("p (a b) -> p a b", a=2)
        STAGED = part(18720, 2, PTOP).bitcast(I32)

        R0 = 10256
        g_i = A[0:16, R0:R0 + S]
        g_f = A[0:16, R0 + S:R0 + 2 * S]
        g_t = A[0:16, R0 + 2 * S:R0 + 3 * S]
        g_e = A[0:16, R0 + 3 * S:R0 + 4 * S]
        g_b = A[0:16, R0 + 4 * S:R0 + 5 * S]
        g_r = A[0:16, R0 + 5 * S:R0 + 6 * S]
        g_m = A[0:16, R0 + 6 * S:R0 + 7 * S]
        g_floor = A[0:16, R0 + 7 * S:R0 + 8 * S]
        m_rT = part(R0 + 8 * S, NT, MH)
        m_floor = part(R0 + 8 * S + 16, NT, MH)
        m_den = part(R0 + 8 * S + 32, 8)
        m_w = part(R0 + 8 * S + 64, 2, 3 * P)
        m_p = part(R0 + 8 * S + 64 + 6 * P, 2, 3 * P)
        m_cw = part(R0 + 8 * S + 64 + 12 * P, 8, 4)
        F0 = 18944
        fx = small[0:16, :]
        f_l = A[0:16, F0:F0 + S]
        f_e = A[0:16, F0 + S:F0 + 2 * S]
        f_c = A[0:16, F0 + 2 * S:F0 + 3 * S]


        k_log = part(14336, 3 * TW)
        k_lost = part(15872, 3 * TW)
        k_exp = part(17408, 3 * TW)
        k_att = part(18944, 3 * TW)

        def soft_bufs(st):
            w = st["work"]
            return A[:, w:w + 3 * TW], A[:, w + 3 * TW:w + 6 * TW]

        def soft_small(st):
            return small[:, 0:2 * HG], small[:, 16:16 + 2 * HG], small[:, 32:32 + 2 * HG]

        def head_square(st):
            n = st["heads"] * st["hd"]
            return H[:, :, :] if n <= D else part(11840, NT, n)

        def heads_of(src, t, n):
            return src[:, t, 0:n]

        f_gate = part(0, RING, S)
        f_hidden = part(RING * S, RING, S)

        def hidden_loop(eng, one):
            for q in range(RING):
                one(q, 0)
            with eng.Fori(1, FB // RING) as i:
                for q in range(RING):
                    one(q, i)
            for q in range(FB // RING * RING, FB):
                one(q, 0)

        r_freq = r_freq_own[:, :]
        r_pos = small[:, 0:NT]
        r_ang = small[:, 64:128]
        r_turn = small[:, 128:192]
        r_cs = small[:, 192:256]
        r_int = rope_int[:, :]
        r_tmp = part(14912, 4 * AH * (ROPE // 2))
        rope_loaded = sem("rope_loaded")

        block = ctx.enter_context(nc.Block())

        @block.sync
        def _(sp):
            sp.dma_start(X[:, :, :], d["x"]).then_inc(inputs_loaded, 16)

            def load(st, name, j, pos, lap, floats):
                sp.wait_ge(tile_used, lap * RING + pos + 1)
                src = d[name][j] if isinstance(j, int) else \
                    d[name][bass.ds(j, 1)].rearrange("a p n -> (a p) n")
                sp.dma_start(W[:, pos % RING, 0:floats], src).then_inc(w_loaded[pos % RING], 16)

            for st in STAGES:
                k, pos = st["kind"], st["tile0"]
                if k in ("ada", "linear", "linearT"):
                    kc, width, tiles = st.get("kc", KD), st.get("width", TW), st["tiles"]
                    if tiles % RING == 0 and tiles >= 2 * RING:
                        with sp.Fori(0, tiles // RING) as i:
                            for q in range(RING):
                                load(st, st["weights"], i * RING + q, pos + q, i, kc * width)
                    else:
                        for j in range(tiles):
                            load(st, st["weights"], j, pos + j, 0, kc * width)
                elif k == "gates":
                    load(st, st["weights"], 0, pos, 0, KD * st["groups"] * st["m"])
                elif k == "subkeys":
                    load(st, f"sub_keys{st['layer']}", 0, pos, 0, 2 * PK)
                elif k == "ffn":
                    laps = FB // RING
                    with sp.Fori(0, laps) as i:
                        for q in range(RING):
                            load(st, st["weights"], i * RING + q, pos + q, i, 3 * D)
                    for j in range(laps * RING, FB):
                        load(st, st["weights"], j, pos + j, 0, 3 * D)
            sp.wait_ge(stage_done, 4 * len(STAGES))
            sp.dma_start(d["out"], X[:, :, :]).then_inc(stored, 16)
            sp.wait_ge(stored, 16)

        @block.gpsimd
        def _(pool):
            pool.memset(ident[:, :], 0.0)
            pool.memset(ones[:, :], 1.0)
            pool.memset(causal[:, :], 0.0)
            pool.memset(zrow[:, :], 0.0)
            pool.memset(eps[:, :], EPS)
            pool.memset(m_v[:, :, :, MV:MV + 1], 1.0)
            pool.iota(iota16[:, :], pattern=[[1, 16]], base=0, channel_multiplier=0,
                      allow_small_or_imprecise_dtypes=True)
            pool.drain()
            pool.affine_select(out=ident[:, :], in_=ident[:, :], compare_op=ALU.not_equal, fill=1.0,
                               base=0, pattern=[[-1, P]], channel_multiplier=1)
            pool.affine_select(out=after[:, :], in_=ones[:, :], compare_op=ALU.is_gt, fill=0.0,
                               base=0, pattern=[[-1, P]], channel_multiplier=1)
            pool.affine_select(out=before[:, :], in_=ones[:, :], compare_op=ALU.is_gt, fill=0.0,
                               base=0, pattern=[[1, P]], channel_multiplier=-1)
            pool.affine_select(out=upto[:, :], in_=ones[:, :], compare_op=ALU.is_ge, fill=0.0,
                               base=0, pattern=[[1, P]], channel_multiplier=-1)
            pool.affine_select(out=causal[:, :], in_=causal[:, :], compare_op=ALU.is_ge, fill=-HUGE,
                               base=P, pattern=[[-1, S]], channel_multiplier=1)
            pool.drain().then_inc(consts_ready, 1)

            def gather(st):
                u_dram, v_dram = d[f"peer_u{st['layer']}"], d[f"peer_v{st['layer']}"]
                n0 = st["gather0"] * NT * PSLOTS

                def claim(name, count):
                    pool.wait_ge(SEM[name], count)
                    pool.sem_inc(SEM["claimed"], 1)

                def fetch(t, i, e):
                    m = n0 + t * PSLOTS + i * PTOP
                    pool.tensor_copy(STAGED[:, e, :], EXPERT[:, t, bass.ds(i * PTOP, PTOP)]
                                     ).then_inc(SEM["indices_staged"], 1)
                    claim("indices_staged", at(st, "indices_staged", t * PH + 1) + i)
                    for ab in range(2):
                        for ring, table, free, loaded in ((UROWS, u_dram, "expert_free", u_loaded),
                                                          (VROWS, v_dram, "mix_free", v_loaded)):
                            for q in range(BATCH):
                                claim(free, m + ab * BATCH + q + 1)
                                pool.indirect_dma_start(
                                    ring[:, q, :], None, table,
                                    bass.IndirectOffsetOnAxis(ap=STAGED[:, e, ab * BATCH + q:ab * BATCH + q + 1],
                                                              axis=0)).then_inc(loaded[q], 16)

                for t in range(NT):
                    with pool.Fori(0, PH // 2) as i:
                        for e in range(2):
                            fetch(t, i * 2 + e, e)

            for st in STAGES:
                enter(pool, st)
                if st["kind"] == "gather":
                    gather(st)
                leave(pool)


        def used(pos, lap=0):
            return RING + pos + 1 + lap * RING

        @block.tensor
        def _(pe):
            mm, tr = nc.tensor.matmul, nc.tensor.transpose
            pe.wait_ge(consts_ready, 1)
            pe.drain().then_inc(tile_used, RING)

            def tile_product(st, lhs, kc, width, q, lap, free):
                pos = st["tile0"] + q
                w_wait(pe, pos, lap)
                w = wslot(pos, kc, width)
                for t in range(NT):
                    if free:
                        pe.wait_ge(SEM[f"bank_free{t}"], at(st, f"bank_free{t}", q - RING + 1) + lap * RING)
                    for k in range(kc):
                        ins = mm(PS[:, 2 * (q % RING) + t, 0:width], lhs(k, t), w[:, k, :],
                                 start=k == 0, stop=k == kc - 1)
                    ins.then_inc(SEM["bank_ready"] if t == 0 else tile_used, 1)

            def linear(st):
                kc, width, tiles = st["kc"], st["width"], st["tiles"]
                for j in range(tiles):
                    tile_product(st, lambda k, t: XT[:, k, t * P:(t + 1) * P], kc, width, j, 0, j >= RING)

            def ada(st):
                if st["n"] == 0:
                    pe.wait_ge(SEM["angles_ready"], 0 + 1)

                def one(q, lap, free):
                    pos = st["tile0"] + q
                    w_wait(pe, pos, lap)
                    if free:
                        pe.wait_ge(SEM["bank_free0"], at(st, "bank_free0", q - RING + 1) + lap * RING)
                    w = wslot(pos, KD, TW)
                    for k in range(KD):
                        ins = mm(PS[:, 2 * (q % RING), :], CB[:, k, :], w[:, k, :], start=k == 0, stop=k == KD - 1)
                    ins.then_inc(tile_used, 1)

                tiles = st["tiles"]
                if tiles % RING == 0 and tiles >= 2 * RING:
                    for q in range(RING):
                        one(q, 0, False)
                    with pe.Fori(1, tiles // RING) as i:
                        for q in range(RING):
                            one(q, i, True)
                else:
                    for q in range(tiles):
                        one(q, 0, q >= RING)

            def linearT(st):
                for j in range(st["tiles"]):
                    pos = st["tile0"] + j
                    w_wait(pe, pos)
                    w = wslot(pos, KD, TW)
                    for b in range(4):
                        n = 4 * j + b
                        if n >= 8:
                            pe.wait_ge(SEM[f"turned_taken{n % 2}"], at(st, f"turned_taken{n % 2}", (n - 8) // 2 + 1))
                        for k in range(KD):
                            ins = mm(PS[:, n % 8, 0:S], w[:, k, b * P:(b + 1) * P], XT[:, k, :],
                                     start=k == 0, stop=k == KD - 1)
                        ins.then_inc(SEM["bank_ready"] if b < 3 else tile_used, 1)

            def gates(st):
                w_wait(pe, st["tile0"])
                m, groups = st["m"], st["groups"]
                w = wslot(st["tile0"], KD, m * groups)
                for g in range(groups):
                    for k in range(KD):
                        ins = mm(PS[0:m, g, 0:S], w[:, k, g * m:(g + 1) * m], XT[:, k, :],
                                 start=k == 0, stop=k == KD - 1)
                ins.then_inc(tile_used, 1)
                if groups == 2:
                    pe.wait_ge(SEM["scan_ready"], at(st, "scan_ready", 1))
                    for t in range(NT):
                        tr(PS[:, 2, t * MH:(t + 1) * MH], g_r[0:MH, t * P:(t + 1) * P], ident[0:MH, 0:MH])
                        ins = tr(PS[:, 3, t * MH:(t + 1) * MH], g_floor[0:MH, t * P:(t + 1) * P], ident[0:MH, 0:MH])
                    ins.then_inc(SEM["rowsT_ready"], 1)

            def transposes(st, jobs):
                n = 0
                for src, chunks, width, _ in jobs:
                    for t in range(NT):
                        for c0 in range(0, chunks, 4):
                            if n >= 8:
                                pe.wait_ge(SEM[f"turned_taken{n % 2}"],
                                           at(st, f"turned_taken{n % 2}", (n - 8) // 2 + 1))
                            for c in range(c0, min(c0 + 4, chunks)):
                                ins = tr(PS[0:width, n % 8, (c - c0) * P:(c - c0 + 1) * P], src(t, c), ident[:, :])
                            ins.then_inc(SEM["turned"], 1)
                            n += 1

            def norm(st):
                pe.wait_ge(SEM["h_ready"], at(st, "h_ready", NT))
                dst = st["dst"]
                transposes(st, [(lambda t, c: dst(t)[:, c * P:(c + 1) * P], st["width"] // P, P, XT)])

            def mlstm(st):
                q_of = lambda h: m_conv[(h % 2) * MQK:(h % 2 + 1) * MQK, h // 2, :]
                k_of = lambda h: m_conv[(h % 2) * MQK:(h % 2 + 1) * MQK, MH // 2 + h // 2, :]

                def scores(h):
                    b = h % 2
                    if h >= 2:
                        pe.wait_ge(SEM["probs_ready"], at(st, "probs_ready", h - 1))
                    mm(PS[:, b, 0:S], ident[0:MH, h:h + 1].to_broadcast([MH, P]), g_m[0:MH, :],
                       start=True, stop=True).then_inc(SEM["decay_spread"], 1)
                    mm(PS[:, 2 + b, 0:S], k_of(h)[:, 0:P], q_of(h), start=True, stop=True)
                    mm(PS[:, 2 + b, S:S + P], k_of(h)[:, P:S], q_of(h)[:, P:S], start=True, stop=True
                       ).then_inc(SEM["scores_ready"], 1)

                scores(0)
                for h in range(MH):
                    if h + 1 < MH:
                        scores(h + 1)
                    b = h % 2
                    pe.wait_ge(SEM["probs_ready"], at(st, "probs_ready", h + 1))
                    if h >= 2:
                        pe.wait_ge(SEM["pv_taken"], at(st, "pv_taken", h - 1))
                    mm(PS[:, 4 + b, 0:MV + 1], m_p[:, b, 0:P], m_v[:, 0, h, :], start=True, stop=True)
                    mm(PS[:, 4 + b, 256:256 + MV + 1], m_p[:, b, P:S], m_v[:, 0, h, :], start=True, stop=False)
                    mm(PS[:, 4 + b, 256:256 + MV + 1], m_p[:, b, S:S + P], m_v[:, 1, h, :], start=False, stop=True
                       ).then_inc(SEM["pv_ready"], 1)

            def subkeys(st):
                w_wait(pe, st["tile0"])
                w = wslot(st["tile0"], 2, PK)
                for t in range(NT):
                    for b in range(16):
                        ins = mm(PS[:, t * 4 + b // 4, (b % 4) * P:(b % 4 + 1) * P],
                                 QUERY[:, b, t * P:(t + 1) * P], w[:, b % 2, :], start=True, stop=True)
                        if b % 4 == 3:
                            ins.then_inc(tile_used if t * 4 + b // 4 == 7 else SEM["bank_ready"], 1)

            def gather(st):
                for b in range(4):
                    mm(PS[:, b, :], zrow[:, 0:P], zrow[:, :], start=True, stop=False, skip_group_check=True)
                m0 = st["gather0"] * NT * PSLOTS
                for t in range(NT):
                    with pe.Fori(0, PH) as i:
                        for ab in range(2):
                            for q in range(BATCH):
                                n = t * PSLOTS + ab * BATCH + q
                                pe.wait_ge(v_loaded[q], 16 * ((m0 + n) // BATCH + 1) + 32 * i)
                                pe.wait_ge(SEM["diag_ready"], at(st, "diag_ready", n + 1) + PTOP * i)
                                for c in range(2):
                                    ins = mm(PS[:, 2 * t + c, :], DIAG[:, q, :], VROWS[:, q, c * TW:(c + 1) * TW],
                                             start=False, stop=False, skip_group_check=True)
                                ins.then_inc(SEM["mix_free"], 1)
                for b in range(4):
                    ins = mm(PS[:, b, :], zrow[:, 0:P], zrow[:, :], start=False, stop=True, skip_group_check=True)
                ins.then_inc(SEM["mixed"], 1)

            def stick(st):
                qT, kT, v = st["qT"], st["kT"], st["v"]
                for g in range(SH // HG):
                    for h in range(HG):
                        hh = g * HG + h
                        mm(PS[:, h // 2, (h % 2) * S:(h % 2 + 1) * S], kT[0:SD, hh, 0:P], qT[0:SD, hh, :],
                           start=True, stop=True)
                        ins = mm(PS[:, 2, h * P:(h + 1) * P], kT[0:SD, hh, P:S], qT[0:SD, hh, P:S],
                                 start=True, stop=True)
                    ins.then_inc(SEM["scores_ready"], 1)
                    pe.wait_ge(SEM["log_in"], at(st, "log_in", g + 1))
                    lost = k_lost
                    for n in range(2):
                        mm(PS[:, 3 + n, :], after[:, :], lost[:, n * TW:(n + 1) * TW], start=True, stop=False)
                        mm(PS[:, 3 + n, :].rearrange("p (h t) -> p h t", t=S)[:, :, P:S], ones[:, :],
                           lost[:, 2 * TW + 2 * n * P:2 * TW + (2 * n + 2) * P].rearrange("p (h t) -> p h t", t=P),
                           start=False, stop=True)
                    mm(PS[:, 5, :], after[:, :], lost[:, 2 * TW:3 * TW], start=True, stop=True
                       ).then_inc(SEM["between_ready"], 1)
                    pe.wait_ge(SEM["probs_ready"], at(st, "probs_ready", g + 1))
                    if g:
                        pe.wait_ge(SEM["pv_taken"], at(st, "pv_taken", g))
                    for h in range(HG):
                        hh = g * HG + h
                        o = lambda t: PS[:, 6, t * 256 + h * SD:t * 256 + (h + 1) * SD]
                        mm(o(0), k_att[:, h * S:h * S + P], v(0, hh), start=True, stop=True)
                        mm(o(1), k_att[:, h * S + P:(h + 1) * S], v(0, hh), start=True, stop=False)
                        ins = mm(o(1), k_att[:, 2 * TW + h * P:2 * TW + (h + 1) * P], v(1, hh), start=False, stop=True)
                    ins.then_inc(SEM["pv_ready"], 1)

            def softmax(st):
                qT, kT, v, dk = st["qT"], st["kT"], st["v"], st["dk"]
                prob, probT = soft_bufs(st)
                for g in range(AH // HG):
                    for h in range(HG):
                        hh = g * HG + h
                        for t, (bank, at_, n) in enumerate(((0, h * P, P), (1 + h // 2, (h % 2) * S, S))):
                            o = PS[:, bank, at_:at_ + n]
                            ins = mm(o, qT[0:dk, hh, t * P:(t + 1) * P], kT[0:dk, hh, 0:n],
                                     start=True, stop=not st["decay"])
                            if st["decay"]:
                                ins = mm(o, ident[0:AH, hh:hh + 1].to_broadcast([AH, P]), f_c[0:AH, 0:n],
                                         start=False, stop=True)
                    ins.then_inc(SEM["scores_ready"], 1)
                    pe.wait_ge(SEM["exp_ready"], at(st, "exp_ready", g + 1))
                    for n in range(3):
                        for c in range(4):
                            ins = tr(PS[:, 3 + n, c * P:(c + 1) * P], prob[:, (4 * n + c) * P:(4 * n + c + 1) * P],
                                     ident[:, :])
                        ins.then_inc(SEM["probsT_ready"], 1)
                    pe.wait_ge(SEM["probsT_taken0"], at(st, "probsT_taken0", 2 * g + 2))
                    pe.wait_ge(SEM["probsT_taken1"], at(st, "probsT_taken1", g + 1))
                    if g:
                        pe.wait_ge(SEM["pv_taken"], at(st, "pv_taken", g))
                    for h in range(HG):
                        hh = g * HG + h
                        o = lambda t: PS[:, 6, t * 256 + h * AV:t * 256 + (h + 1) * AV]
                        mm(o(0), probT[:, h * P:(h + 1) * P], v(0, hh), start=True, stop=True)
                        late = 4 * P + h * S
                        mm(o(1), probT[:, late:late + P], v(0, hh), start=True, stop=False)
                        ins = mm(o(1), probT[:, late + P:late + S], v(1, hh), start=False, stop=True)
                    ins.then_inc(SEM["pv_ready"], 1)

            def ffn(st):
                pos = st["tile0"]
                for b in range(4):
                    mm(PS[:, 4 + b, :], zrow[:, 0:P], zrow[:, :], start=True, stop=False, skip_group_check=True)

                def gate_up(q, lap):
                    w_wait(pe, pos + q, lap)
                    w = W[:, (pos + q) % RING, 0:2 * D].rearrange("p (a k n) -> p a k n", a=2, n=P)
                    for a in range(2):
                        for k in range(KD):
                            ins = mm(PS[:, q % RING, a * S:(a + 1) * S], w[:, a, k, :], XT[:, k, :],
                                     start=k == 0, stop=k == KD - 1)
                    ins.then_inc(SEM["gu_ready"], 1)

                def down(q, lap):
                    pe.wait_ge(SEM["hidden_ready"], at(st, "hidden_ready", q + 1) + lap * RING)
                    w = W[:, (pos + q) % RING, 2 * D:3 * D]
                    for t in range(NT):
                        for c in range(2):
                            ins = mm(PS[:, 4 + 2 * t + c, :], f_hidden[:, q % RING, t * P:(t + 1) * P],
                                     w[:, c * TW:(c + 1) * TW], start=False, stop=False, skip_group_check=True)
                    ins.then_inc(tile_used, 1)

                gate_up(0, 0)
                laps = (FB - 1) // RING
                with pe.Fori(0, laps) as i:
                    for q in range(RING):
                        gate_up(q + 1, i)
                        down(q, i)
                for q in range(laps * RING, FB - 1):
                    gate_up(q + 1, 0)
                    down(q, 0)
                down(FB - 1, 0)
                for b in range(4):
                    ins = mm(PS[:, 4 + b, :], zrow[:, 0:P], zrow[:, :], start=False, stop=True, skip_group_check=True)
                ins.then_inc(SEM["mixed"], 1)

            parts = dict(ada=ada, norm=norm, linear=linear, linearT=linearT, gates=gates, mlstm=mlstm,
                         turn=lambda st: transposes(st, st["jobs"]), subkeys=subkeys, gather=gather, stick=stick,
                         softmax=softmax, ffn=ffn)
            for st in STAGES:
                enter(pe, st)
                if st["kind"] in parts:
                    parts[st["kind"]](st)
                leave(pe)

        @block.scalar
        def _(act):
            f = nc.scalar.activation

            def load_gain(n):
                name, width = gains[n]
                act.dma_start(GAIN[:, n % 2, 0:width], d[name].partition_broadcast(P)).then_inc(gain_loaded[n % 2], 16)

            act.dma_start(ccol[:, :], d["c"]).then_inc(bias_loaded, 16)
            act.dma_start(bias8[0:MH, :], d["ma_b_if"]).then_inc(inputs_loaded, 16)
            act.dma_start(bias16[:, :], d["fox_b_f"]).then_inc(inputs_loaded, 16)
            act.dma_start(m_cw, d["conv_w"]).then_inc(inputs_loaded, 16)
            act.dma_start(posi[:, :], d["positions"]).then_inc(inputs_loaded, 16)
            act.dma_start(r_freq, d["rope_freq"].partition_broadcast(P)).then_inc(rope_loaded, 16)
            load_gain(0)
            act.wait_ge(bias_loaded, 16)
            f(ccol[:, :], ccol[:, :], ACT.Silu).then_inc(SEM["sines_ready"], 1)
            act.drain().then_inc(SEM["diag_ready"], 1)

            def linear(st):
                for j in range(st["tiles"]):
                    for t in range(NT):
                        what, dst, *_ = st["out"](t, j)
                        if what in ("sigmoid", "copy by ACT") or (what == "copy" and t == 0):
                            if t == 0:
                                act.wait_ge(SEM["bank_ready"], at(st, "bank_ready", j + 1))
                            else:
                                act.wait_ge(tile_used, used(st["tile0"] + j))
                            src = PS[:, 2 * (j % RING) + t, 0:st["width"]]
                            if len(dst.shape) == 3:
                                src = src.rearrange("p (a b) -> p a b", b=dst.shape[2])
                            f(dst, src, ACT.Sigmoid if what == "sigmoid" else ACT.Copy
                              ).then_inc(SEM[f"bank_free{t}"], 1)

            def linearT(st):
                for n in range(0, 4 * st["tiles"], 2):
                    act.wait_ge(SEM["bank_ready"], at(st, "bank_ready", 3 * (n // 4) + n % 4 + 1))
                    f(st["dst"][:, n, :], PS[:, n % 8, 0:S], ACT.Copy).then_inc(SEM["turned_taken0"], 1)

            def log_sigmoid_in(m, pre, a, e):
                f(a[0:m, :], pre[0:m, :], ACT.Abs)
                act.drain()
                f(e[0:m, :], a[0:m, :], ACT.Exp, scale=-1.0)
                act.drain()
                f(e[0:m, :], e[0:m, :], ACT.Ln, bias=1.0).then_inc(SEM["log_out"], 1)

            def gates(st):
                act.wait_ge(inputs_loaded, 16 * 5)
                act.wait_ge(tile_used, used(st["tile0"]))
                if st["groups"] == 2:
                    f(g_i[0:MH, :], PS[0:MH, 0, 0:S], ACT.Identity, bias=bias8[0:MH, 0:1])
                    f(g_f[0:MH, :], PS[0:MH, 1, 0:S], ACT.Identity, bias=bias8[0:MH, 1:2])
                    act.drain().then_inc(SEM["gates_in"], 1)
                    log_sigmoid_in(MH, g_f, g_t, g_e)
                    act.wait_ge(SEM["rowsT_ready"], at(st, "rowsT_ready", 1))
                    f(m_floor, PS[:, 3, 0:NT * MH].rearrange("p (a b) -> p a b", b=MH), ACT.Exp
                      ).then_inc(SEM["floor_ready"], 1)
                else:
                    f(fx, PS[0:AH, 0, 0:S], ACT.Identity, bias=bias16[:, 0:1])
                    act.drain().then_inc(SEM["gates_in"], 1)
                    log_sigmoid_in(AH, fx, f_l, f_e)

            def taken(st, jobs):
                n = 0
                for _, chunks, width, dst in jobs:
                    for t in range(NT):
                        for c0 in range(0, chunks, 4):
                            if n % 2 == 0:
                                c1 = min(c0 + 4, chunks)
                                act.wait_ge(SEM["turned"], at(st, "turned", n + 1))
                                f(dst[0:width, c0:c1, t * P:(t + 1) * P],
                                  PS[0:width, n % 8, 0:(c1 - c0) * P].rearrange("p (a b) -> p a b", b=P),
                                  ACT.Copy).then_inc(SEM["turned_taken0"], 1)
                            n += 1

            def norm(st):
                if st["gain"] + 1 < len(gains):
                    load_gain(st["gain"] + 1)
                if st["n"] == 1:
                    act.wait_ge(inputs_loaded, 16 * 5)
                w = st["width"]
                for t in range(NT):
                    f(st["dst"](t), st["src"](t), ACT.Square, accum_out=ss[:, t:t + 1])
                act.drain()
                f(rms[:, 0:NT], ss[:, 0:NT], ACT.Sqrt, scale=1.0 / w, bias=eps[:, 0:1]
                  ).then_inc(SEM["rms_ready"], 1)
                taken(st, [(None, w // P, P, XT)])

            def headnorm(st):
                if st["gain"] + 1 < len(gains):
                    load_gain(st["gain"] + 1)
                n = st["heads"] * st["hd"]
                sq = head_square(st)
                for t in range(NT):
                    f(sq[:, t, 0:n], heads_of(st["src"], t, n), ACT.Square)
                act.drain().then_inc(SEM["sq_ready"], 1)
                act.wait_ge(SEM["sum_ready"], at(st, "sum_ready", 1))
                m = NT * st["heads"]
                f(rms[:, 0:m], ss[:, 0:m], ACT.Sqrt, scale=1.0 / st["hd"], bias=eps[:, 0:1]
                  ).then_inc(SEM["rms_ready"], 1)

            def conv(st):
                for b in range(8):
                    act.wait_ge(SEM["conv_ready"], at(st, "conv_ready", b + 1))
                    f(m_conv[:, b, :], m_conv[:, b, :], ACT.Silu)

            def mlstm(st):
                for h in range(MH):
                    act.wait_ge(SEM["exponent_ready"], at(st, "exponent_ready", h + 1))
                    f(m_w[:, h % 2, :], m_w[:, h % 2, :], ACT.Exp).then_inc(SEM["exp_ready"], 1)

            def subkeys(st):
                for t in range(NT):
                    for b in range(0, 4, 2):
                        n = t * 4 + b
                        act.wait_ge(SEM["bank_ready"], at(st, "bank_ready", n + 1))
                        f(SCORE[:, t, 4 * b:4 * b + 4, :], PS[:, n, :].rearrange("p (a b) -> p a b", b=P), ACT.Copy)

            def topk(st):
                act.wait_ge(SEM["top_shifted"], at(st, "top_shifted", 1))
                f(BESTV[:, :, :, :], BESTV[:, :, :, :], ACT.Exp).then_inc(SEM["top_exp"], 1)

            def gather(st):
                for t in range(NT):
                    with act.Fori(0, PH) as i:
                        for ab in range(2):
                            n = t * PSLOTS + ab * BATCH
                            act.wait_ge(SEM["dots_ready"], at(st, "dots_ready", n // BATCH + 1) + 2 * i)
                            f(GELU[:, ab, :], DOTS[:, ab, :], ACT.Gelu).then_inc(SEM["gelu_ready"], 1)
                            act.wait_ge(SEM["weights_ready"], at(st, "weights_ready", n // BATCH + 1) + 2 * i)
                            for q in range(BATCH):
                                act.wait_ge(SEM["mix_free"], at(st, "mix_free", n + q + 1) + PTOP * i)
                                f(DIAG[:, q, :], ident[:, :], ACT.Copy, scale=WEIGHTS[:, ab, q:q + 1]
                                  ).then_inc(SEM["diag_ready"], 1)

            def stick(st):
                for g in range(SH // HG):
                    act.wait_ge(SEM["scores_ready"], at(st, "scores_ready", g + 1))
                    z = PS[:, 0:3, :]
                    view = lambda b: b.rearrange("p (a b) -> p a b", b=TW)
                    if g:
                        act.wait_ge(SEM["probs_ready"], at(st, "probs_ready", g))
                    f(view(k_log), z, ACT.Abs)
                    act.drain()
                    f(k_log, k_log, ACT.Exp, scale=-1.0)
                    act.drain()
                    f(k_log, k_log, ACT.Ln, bias=1.0).then_inc(SEM["soft_ready"], 1)
                    act.wait_ge(SEM["exponent_ready"], at(st, "exponent_ready", g + 1))
                    f(k_att, k_exp, ACT.Exp).then_inc(SEM["exp_ready"], 1)

            def softmax(st):
                prob, probT = soft_bufs(st)
                sums, nmax, rsum = soft_small(st)
                for g in range(AH // HG):
                    act.wait_ge(SEM["max_ready"], at(st, "max_ready", g + 1))
                    for t in range(NT):
                        for h in range(HG):
                            a0, n = (h * P, P) if t == 0 else (4 * P + h * S, S)
                            f(prob[:, a0:a0 + n], prob[:, a0:a0 + n], ACT.Exp, bias=nmax[:, t * HG + h:t * HG + h + 1],
                              accum_out=sums[:, t * HG + h:t * HG + h + 1])
                    act.drain().then_inc(SEM["exp_ready"], 1)
                    for n in (0, 2):
                        act.wait_ge(SEM["probsT_ready"], at(st, "probsT_ready", 3 * g + n + 1))
                        f(probT[:, n * TW:(n + 1) * TW], PS[:, 3 + n, :], ACT.Copy).then_inc(SEM["probsT_taken0"], 1)

            def ffn(st):
                def one(q, lap):
                    act.wait_ge(SEM["gu_ready"], at(st, "gu_ready", q + 1) + lap * RING)
                    if not isinstance(lap, int) or q >= RING:
                        act.wait_ge(SEM["hidden_ready"], at(st, "hidden_ready", q - RING + 1) + lap * RING)
                    f(f_gate[:, q % RING, :], PS[:, q % RING, 0:S], ACT.Silu).then_inc(SEM["hidden_silu"], 1)
                hidden_loop(act, one)

            def rope(st):
                act.wait_ge(SEM["angles_ready"], at(st, "angles_ready", 1))
                f(r_cs, r_ang, ACT.Sin).then_inc(SEM["sines_ready"], 1)

            def ada(st):
                act.dma_start(st["dst"][:, 0:st["tiles"] * TW], d[st["bias"]].partition_broadcast(P)
                              ).then_inc(bias_loaded, 16)

            def fetch(st):
                act.dma_start(st["dst"], d[st["name"]]).then_inc(fetched, 16)
                act.wait_ge(fetched, 16 * (st["fetch0"] + 1))

            parts = dict(ada=ada, norm=norm, linear=linear, linearT=linearT, gates=gates, conv=conv, mlstm=mlstm,
                         headnorm=headnorm, turn=lambda st: taken(st, st["jobs"]), subkeys=subkeys, topk=topk,
                         gather=gather, stick=stick, softmax=softmax, ffn=ffn, rope=rope, fetch=fetch)
            for st in STAGES:
                enter(act, st)
                if st["kind"] in parts:
                    parts[st["kind"]](st)
                leave(act)

        @block.vector
        def _(dve):
            v = nc.vector
            tt, ts, stt, cp = v.tensor_tensor, v.tensor_scalar, v.scalar_tensor_tensor, v.tensor_copy

            dve.drain().then_inc(SEM["expert_free"], BATCH)
            dve.drain().then_inc(SEM["mix_free"], BATCH)
            dve.wait_ge(consts_ready, 1)
            dve.wait_ge(SEM["sines_ready"], 1)
            for k in range(KD):
                ts(CB[:, k, :], ones[:, :], ccol[:, k:k + 1], None, ALU.mult)
            dve.drain().then_inc(SEM["angles_ready"], 1)

            def ada(st):
                pos, tiles, dst = st["tile0"], st["tiles"], st["dst"]
                dve.wait_ge(bias_loaded, 16 * (st["ada0"] + 2))

                def one(q, lap):
                    dve.wait_ge(tile_used, used(pos + q, lap))
                    o = dst[:, q * TW:(q + 1) * TW] if isinstance(lap, int) else \
                        dst[:, bass.ds(lap * (RING * TW) + q * TW, TW)]
                    tt(o, o, PS[:, 2 * (q % RING), :], ALU.add).then_inc(SEM["bank_free0"], 1)

                if tiles % RING == 0 and tiles >= 2 * RING:
                    with dve.Fori(0, tiles // RING) as i:
                        for q in range(RING):
                            one(q, i)
                else:
                    for q in range(tiles):
                        one(q, 0)
                dve.drain()
                for s in st["scales"]:
                    ts(dst[:, s * D:(s + 1) * D], dst[:, s * D:(s + 1) * D], 1.0, None, ALU.add)

            def linear(st):
                for j in range(st["tiles"]):
                    for t in range(NT):
                        what, dst, *gate = st["out"](t, j)
                        if what == "residual" or (what == "copy" and t == 1):
                            if t == 0:
                                dve.wait_ge(SEM["bank_ready"], at(st, "bank_ready", j + 1))
                            else:
                                dve.wait_ge(tile_used, used(st["tile0"] + j))
                            src = PS[:, 2 * (j % RING) + t, 0:st["width"]]
                            if what == "copy":
                                if len(dst.shape) == 3:
                                    src = src.rearrange("p (a b) -> p a b", b=dst.shape[2])
                                cp(dst, src).then_inc(SEM[f"bank_free{t}"], 1)
                            elif gate[0] is None:
                                tt(dst, dst, src, ALU.add).then_inc(SEM[f"bank_free{t}"], 1)
                            else:
                                tmp = H[:, t, j * TW:(j + 1) * TW]
                                tt(tmp, gate[0], src, ALU.mult).then_inc(SEM[f"bank_free{t}"], 1)
                                dve.drain()
                                tt(dst, dst, tmp, ALU.add)

            def linearT(st):
                for n in range(1, 4 * st["tiles"], 2):
                    if n % 4 == 3:
                        dve.wait_ge(tile_used, used(st["tile0"] + n // 4))
                    else:
                        dve.wait_ge(SEM["bank_ready"], at(st, "bank_ready", 3 * (n // 4) + n % 4 + 1))
                    cp(st["dst"][:, n, :], PS[:, n % 8, 0:S]).then_inc(SEM["turned_taken1"], 1)

            def log_sigmoid_cumsum(st, m, pre, e, t_, out):
                dve.wait_ge(SEM["gates_in"], at(st, "gates_in", 1))
                dve.wait_ge(SEM["log_out"], at(st, "log_out", 1))
                stt(t_[0:m, :], pre[0:m, :], 0.0, e[0:m, :], ALU.min, ALU.subtract)
                dve.drain()
                v.tensor_tensor_scan(out=out[0:m, :], data0=t_[0:m, :], data1=zrow[0:m, 0:S], initial=0.0,
                                     op0=ALU.add, op1=ALU.add)
                dve.drain().then_inc(SEM["log_in"], 1)

            def gates(st):
                if st["groups"] == 2:
                    log_sigmoid_cumsum(st, MH, g_f, g_e, g_t, g_b)
                    tt(g_r[0:MH, :], g_i[0:MH, :], g_b[0:MH, :], ALU.subtract)
                    dve.drain()
                    v.tensor_tensor_scan(out=g_m[0:MH, :], data0=g_r[0:MH, :], data1=g_r[0:MH, :], initial=0.0,
                                         op0=ALU.max, op1=ALU.max)
                    dve.drain()
                    stt(g_floor[0:MH, :], g_b[0:MH, :], -1.0, g_m[0:MH, :], ALU.mult, ALU.subtract)
                    dve.drain().then_inc(SEM["scan_ready"], 1)
                    dve.wait_ge(SEM["rowsT_ready"], at(st, "rowsT_ready", 1))
                    cp(m_rT, PS[:, 2, 0:NT * MH].rearrange("p (a b) -> p a b", b=MH)).then_inc(SEM["rows_taken"], 1)
                else:
                    log_sigmoid_cumsum(st, AH, fx, f_e, f_l, f_c)
                    ts(f_c[0:AH, :], f_c[0:AH, :], -1.0, None, ALU.mult)

            def taken(st, jobs):
                n = 0
                for _, chunks, width, dst in jobs:
                    for t in range(NT):
                        for c0 in range(0, chunks, 4):
                            if n % 2 == 1:
                                c1 = min(c0 + 4, chunks)
                                dve.wait_ge(SEM["turned"], at(st, "turned", n + 1))
                                cp(dst[0:width, c0:c1, t * P:(t + 1) * P],
                                   PS[0:width, n % 8, 0:(c1 - c0) * P].rearrange("p (a b) -> p a b", b=P)
                                   ).then_inc(SEM["turned_taken1"], 1)
                            n += 1

            def gain_wait(st):
                n = st["gain"]
                dve.wait_ge(gain_loaded[n % 2], 16 * (n // 2 + 1))

            def norm(st):
                w, n = st["width"], st["gain"]
                gain_wait(st)
                g = GAIN[:, n % 2, 0:w]
                if st["scale"] is not None:
                    tt(g, g, st["scale"], ALU.mult)
                dve.wait_ge(SEM["rms_ready"], at(st, "rms_ready", 1))
                v.reciprocal(rs[:, 0:NT], rms[:, 0:NT])
                dve.drain()
                for t in range(NT):
                    ins = stt(st["dst"](t), st["src"](t), rs[:, t:t + 1], g, ALU.mult, ALU.mult)
                    if st["shift"] is not None:
                        dve.drain()
                        ins = tt(st["dst"](t), st["dst"](t), st["shift"], ALU.add)
                    ins.then_inc(SEM["h_ready"], 1)
                taken(st, [(None, w // P, P, XT)])

            def headnorm(st):
                heads, hd, src = st["heads"], st["hd"], st["src"]
                n = heads * hd
                sq = head_square(st)
                gain_wait(st)
                dve.wait_ge(SEM["sq_ready"], at(st, "sq_ready", 1))
                for t in range(NT):
                    v.tensor_reduce(out=ss[:, t * heads:(t + 1) * heads],
                                    in_=sq[:, t, 0:n].rearrange("p (h e) -> p h e", e=hd), axis=AX.X, op=ALU.add)
                dve.drain().then_inc(SEM["sum_ready"], 1)
                dve.wait_ge(SEM["rms_ready"], at(st, "rms_ready", 1))
                m = NT * heads
                v.reciprocal(rs[:, 0:m], rms[:, 0:m])
                dve.drain()
                if st["factor"] != 1.0:
                    ts(rs[:, 0:m], rs[:, 0:m], st["factor"], None, ALU.mult)
                    dve.drain()
                gain = GAIN[:, st["gain"] % 2, :]
                for t in range(NT):
                    x = heads_of(src, t, n).rearrange("p (h e) -> p h e", e=hd)
                    tt(x, x, rs[:, t * heads:(t + 1) * heads].unsqueeze(2).to_broadcast([P, heads, hd]), ALU.mult)
                dve.drain()
                for t in range(NT):
                    x = heads_of(src, t, n).rearrange("p (h e) -> p h e", e=hd)
                    if st["times"] is None:
                        tt(x, x, gain[:, 0:hd].unsqueeze(1).to_broadcast([P, heads, hd]), ALU.mult)
                    else:
                        tt(heads_of(src, t, n), heads_of(src, t, n), gain[:, 0:n], ALU.mult)
                if st["times"] is not None:
                    dve.drain()
                    for t in range(NT):
                        tt(heads_of(src, t, n), heads_of(src, t, n), st["times"][:, t, :], ALU.mult)

            def conv(st):
                dve.wait_ge(inputs_loaded, 16 * 5)
                for b in range(8):
                    ts(m_conv[:, b, :], m_qk[:, b, :], m_cw[:, b, 3:4], None, ALU.mult)
                    for back in (1, 2, 3):
                        dve.drain()
                        ins = stt(m_conv[:, b, back:S], m_qk[:, b, 0:S - back], m_cw[:, b, 3 - back:4 - back],
                                  m_conv[:, b, back:S], ALU.mult, ALU.add)
                    ins.then_inc(SEM["conv_ready"], 1)

            def mlstm(st):
                def exponent(h):
                    b = h % 2
                    dve.wait_ge(SEM["decay_spread"], at(st, "decay_spread", h + 1))
                    for s in range(2):
                        cols = slice(0, S) if s == 0 else slice(S, S + P)
                        src = PS[:, b, 0:S] if s == 0 else PS[:, b, P:S]
                        stt(m_w[:, b, cols], src, -1.0,
                            m_rT[:, s, h:h + 1].to_broadcast([P, S if s == 0 else P]), ALU.mult, ALU.add)
                    dve.drain()
                    ts(m_w[:, b, :], m_w[:, b, :], 0.0, None, ALU.min).then_inc(SEM["exponent_ready"], 1)

                exponent(0)
                for h in range(MH):
                    b = h % 2
                    if h + 1 < MH:
                        exponent(h + 1)
                    dve.wait_ge(SEM["exp_ready"], at(st, "exp_ready", h + 1))
                    diag = m_w[:, b, :].rearrange("p (a b) -> p a b", b=P)[:, 0:3:2, :]
                    tt(diag, diag, upto[:, :].unsqueeze(1).to_broadcast([P, 2, P]), ALU.mult)
                    dve.drain()
                    dve.wait_ge(SEM["scores_ready"], at(st, "scores_ready", h + 1))
                    if h >= 2:
                        dve.wait_ge(SEM["pv_ready"], at(st, "pv_ready", h - 1))
                    stt(m_p[:, b, :], PS[:, 2 + b, 0:3 * P], MQK ** -0.5, m_w[:, b, :], ALU.mult, ALU.mult
                        ).then_inc(SEM["probs_ready"], 1)
                    dve.wait_ge(SEM["pv_ready"], at(st, "pv_ready", h + 1))
                    num = PS[:, 4 + b, :].rearrange("p (t n) -> p t n", t=2)
                    den = m_den.rearrange("p (a b) -> p a b", a=4)
                    cp(den[:, 0, 0:2].unsqueeze(2), num[:, :, MV:MV + 1])
                    dve.drain()
                    stt(den[:, 1, 0:2], den[:, 0, 0:2], -1.0, den[:, 0, 0:2], ALU.mult, ALU.max)
                    dve.drain()
                    tt(den[:, 2, 0:2].unsqueeze(2), den[:, 1, 0:2].unsqueeze(2), m_floor[:, :, h:h + 1], ALU.max)
                    dve.drain()
                    v.reciprocal(den[:, 3, 0:2], den[:, 2, 0:2])
                    dve.drain()
                    for t in range(NT):
                        ts(m_h[:, t, h * MV:(h + 1) * MV], num[:, t, 0:MV], den[:, 3, t:t + 1], None, ALU.mult)
                    dve.drain().then_inc(SEM["pv_taken"], 1)

            def subkeys(st):
                for t in range(NT):
                    for b in range(1, 4, 2):
                        n = t * 4 + b
                        if n == 7:
                            dve.wait_ge(tile_used, used(st["tile0"]))
                        else:
                            dve.wait_ge(SEM["bank_ready"], at(st, "bank_ready", n + 1))
                        cp(SCORE[:, t, 4 * b:4 * b + 4, :], PS[:, n, :].rearrange("p (a b) -> p a b", b=P))

            def best16(rows, vals, idx):
                for r, x, i in zip(rows, vals, idx):
                    v.max(x[:, 0:8], r)
                dve.drain()
                for r, x, i in zip(rows, vals, idx):
                    v.max_index(i[:, 0:8], x[:, 0:8], r)
                dve.drain()
                for r, x, i in zip(rows, vals, idx):
                    v.match_replace(out=r, in_to_replace=x[:, 0:8], in_values=r, imm_value=-HUGE)
                dve.drain()
                for r, x, i in zip(rows, vals, idx):
                    v.max(x[:, 8:16], r)
                dve.drain()
                for r, x, i in zip(rows, vals, idx):
                    v.max_index(i[:, 8:16], x[:, 8:16], r)
                dve.drain()

            def topk(st):
                every = [(t, h, p) for t in range(NT) for h in range(PH) for p in range(2)]
                best16([SCORE[:, t, 2 * h + p, :] for t, h, p in every], [TOPV[:, t, h, p, :] for t, h, p in every],
                       [TOPI[:, t, h, p, :] for t, h, p in every])
                cp(TOPIF[:, :, :, :, :].rearrange("p a b c e -> p (a b c e)"),
                   TOPI[:, :, :, :, :].rearrange("p a b c e -> p (a b c e)"))
                full = [P, PH, PTOP, PTOP]
                for t in range(NT):
                    tt(CAND[:, t, :, :].rearrange("p h (a b) -> p h a b", b=PTOP),
                       TOPV[:, t, :, 0, :].unsqueeze(3).to_broadcast(full),
                       TOPV[:, t, :, 1, :].unsqueeze(2).to_broadcast(full), ALU.add)
                dve.drain()
                both = [(t, h) for t in range(NT) for h in range(PH)]
                best16([CAND[:, t, h, :] for t, h in both], [BESTV[:, t, h, :] for t, h in both],
                       [BESTI[:, t, h * PTOP:(h + 1) * PTOP] for t, h in both])
                shape = [P, NT, PH, PTOP]
                cp(PSUMS.rearrange("p (a b) -> p a b", b=PH), BESTV[:, :, :, 0])
                ts(BROW, BESTI, 4, None, ALU.logical_shift_right)
                ts(BCOL, BESTI, PTOP - 1, None, ALU.bitwise_and)
                dve.drain()
                tt(BESTV, BESTV, PSUMS.rearrange("p (a b) -> p a b", b=PH).unsqueeze(3).to_broadcast(shape),
                   ALU.subtract).then_inc(SEM["top_shifted"], 1)
                cp(BROWF, BROW)
                cp(BCOLF, BCOL)
                dve.drain()
                for t in range(NT):
                    for place, half, out in ((BROWF, 0, EXPROW), (BCOLF, 1, EXPCOL)):
                        tt(HOT, place[:, t, :].rearrange("p (h k) -> p h k", k=PTOP).unsqueeze(3).to_broadcast(full),
                           iota16[:, :].unsqueeze(1).unsqueeze(1).to_broadcast(full), ALU.is_equal)
                        dve.drain()
                        tt(HOT, HOT, TOPIF[:, t, :, half, :].unsqueeze(2).to_broadcast(full), ALU.mult)
                        dve.drain()
                        v.tensor_reduce(out=out[:, t, :].rearrange("p (h k) -> p h k", k=PTOP), in_=HOT,
                                        axis=AX.X, op=ALU.add)
                        dve.drain()
                stt(EXPERT, EXPROW, float(PK), EXPCOL, ALU.mult, ALU.add)
                dve.wait_ge(SEM["top_exp"], at(st, "top_exp", 1))
                v.tensor_reduce(out=PSUMS.rearrange("p (a b) -> p a b", b=PH), in_=BESTV, axis=AX.X, op=ALU.add)
                dve.drain()
                v.reciprocal(PSUMS, PSUMS)
                dve.drain()
                tt(GATE.rearrange("p t (h k) -> p t h k", k=PTOP), BESTV,
                   PSUMS.rearrange("p (a b) -> p a b", b=PH).unsqueeze(3).to_broadcast(shape), ALU.mult)

            def gather(st):
                m0 = st["gather0"] * NT * PSLOTS
                for t in range(NT):
                    with dve.Fori(0, PH) as i:
                        for ab in range(2):
                            n = t * PSLOTS + ab * BATCH
                            for q in range(BATCH):
                                dve.wait_ge(u_loaded[q], 16 * ((m0 + n) // BATCH + 1) + 32 * i)
                                v.tensor_tensor_reduce(out=UROWS[:, q, :], in0=UROWS[:, q, :], in1=H[:, t, :], scale=1.0,
                                                       scalar=0.0, op0=ALU.mult, op1=ALU.add,
                                                       accum_out=DOTS[:, ab, q:q + 1]
                                                       ).then_inc(SEM["expert_free"], 1)
                            dve.drain().then_inc(SEM["dots_ready"], 1)
                            dve.wait_ge(SEM["gelu_ready"], at(st, "gelu_ready", n // BATCH + 1) + 2 * i)
                            dve.wait_ge(SEM["diag_ready"], at(st, "diag_ready", t * PSLOTS) + PTOP * i)
                            tt(WEIGHTS[:, ab, :], GELU[:, ab, :], GATE[:, t, bass.ds(i * PTOP + ab * BATCH, BATCH)],
                               ALU.mult).then_inc(SEM["weights_ready"], 1)
                dve.wait_ge(SEM["mixed"], at(st, "mixed", 1))

            def mix_in(st):
                for t in range(NT):
                    tt(H[:, t, :], PS[:, 2 * t:2 * t + 2, :].rearrange("p a b -> p (a b)"), mod(5), ALU.mult)
                dve.drain()
                for t in range(NT):
                    tt(X[:, t, :], X[:, t, :], H[:, t, :], ALU.add)

            def stick(st):
                view = lambda b: b.rearrange("p (a b) -> p a b", b=TW)

                def masked(b):
                    for x in (b[:, 0:2 * TW].rearrange("p (h t) -> p h t", t=S)[:, :, 0:P],
                              b[:, 2 * TW:3 * TW].rearrange("p (h t) -> p h t", t=P)):
                        ins = tt(x, x, before[:, :].unsqueeze(1).to_broadcast([P, HG, P]), ALU.mult)
                    return ins

                for g in range(SH // HG):
                    dve.wait_ge(SEM["soft_ready"], at(st, "soft_ready", g + 1))
                    z = PS[:, 0:3, :]
                    stt(view(k_lost), z, 0.0, view(k_log), ALU.max, ALU.add)
                    stt(view(k_exp), z, 0.0, view(k_log), ALU.min, ALU.subtract)
                    dve.drain()
                    masked(k_lost)
                    dve.drain().then_inc(SEM["log_in"], 1)
                    dve.wait_ge(SEM["between_ready"], at(st, "between_ready", g + 1))
                    tt(view(k_exp), view(k_exp), PS[:, 3:6, :], ALU.subtract)
                    dve.drain()
                    ts(k_exp, k_exp, 0.0, None, ALU.min).then_inc(SEM["exponent_ready"], 1)
                    dve.wait_ge(SEM["exp_ready"], at(st, "exp_ready", g + 1))
                    masked(k_att)
                    dve.drain().then_inc(SEM["probs_ready"], 1)
                    dve.wait_ge(SEM["pv_ready"], at(st, "pv_ready", g + 1))
                    cp(H[:, :, g * 256:(g + 1) * 256], PS[:, 6, :].rearrange("p (t n) -> p t n", t=2)
                       ).then_inc(SEM["pv_taken"], 1)

            def softmax(st):
                prob, probT = soft_bufs(st)
                sums, nmax, rsum = soft_small(st)
                for g in range(AH // HG):
                    dve.wait_ge(SEM["scores_ready"], at(st, "scores_ready", g + 1))
                    early = prob[:, 0:TW].rearrange("p (h n) -> p h n", n=P)
                    late = prob[:, TW:3 * TW].rearrange("p (h n) -> p h n", n=S)
                    tt(early, PS[:, 0, :].rearrange("p (h n) -> p h n", n=P),
                       causal[:, P:S].unsqueeze(1).to_broadcast([P, HG, P]), ALU.add)
                    tt(late, PS[:, 1:3, :].rearrange("p a (h n) -> p (a h) n", n=S),
                       causal[:, :].unsqueeze(1).to_broadcast([P, HG, S]), ALU.add)
                    dve.drain()
                    v.tensor_reduce(out=nmax[:, 0:HG], in_=early, axis=AX.X, op=ALU.max, negate=True)
                    v.tensor_reduce(out=nmax[:, HG:2 * HG], in_=late, axis=AX.X, op=ALU.max, negate=True)
                    dve.drain().then_inc(SEM["max_ready"], 1)
                    dve.wait_ge(SEM["probsT_ready"], at(st, "probsT_ready", 3 * g + 2))
                    cp(probT[:, TW:2 * TW], PS[:, 4, :]).then_inc(SEM["probsT_taken1"], 1)
                    dve.wait_ge(SEM["exp_ready"], at(st, "exp_ready", g + 1))
                    v.reciprocal(rsum, sums)
                    dve.drain()
                    dve.wait_ge(SEM["pv_ready"], at(st, "pv_ready", g + 1))
                    for t in range(NT):
                        ins = tt(H[:, t, g * 256:(g + 1) * 256].rearrange("p (h n) -> p h n", n=AV),
                                 PS[:, 6, t * 256:(t + 1) * 256].rearrange("p (h n) -> p h n", n=AV),
                                 rsum[:, t * HG:(t + 1) * HG].unsqueeze(2).to_broadcast([P, HG, AV]), ALU.mult)
                    dve.drain().then_inc(SEM["pv_taken"], 1)

            def mla_keys(st):
                for t in range(NT):
                    k = st["k"][:, t, :].rearrange("p (h e) -> p h e", e=MLA_D)
                    cp(k[:, :, 0:NOPE], st["kv"][:, t, :].rearrange("p (h e) -> p h e", e=2 * AV)[:, :, 0:NOPE])
                    cp(k[:, :, NOPE:MLA_D],
                       st["z"][:, t, MLA_Q + MLA_KV:800].unsqueeze(1).to_broadcast([P, AH, ROPE]))

            def rope(st):
                half = ROPE // 2
                dve.wait_ge(inputs_loaded, 16 * 5)
                dve.wait_ge(rope_loaded, 16)
                cp(r_pos, posi[:, :])
                dve.drain()
                ang = r_ang.rearrange("p (c t n) -> p c t n", c=2, n=half)
                turns = r_turn.rearrange("p (c t n) -> p c t n", c=2, n=half)
                for t in range(NT):
                    ts(ang[:, 1, t, :], r_freq, r_pos[:, t:t + 1], None, ALU.mult)
                dve.drain()
                ts(turns[:, 1, :, :], ang[:, 1, :, :], 1.0 / (2 * math.pi), None, ALU.mult)
                dve.drain()
                cp(r_int, r_turn[:, 32:64])
                dve.drain()
                cp(r_turn[:, 32:64], r_int)
                dve.drain()
                big = 6.28125
                stt(ang[:, 1], turns[:, 1], -big, ang[:, 1], ALU.mult, ALU.add)
                dve.drain()
                stt(ang[:, 1], turns[:, 1], -(2 * math.pi - big), ang[:, 1], ALU.mult, ALU.add)
                dve.drain()
                ts(ang[:, 0], ang[:, 1], math.pi / 2, None, ALU.add)
                dve.drain()
                for above, sign in ((ALU.is_gt, -1.0), (ALU.is_lt, 1.0)):
                    ts(r_turn, r_ang, -sign * math.pi, sign * 2 * math.pi, above, ALU.mult)
                    dve.drain()
                    tt(r_ang, r_ang, r_turn, ALU.add)
                    dve.drain()
                ts(r_ang, r_ang, 3.1415925, -3.1415925, ALU.min, ALU.max).then_inc(SEM["angles_ready"], 1)
                dve.wait_ge(SEM["sines_ready"], at(st, "sines_ready", 1))
                cs = r_cs.rearrange("p (c t n) -> p c t n", c=2, n=half)
                tmp = r_tmp.rearrange("p (c h n) -> p c h n", c=4, n=half)
                for x in st["parts"]:
                    for t in range(NT):
                        y = x[:, t, :].rearrange("p (h e) -> p h e", e=MLA_D)
                        x1, x2 = y[:, :, NOPE:NOPE + half], y[:, :, NOPE + half:MLA_D]
                        cos, sin = (cs[:, c, t, :].unsqueeze(1).to_broadcast([P, AH, half]) for c in range(2))
                        for n, (a, b) in enumerate(((x1, cos), (x2, sin), (x1, sin), (x2, cos))):
                            tt(tmp[:, n], a, b, ALU.mult)
                        dve.drain()
                        tt(x1, tmp[:, 0], tmp[:, 1], ALU.subtract)
                        tt(x2, tmp[:, 2], tmp[:, 3], ALU.add)
                        dve.drain()

            def ffn(st):
                def one(q, lap):
                    dve.wait_ge(SEM["hidden_silu"], at(st, "hidden_silu", q + 1) + lap * RING)
                    if not isinstance(lap, int) or q >= RING:
                        dve.wait_ge(tile_used, used(st["tile0"] + q - RING, lap))
                    tt(f_hidden[:, q % RING, :], f_gate[:, q % RING, :], PS[:, q % RING, S:2 * S], ALU.mult
                       ).then_inc(SEM["hidden_ready"], 1)
                hidden_loop(dve, one)
                dve.wait_ge(SEM["mixed"], at(st, "mixed", 1))
                for t in range(NT):
                    stt(X[:, t, :], PS[:, 4 + 2 * t:6 + 2 * t, :].rearrange("p a b -> p (a b)"), 0.5, X[:, t, :],
                        ALU.mult, ALU.add)

            parts = dict(ada=ada, norm=norm, linear=linear, linearT=linearT, gates=gates, conv=conv, mlstm=mlstm,
                         headnorm=headnorm, turn=lambda st: taken(st, st["jobs"]), subkeys=subkeys, topk=topk,
                         gather=gather, mix_in=mix_in, stick=stick, softmax=softmax, mla_keys=mla_keys, rope=rope,
                         ffn=ffn)
            for st in STAGES:
                enter(dve, st)
                if st["kind"] in parts:
                    parts[st["kind"]](st)
                leave(dve)


def kernel(**inputs):
    from concourse import bacc
    from concourse.bass_utils import run_bass_kernel_spmd

    a = {k: np.asarray(v) for k, v in inputs.items()}

    def tiles(w, width):
        k, n = w.shape
        w = w.reshape(k // P, P, n // width, width).transpose(2, 1, 0, 3)
        return np.ascontiguousarray(w.reshape(n // width, P, (k // P) * width))

    def swiglu(w_in, w_out):
        g = tiles(w_in[:, :FF], P)
        u = tiles(w_in[:, FF:], P)
        return np.concatenate([g, u, w_out.reshape(FB, P, D)], axis=2)

    def tokens(x):
        return np.ascontiguousarray(x.reshape(NT, P, -1).transpose(1, 0, 2))

    def columns(x):
        return np.ascontiguousarray(x.reshape(-1, P).T)

    t = {"x": tokens(a["x"][0]), "c": columns(a["c"][0])}
    for i in range(2):
        t[f"ada_w{i}"] = tiles(a["ada_w"][i], TW)
        t[f"ada_b{i}"] = a["ada_b"][i]
        t[f"norm_mix_g{i}"] = a["norm_mix_g"][i]
        t[f"norm_ffn_g{i}"] = a["norm_ffn_g"][i]
        t[f"peer_w_q{i}"] = tiles(a["peer_w_q"][i], TW)
        t[f"sub_keys{i}"] = a["peer_sub_keys"][i].transpose(2, 0, 1).reshape(1, P, 2 * PK)
        t[f"peer_u{i}"] = a["peer_u"][i]
        t[f"peer_v{i}"] = a["peer_v"][i]
        t[f"ffn1_{i}"] = swiglu(a["ffn1_w_in_2"][i], a["ffn1_w_out_2"][i])
        t[f"ffn2_{i}"] = swiglu(a["ffn2_w_in_2"][i], a["ffn2_w_out_2"][i])
        t[f"ple_gate{i}"] = tiles(a["ple_w_gate_2"][i], TW)
        t[f"ple_proj{i}"] = tiles(a["ple_w_proj_2"][i], TW)
        t[f"p{i}"] = tokens(a["p_2"][i, 0])
        t[f"g_ffn1_{i}"] = a["g_ffn1_2"][i]
        t[f"g_mix_{i}"] = a["g_mix_2"][i]
        t[f"g_ffn2_{i}"] = a["g_ffn2_2"][i]
        t[f"g_ple{i}"] = a["g_ple_2"][i]
    w = a["ma_w_in"][0]
    t["ma_w_qk"] = tiles(w[:, :D], TW)
    t["ma_w_vo"] = tiles(w[:, D:3 * D], TW)
    t["ma_w_g"] = tiles(w[:, 3 * D:], 2 * MH)
    t["ma_b_if"] = a["ma_b_if"][0].reshape(2, MH).T
    t["conv_w"] = a["ma_conv_w"][0].reshape(4, 8, P).transpose(2, 1, 0)
    t["ma_hnorm_g"] = a["ma_hnorm_g"][0].reshape(-1)
    t["ma_w_out"] = tiles(a["ma_w_out"][0], TW)
    t["kv_ada_w"] = tiles(a["kv_ada_w"], TW)
    t["kv_ada_b"] = a["kv_ada_b"]
    t["kv_norm_g"] = a["kv_norm_g"]
    t["kv_w"] = tiles(a["kv_w"], TW)
    t["k_norm_g"] = a["k_norm_g"]
    t["sb_w_q"] = tiles(a["sb_w_q"][0], TW)
    t["sb_q_norm_g"] = a["sb_q_norm_g"][0]
    t["sb_w_out"] = tiles(a["sb_w_out"][0], TW)
    t["mla_w_in"] = tiles(a["mla_w_in_2"][0], 400)
    t["mla_g_q_lat"] = a["mla_g_q_lat_2"][0]
    t["mla_w_uq"] = tiles(a["mla_w_uq_2"][0], TW)
    t["mla_g_kv_lat"] = a["mla_g_kv_lat_2"][0]
    t["mla_w_ukv"] = tiles(a["mla_w_ukv_2"][0], TW)
    t["mla_g_qn"] = a["mla_g_qn_2"][0]
    t["mla_g_kn"] = a["mla_g_kn_2"][0]
    t["mla_w_o"] = tiles(a["mla_w_o_2"][0], TW)
    w = a["fox_w_in_2"][0]
    t["fox_w_in"] = tiles(w[:, :3 * D], TW)
    t["fox_w_g"] = tiles(w[:, 3 * D:], AH)
    t["fox_b_f"] = a["fox_b_f_2"][0].reshape(AH, 1)
    t["fox_g_qn"] = a["fox_g_qn_2"][0]
    t["fox_g_kn"] = a["fox_g_kn_2"][0]
    t["fox_w_o"] = tiles(a["fox_w_o_2"][0], TW)
    t["positions"] = a["positions_2"][0].reshape(NT, P).T
    t["rope_freq"] = (10000.0 ** (-np.arange(0, ROPE, 2, dtype=np.float32) / ROPE)).astype(np.float32)

    nc = bacc.Bacc("TRN2", target_bir_lowering=False, num_devices=1)
    arrays, d = {}, {}
    for name, x in t.items():
        x = np.ascontiguousarray(x)
        arrays["in_" + name] = x
        d[name] = nc.dram_tensor("in_" + name, x.shape, mybir.dt.from_np(x.dtype), kind="ExternalInput").ap()
    d["out"] = nc.dram_tensor("out_0", (P, NT, D), F32, kind="ExternalOutput").ap()
    build(nc, d)
    r = run_bass_kernel_spmd(nc, [arrays], core_ids=[0])
    out = np.asarray(r.results[0]["out_0"])
    return np.ascontiguousarray(out.transpose(1, 0, 2)).reshape(1, S, D)
```

```python
import math
from contextlib import ExitStack

import numpy as np

import concourse.bass as bass
from concourse import mybir

F32 = mybir.dt.float32
F32R = mybir.dt.float32r
I32 = mybir.dt.int32
U32 = mybir.dt.uint32
ALU = mybir.AluOpType
ACT = mybir.ActivationFunctionType
AX = mybir.AxisListType

P = 128
S = 256
NT = S // P
D = 1024
KD = D // P
TW = 512
EPS = 1e-6
HUGE = 3.0e38

MH, MQK, MV = 8, 64, 128
SH, SD = 16, 64
PH, PK, PTOP = 8, 128, 16
PSLOTS = PH * PTOP
FF = 2816
FB = FF // P
AH = 16
MLA_Q, MLA_KV, NOPE, ROPE, AV = 512, 256, 64, 32, 64
MLA_D = NOPE + ROPE
FOX_D = 64
HG = 4
RING = 6
UNIT = 2 * TW
PAIRS = 3
BATCH = 8


def build(nc, d):
    ctx = ExitStack()
    with ctx:
        def sb(name, shape, dt=F32):
            return ctx.enter_context(nc.sbuf_tensor("sb_" + name, shape, dt))

        def sem(name):
            return ctx.enter_context(nc.semaphore(name))

        X = sb("x", [P, NT, D])
        H = sb("h", [P, NT, D])
        XT = (sb("xT_hi", [P, KD, S], F32R), sb("xT_lo", [P, KD, S], F32R))
        MOD = sb("mod", [P, 6 * D])
        GAIN = sb("gain", [P, 2, D])
        w_at = nc.sbuf_base
        W = sb("w", [P, RING, UNIT])
        WL = nc.alloc_sbuf_tensor_at("sb_w_lo", [P, RING, UNIT], F32R, offset=w_at)
        WH = sb("w_hi", [P, RING, UNIT], F32R)
        CB = (sb("cb_hi", [P, KD, P], F32R), sb("cb_lo", [P, KD, P], F32R))
        ident = sb("ident", [P, P])
        ones = sb("ones", [P, P])
        after = sb("after", [P, P])
        before = sb("before", [P, P])
        upto = sb("upto", [P, P])
        causal = sb("causal", [P, S])
        zrow = sb("zrow", [P, TW])
        iota16 = sb("iota16", [P, 16])
        eps = sb("eps", [P, 1])
        ccol = sb("ccol", [P, KD])
        ss = sb("ss", [P, 32])
        rms = sb("rms", [P, 32])
        rs = sb("rs", [P, 32])
        small = sb("small", [P, 256])
        bias8 = sb("bias8", [16, 2])
        bias16 = sb("bias16", [16, 1])
        posi = sb("posi", [P, NT], I32)
        rope_int = sb("rope_int", [P, NT * ROPE // 2], I32)
        r_freq_own = sb("rope_freq", [P, ROPE // 2])
        ARENA = 18432
        arena_at = nc.sbuf_base
        A = sb("arena", [P, ARENA])
        AR = nc.alloc_sbuf_tensor_at("sb_arena_r", [P, ARENA], F32R, offset=arena_at)
        PS = ctx.enter_context(nc.psum_tensor("ps", [P, 8, TW], F32))

        def part(start, *shape, of=None):
            n = int(np.prod(shape))
            assert start + n <= ARENA, (start, shape)
            v = (A if of is None else of)[:, start:start + n]
            if len(shape) == 2:
                v = v.rearrange("p (a b) -> p a b", b=shape[1])
            elif len(shape) == 3:
                v = v.rearrange("p (a b c) -> p a b c", b=shape[1], c=shape[2])
            elif len(shape) == 4:
                v = v.rearrange("p (a b c e) -> p a b c e", b=shape[1], c=shape[2], e=shape[3])
            return v

        STAGES = []

        def stage(kind, **kw):
            kw["kind"] = kind
            kw["n"] = len(STAGES)
            STAGES.append(kw)

        gains = []

        def norm(src, width, gain, shift=None, scale=None, dst=None):
            gains.append((gain, width))
            stage("norm", src=src, width=width, gain=len(gains) - 1, shift=shift, scale=scale,
                  dst=dst or (lambda t: H[:, t, 0:width]))

        def turn(jobs):
            stage("turn", jobs=jobs)

        def linear(name, kc, tiles, width, out):
            stage("linear", weights=name, kc=kc, tiles=tiles, width=width, out=out)

        def headnorm(src, heads, hd, gain, factor=1.0, times=None):
            gains.append((gain, heads * hd if times else hd))
            stage("headnorm", src=src, heads=heads, hd=hd, gain=len(gains) - 1, factor=factor, times=times)

        def model_norm(gain, shift=None, scale=None):
            norm(lambda t: X[:, t, :], D, gain, shift, scale)

        def mod(i):
            return MOD[:, i * D:(i + 1) * D]

        def copy_to(dst, width=TW):
            return lambda t, j: ("copy", dst[:, t, j * width:(j + 1) * width])

        def residual(gate):
            return lambda t, j: ("residual", X[:, t, j * TW:(j + 1) * TW],
                                 None if gate is None else gate[:, j * TW:(j + 1) * TW])

        def peer(layer):
            model_norm(f"norm_ffn_g{layer}", mod(3), mod(4))
            stage("linearT", weights=f"peer_w_q{layer}", tiles=4,
                  dst=(part(0, 16, S, of=AR), part(4096, 16, S, of=AR)))
            stage("subkeys", layer=layer, weights=f"sub_keys{layer}")
            stage("topk")
            stage("gather", layer=layer)
            stage("mix_in")

        def ffn(name, gain):
            model_norm(gain)
            stage("ffn", weights=name)

        stage("ada", weights="ada_w0", bias="ada_b0", tiles=12, dst=MOD, scales=(1, 4))
        model_norm("norm_mix_g0", mod(0), mod(1))
        m_qk, m_conv = part(0, 8, S), part(2048, 8, S)
        m_v = part(4096, NT, MH, MV + 1)
        m_o = part(6160, NT, D)
        m_h = part(8208, NT, D)
        stage("linearT", weights="ma_w_qk", tiles=2, dst=m_qk)
        stage("linear", weights="ma_w_vo", kc=KD, tiles=4, width=TW,
              out=lambda t, j: ("copy by ACT", m_v[:, t, 4 * j:4 * j + 4, 0:MV]) if j < 2
              else ("sigmoid", m_o[:, t, (j - 2) * TW:(j - 1) * TW]))
        stage("gates", weights="ma_w_g", groups=2, m=MH)
        stage("conv")
        stage("mlstm")
        headnorm(m_h, MH, MV, "ma_hnorm_g", times=m_o)
        turn([(lambda t, k: m_h[:, t, k * P:(k + 1) * P], KD, P, XT)])
        linear("ma_w_out", KD, 2, TW, residual(mod(2)))
        peer(0)

        stage("ada", weights="ada_w1", bias="ada_b1", tiles=12, dst=MOD, scales=(1, 4))
        KVMOD = part(14336, 2 * D)
        stage("ada", weights="kv_ada_w", bias="kv_ada_b", tiles=4, dst=KVMOD, scales=(1,))
        s_kv = part(0, NT, 2 * D)
        s_q = part(4096, NT, D)
        s_qT, s_kT = part(6144, SH, S), part(10240, SH, S)
        model_norm("kv_norm_g", KVMOD[:, 0:D], KVMOD[:, D:2 * D])
        linear("kv_w", KD, 4, TW, copy_to(s_kv))
        model_norm("norm_mix_g1", mod(0), mod(1))
        linear("sb_w_q", KD, 2, TW, copy_to(s_q))
        headnorm(s_kv[:, :, 0:D], SH, SD, "k_norm_g")
        headnorm(s_q, SH, SD, "sb_q_norm_g", factor=SD ** -0.5)
        turn([(lambda t, h: s_q[:, t, h * SD:(h + 1) * SD], SH, SD, s_qT),
              (lambda t, h: s_kv[:, t, h * SD:(h + 1) * SD], SH, SD, s_kT)])
        stage("stick", qT=s_qT, kT=s_kT, v=lambda s, h: s_kv[:, s, D + h * SD:D + (h + 1) * SD])
        turn([(lambda t, k: H[:, t, k * P:(k + 1) * P], KD, P, XT)])
        linear("sb_w_out", KD, 2, TW, residual(mod(2)))
        peer(1)

        def embed(i):
            model_norm(f"g_ple{i}")
            e_g, e_p = part(0, NT, D), part(2048, NT, 256)
            linear(f"ple_gate{i}", KD, 2, TW, lambda t, j: ("sigmoid", e_g[:, t, j * TW:(j + 1) * TW]))
            stage("fetch", name=f"p{i}", dst=e_p)
            turn([(lambda t, k: e_p[:, t, k * P:(k + 1) * P], 2, P, XT)])
            linear(f"ple_proj{i}", 2, 2, TW,
                   lambda t, j: ("residual", X[:, t, j * TW:(j + 1) * TW], e_g[:, t, j * TW:(j + 1) * TW]))

        ffn("ffn1_0", "g_ffn1_0")
        model_norm("g_mix_0")
        a_z = part(0, NT, 800)
        a_kv = MOD[:, 0:NT * 2 * D].rearrange("p (t n) -> p t n", t=NT)
        a_q = part(1600, NT, AH * MLA_D)
        a_k = part(4672, NT, AH * MLA_D)
        a_qT, a_kT = part(7744, AH, S), part(11840, AH, S)
        linear("mla_w_in", KD, 2, 400, copy_to(a_z, 400))
        norm(lambda t: a_z[:, t, 0:MLA_Q], MLA_Q, "mla_g_q_lat")
        linear("mla_w_uq", MLA_Q // P, 3, TW, copy_to(a_q))
        norm(lambda t: a_z[:, t, MLA_Q:MLA_Q + MLA_KV], MLA_KV, "mla_g_kv_lat")
        linear("mla_w_ukv", MLA_KV // P, 4, TW, copy_to(a_kv))
        stage("mla_keys", z=a_z, kv=a_kv, k=a_k)
        headnorm(a_q, AH, MLA_D, "mla_g_qn", factor=MLA_D ** -0.5)
        headnorm(a_k, AH, MLA_D, "mla_g_kn")
        stage("rope", parts=(a_q, a_k))
        turn([(lambda t, h: a_q[:, t, h * MLA_D:(h + 1) * MLA_D], AH, MLA_D, a_qT),
              (lambda t, h: a_k[:, t, h * MLA_D:(h + 1) * MLA_D], AH, MLA_D, a_kT)])
        stage("softmax", qT=a_qT, kT=a_kT, dk=MLA_D, decay=False, work=1600,
              v=lambda s, h: a_kv[:, s, h * 2 * AV + AV:(h + 1) * 2 * AV])
        turn([(lambda t, k: H[:, t, k * P:(k + 1) * P], KD, P, XT)])
        linear("mla_w_o", KD, 2, TW, residual(None))
        ffn("ffn2_0", "g_ffn2_0")
        embed(0)

        ffn("ffn1_1", "g_ffn1_1")
        model_norm("g_mix_1")
        f_z = part(0, NT, 3 * D)
        f_qT, f_kT = part(6144, AH, S), part(10240, AH, S)
        linear("fox_w_in", KD, 6, TW, copy_to(f_z))
        stage("gates", weights="fox_w_g", groups=1, m=AH)
        headnorm(f_z[:, :, 0:D], AH, FOX_D, "fox_g_qn", factor=FOX_D ** -0.5)
        headnorm(f_z[:, :, D:2 * D], AH, FOX_D, "fox_g_kn")
        turn([(lambda t, h: f_z[:, t, h * FOX_D:(h + 1) * FOX_D], AH, FOX_D, f_qT),
              (lambda t, h: f_z[:, t, D + h * FOX_D:D + (h + 1) * FOX_D], AH, FOX_D, f_kT)])
        stage("softmax", qT=f_qT, kT=f_kT, dk=FOX_D, decay=True, work=14336,
              v=lambda s, h: f_z[:, s, 2 * D + h * FOX_D:2 * D + (h + 1) * FOX_D])
        turn([(lambda t, k: H[:, t, k * P:(k + 1) * P], KD, P, XT)])
        linear("fox_w_o", KD, 2, TW, residual(None))
        ffn("ffn2_1", "g_ffn2_1")
        embed(1)

        stage_done = sem("stage_done")
        consts_ready = sem("consts_ready")
        inputs_loaded = sem("inputs_loaded")
        gain_loaded = [sem("gain_loaded0"), sem("gain_loaded1")]
        bias_loaded = sem("bias_loaded")
        fetched = sem("fetched")
        stored = sem("stored")
        w_loaded = [sem(f"w_loaded{q}") for q in range(RING)]
        unit_used = sem("unit_used")
        hi_ready = sem("hi_ready")
        lo_ready = sem("lo_ready")
        names = ["bank_ready", "bank_free0", "bank_free1", "rms_ready", "h_ready", "sq_ready", "sum_ready",
                 "turned", "turned_taken0", "turned_taken1",
                 "gates_in", "log_in", "log_out", "scan_ready", "rowsT_ready", "rows_taken", "floor_ready",
                 "decay_spread", "exponent_ready", "exp_ready", "scores_ready", "probs_ready", "pv_ready",
                 "pv_taken", "soft_ready", "between_ready", "max_ready", "probsT_ready",
                 "probsT_taken0", "probsT_taken1", "conv_ready",
                 "hidden_silu", "hidden_raw", "hidden_hi", "hidden_ready", 
                 "angles_ready", "sines_ready", "top_shifted", "top_exp",
                 "expert_free", "mix_free", "dots_ready", "gelu_ready", "weights_ready", "diag_ready",
                 "claimed", "indices_staged", "mixed"]
        SEM = {n: sem(n) for n in names}
        u_loaded = [sem(f"u_loaded{q}") for q in range(BATCH)]
        v_loaded = [sem(f"v_loaded{q}") for q in range(BATCH)]

        def counts(st):
            k = st["kind"]
            c = {}
            if k == "ada":
                c = dict(bank_free0=st["tiles"])
            elif k == "linear":
                c = dict(bank_ready=st["tiles"], bank_free0=st["tiles"], bank_free1=st["tiles"])
            elif k == "linearT":
                n = (4 if isinstance(st["dst"], tuple) else 2) * st["tiles"]
                c = dict(bank_ready=3 * st["tiles"], turned_taken0=n, turned_taken1=n)
            elif k == "gates":
                c = dict(gates_in=1, log_in=1, log_out=1)
                if st["groups"] == 2:
                    c.update(scan_ready=1, rowsT_ready=1, rows_taken=1, floor_ready=1)
            elif k == "norm":
                g = NT * -(-st["width"] // (4 * P))
                c = dict(rms_ready=1, h_ready=NT, turned=g, turned_taken0=g, turned_taken1=g)
            elif k == "turn":
                g = sum(NT * -(-j[1] // 4) for j in st["jobs"])
                n = g if isinstance(st["jobs"][0][3], tuple) else g // 2
                c = dict(turned=g, turned_taken0=n, turned_taken1=n)
            elif k == "headnorm":
                c = dict(sq_ready=1, sum_ready=1, rms_ready=1)
            elif k == "conv":
                c = dict(conv_ready=8)
            elif k == "mlstm":
                c = dict(decay_spread=MH, exponent_ready=MH, exp_ready=MH, scores_ready=MH, probs_ready=MH,
                         pv_ready=MH, pv_taken=MH)
            elif k == "subkeys":
                c = dict(bank_ready=7)
            elif k == "topk":
                c = dict(top_shifted=1, top_exp=1)
            elif k == "gather":
                n = NT * PSLOTS
                c = dict(expert_free=n, mix_free=n, dots_ready=n // BATCH, gelu_ready=n // BATCH,
                         weights_ready=n // BATCH, diag_ready=n, indices_staged=NT * PH, mixed=1)
            elif k == "stick":
                n = SH // HG
                c = dict(scores_ready=n, soft_ready=n, log_in=n, between_ready=n, exponent_ready=n, exp_ready=n,
                         probs_ready=n, pv_ready=n, pv_taken=n)
            elif k == "softmax":
                n = AH // HG
                c = dict(scores_ready=n, max_ready=n, exp_ready=n, probsT_ready=3 * n, probsT_taken0=2 * n,
                         probsT_taken1=n, pv_ready=n, pv_taken=n)
            elif k == "ffn":
                c = dict(hidden_silu=FB, hidden_raw=FB, hidden_hi=FB, hidden_ready=FB, mixed=1)
            elif k == "rope":
                c = dict(angles_ready=1, sines_ready=1)
            return c

        base = []
        running = {n: 0 for n in names}
        running.update(sines_ready=1, angles_ready=1, diag_ready=1)
        units_before = 0
        gathers_before = 0
        norms_before = 0
        ada_before = fetch_before = 0
        for st in STAGES:
            base.append(dict(running))
            for n_, v_ in counts(st).items():
                running[n_] += v_
            st["unit0"] = units_before
            st["units"] = {"ada": st.get("tiles", 0) * KD // 2, "linear": st.get("tiles", 0) * st.get("kc", 0) // 2,
                           "linearT": st.get("tiles", 0) * KD // 2, "gates": st.get("groups", 0), "subkeys": 1,
                           "ffn": 3 * FB}.get(st["kind"], 0)
            st["floats"] = {"linear": 2 * st.get("width", 0), "subkeys": 2 * PK}.get(st["kind"], UNIT)
            units_before += st["units"]
            st["gather0"] = gathers_before
            gathers_before += st["kind"] == "gather"
            st["ada0"] = ada_before
            ada_before += st["kind"] == "ada"
            st["fetch0"] = fetch_before
            fetch_before += st["kind"] == "fetch"

        def at(st, name, n=0):
            return base[st["n"]][name] + n

        def enter(eng, st):
            if st["n"]:
                eng.wait_ge(stage_done, 4 * st["n"])

        def leave(eng):
            eng.drain().then_inc(stage_done, 1)


        QUERY = (part(0, 16, S, of=AR), part(4096, 16, S, of=AR))
        SCORE = part(8192, NT, 16, PK)
        CAND = part(0, NT, PH, PTOP * PTOP)
        TOPV = part(12288, NT, PH, 2, PTOP)
        TOPI = part(12800, NT, PH, 2, PTOP).bitcast(U32)
        TOPIF = part(13312, NT, PH, 2, PTOP)
        BESTV = part(13824, NT, PH, PTOP)
        BESTI = part(14080, NT, PH * PTOP).bitcast(U32)
        BROW = part(14336, NT, PH * PTOP).bitcast(U32)
        BCOL = part(14592, NT, PH * PTOP).bitcast(U32)
        BROWF = part(14848, NT, PH * PTOP)
        BCOLF = part(15104, NT, PH * PTOP)
        HOT = part(4096, PH, PTOP, PTOP)
        EXPROW = part(15360, NT, PH * PTOP)
        EXPCOL = part(15616, NT, PH * PTOP)
        PSUMS = part(15872, NT * PH)
        GATE = part(18176, NT, PSLOTS)
        EXPERT = part(17920, NT, PSLOTS).bitcast(I32)
        UROWS = part(0, BATCH, D)
        VROWS = part(8192, BATCH, D)
        DIAG = part(16384, BATCH, P)
        PEER_SMALL = part(17408, 256)
        DOTS = PEER_SMALL[:, 0:16].rearrange("p (a b) -> p a b", a=2)
        GELU = PEER_SMALL[:, 16:32].rearrange("p (a b) -> p a b", a=2)
        WEIGHTS = PEER_SMALL[:, 32:48].rearrange("p (a b) -> p a b", a=2)
        STAGED = part(17696, 2, PTOP).bitcast(I32)

        R0 = 10256
        g_i = A[0:16, R0:R0 + S]
        g_f = A[0:16, R0 + S:R0 + 2 * S]
        g_t = A[0:16, R0 + 2 * S:R0 + 3 * S]
        g_e = A[0:16, R0 + 3 * S:R0 + 4 * S]
        g_b = A[0:16, R0 + 4 * S:R0 + 5 * S]
        g_r = A[0:16, R0 + 5 * S:R0 + 6 * S]
        g_m = A[0:16, R0 + 6 * S:R0 + 7 * S]
        g_floor = A[0:16, R0 + 7 * S:R0 + 8 * S]
        m_rT = part(R0 + 8 * S, NT, MH)
        m_floor = part(R0 + 8 * S + 16, NT, MH)
        m_den = part(R0 + 8 * S + 32, 8)
        m_w = part(R0 + 8 * S + 64, 2, 3 * P)
        m_p = part(R0 + 8 * S + 64 + 6 * P, 2, 3 * P)
        m_cw = part(R0 + 8 * S + 64 + 12 * P, 8, 4)
        fx = small[0:16, :]
        f_l, f_e, f_c = (MOD[0:16, n * S:(n + 1) * S] for n in range(3))


        k_log = part(4096, 3 * TW)
        k_lost = part(14336, 3 * TW)
        k_exp = part(15872, 3 * TW)
        k_att = k_log

        def soft_bufs(st):
            w = st["work"]
            return A[:, w:w + 3 * TW], A[:, w + 3 * TW:w + 6 * TW]

        def soft_small(st):
            return small[:, 0:2 * HG], small[:, 16:16 + 2 * HG], small[:, 32:32 + 2 * HG]

        def head_square(st):
            n = st["heads"] * st["hd"]
            return H[:, :, :] if n <= D else part(7744, NT, n)

        def heads_of(src, t, n):
            return src[:, t, 0:n]

        f_gate = part(0, 2, S)
        f_raw = part(2 * S, 2, S)
        f_hidden = (part(4 * S, 2, S, of=AR), part(6 * S, 2, S, of=AR))

        r_freq = r_freq_own[:, :]
        r_pos = small[:, 0:NT]
        r_ang = small[:, 64:128]
        r_turn = small[:, 128:192]
        r_cs = small[:, 192:256]
        r_int = rope_int[:, :]
        r_tmp = part(16128, 4 * AH * (ROPE // 2))
        rope_loaded = sem("rope_loaded")

        block = ctx.enter_context(nc.Block())

        @block.sync
        def _(sp):
            sp.dma_start(X[:, :, :], d["x"]).then_inc(inputs_loaded, 16)

            def load(st, n, pos, turn):
                sp.wait_ge(unit_used, turn * RING + pos + 1)
                src = d[st["weights"]][n] if isinstance(n, int) else \
                    d[st["weights"]][bass.ds(n, 1)].rearrange("a p n -> (a p) n")
                sp.dma_start(W[:, pos % RING, 0:st["floats"]], src).then_inc(w_loaded[pos % RING], 16)

            for st in STAGES:
                units, pos = st["units"], st["unit0"]
                turns = units // RING if units >= 2 * RING else 0
                if turns:
                    with sp.Fori(0, turns) as i:
                        for q in range(RING):
                            load(st, i * RING + q, pos + q, i)
                for q in range(turns * RING, units):
                    load(st, q, pos + q, 0)
            sp.wait_ge(stage_done, 4 * len(STAGES))
            sp.dma_start(d["out"], X[:, :, :]).then_inc(stored, 16)
            sp.wait_ge(stored, 16)

        @block.gpsimd
        def _(pool):
            pool.memset(ident[:, :], 0.0)
            pool.memset(ones[:, :], 1.0)
            pool.memset(causal[:, :], 0.0)
            pool.memset(zrow[:, :], 0.0)
            pool.memset(eps[:, :], EPS)
            pool.memset(m_v[:, :, :, MV:MV + 1], 1.0)
            pool.iota(iota16[:, :], pattern=[[1, 16]], base=0, channel_multiplier=0,
                      allow_small_or_imprecise_dtypes=True)
            pool.drain()
            pool.affine_select(out=ident[:, :], in_=ident[:, :], compare_op=ALU.not_equal, fill=1.0,
                               base=0, pattern=[[-1, P]], channel_multiplier=1)
            pool.affine_select(out=after[:, :], in_=ones[:, :], compare_op=ALU.is_gt, fill=0.0,
                               base=0, pattern=[[-1, P]], channel_multiplier=1)
            pool.affine_select(out=before[:, :], in_=ones[:, :], compare_op=ALU.is_gt, fill=0.0,
                               base=0, pattern=[[1, P]], channel_multiplier=-1)
            pool.affine_select(out=upto[:, :], in_=ones[:, :], compare_op=ALU.is_ge, fill=0.0,
                               base=0, pattern=[[1, P]], channel_multiplier=-1)
            pool.affine_select(out=causal[:, :], in_=causal[:, :], compare_op=ALU.is_ge, fill=-HUGE,
                               base=P, pattern=[[-1, S]], channel_multiplier=1)
            pool.drain().then_inc(consts_ready, 1)

            def gather(st):
                u_dram, v_dram = d[f"peer_u{st['layer']}"], d[f"peer_v{st['layer']}"]
                n0 = st["gather0"] * NT * PSLOTS

                def claim(name, count):
                    pool.wait_ge(SEM[name], count)
                    pool.sem_inc(SEM["claimed"], 1)

                def fetch(t, i, e):
                    m = n0 + t * PSLOTS + i * PTOP
                    pool.tensor_copy(STAGED[:, e, :], EXPERT[:, t, bass.ds(i * PTOP, PTOP)]
                                     ).then_inc(SEM["indices_staged"], 1)
                    claim("indices_staged", at(st, "indices_staged", t * PH + 1) + i)
                    for ab in range(2):
                        for ring, table, free, loaded in ((UROWS, u_dram, "expert_free", u_loaded),
                                                          (VROWS, v_dram, "mix_free", v_loaded)):
                            for q in range(BATCH):
                                claim(free, m + ab * BATCH + q + 1)
                                pool.indirect_dma_start(
                                    ring[:, q, :], None, table,
                                    bass.IndirectOffsetOnAxis(ap=STAGED[:, e, ab * BATCH + q:ab * BATCH + q + 1],
                                                              axis=0)).then_inc(loaded[q], 16)

                for t in range(NT):
                    with pool.Fori(0, PH // 2) as i:
                        for e in range(2):
                            fetch(t, i * 2 + e, e)

            for st in STAGES:
                enter(pool, st)
                if st["kind"] == "gather":
                    gather(st)
                leave(pool)


        def used(pos, turn=0):
            return RING + pos + 1 + turn * RING

        def split_hi(act, st, q, turn=0):
            pos, n = st["unit0"] + q, st["floats"]
            act.wait_ge(w_loaded[pos % RING], (turn + pos // RING + 1) * 16)
            nc.scalar.activation(WH[:, pos % RING, 0:n], W[:, pos % RING, 0:n], ACT.Copy).then_inc(hi_ready, 1)

        def split_lo(dve, st, q, turn=0):
            pos, n = st["unit0"] + q, st["floats"]
            dve.wait_ge(hi_ready, pos + 1 + turn * RING)
            nc.vector.tensor_tensor(WL[:, pos % RING, 0:n], W[:, pos % RING, 0:n],
                                    WH[:, pos % RING, 0:n].bitcast(F32), ALU.subtract).then_inc(lo_ready, 1)

        def ffn_schedule(eng, unit, hidden):
            for q in range(5):
                unit(q, 0)
            hidden(0, 0)
            with eng.Fori(0, (FB - 2) // 2) as i:
                for b in range(2):
                    for q in range(3):
                        unit(5 + 3 * b + q, i)
                    hidden(b + 1, i)
            unit(3 * FB - 1, 0)
            hidden(FB - 1, 0)

        @block.tensor
        def _(pe):
            mm, tr = nc.tensor.matmul, nc.tensor.transpose
            pe.wait_ge(consts_ready, 1)
            pe.drain().then_inc(unit_used, RING)

            PASSES = ((0, 0), (0, 1), (1, 0))

            def unit_of(st, q, turn=0):
                pos = st["unit0"] + q
                pe.wait_ge(lo_ready, pos + 1 + turn * RING)
                return WH[:, pos % RING, :], WL[:, pos % RING, :]

            def moving(st, q, turn, lhs, kc, width, halves, free):
                per = kc // 2
                for u in range(per):
                    w = [x[:, 0:2 * width].rearrange("p (k n) -> p k n", n=width)
                         for x in unit_of(st, q * per + u, turn)]
                    for t in range(halves):
                        if u == 0 and free is not None:
                            pe.wait_ge(SEM[f"bank_free{t}"], at(st, f"bank_free{t}", q - PAIRS + 1) + free)
                        for k in range(2):
                            for n, (a, b) in enumerate(PASSES):
                                ins = mm(PS[:, 2 * (q % PAIRS) + t, 0:width], lhs(a, 2 * u + k, t), w[b][:, k, :],
                                         start=u + k + n == 0, stop=u == per - 1 and k == 1 and n == 2)
                        if t == halves - 1:
                            ins.then_inc(unit_used, 1)
                        elif u == per - 1:
                            ins.then_inc(SEM["bank_ready"], 1)

            def linear(st):
                for j in range(st["tiles"]):
                    moving(st, j, 0, lambda a, k, t: XT[a][:, k, t * P:(t + 1) * P], st["kc"], st["width"], NT,
                           0 if j >= PAIRS else None)

            def ada(st):
                if st["n"] == 0:
                    pe.wait_ge(SEM["angles_ready"], 1)
                tiles = st["tiles"]

                def one(j, turn, free):
                    moving(st, j, turn, lambda a, k, t: CB[a][:, k, :], KD, TW, 1, free)

                looped = tiles // PAIRS if tiles >= 2 * PAIRS else 0
                if looped:
                    for j in range(PAIRS):
                        one(j, 0, None)
                    with pe.Fori(1, looped) as i:
                        for j in range(PAIRS):
                            one(j, i * 2, i * PAIRS)
                for j in range(looped * PAIRS, tiles):
                    one(j, 0, 0 if j >= PAIRS else None)

            def linearT(st):
                for j in range(st["tiles"]):
                    for u in range(KD // 2):
                        w = [x.rearrange("p (k n) -> p k n", n=TW) for x in unit_of(st, j * KD // 2 + u)]
                        for b in range(4):
                            n = 4 * j + b
                            if u == 0 and n >= 8:
                                if isinstance(st["dst"], tuple):
                                    pe.wait_ge(SEM["turned_taken1"], at(st, "turned_taken1", n - 7))
                                else:
                                    pe.wait_ge(SEM[f"turned_taken{n % 2}"],
                                               at(st, f"turned_taken{n % 2}", (n - 8) // 2 + 1))
                            for k in range(2):
                                for m, (a, c) in enumerate(PASSES):
                                    ins = mm(PS[:, n % 8, 0:S], w[c][:, k, b * P:(b + 1) * P], XT[a][:, 2 * u + k, :],
                                             start=u + k + m == 0, stop=u == KD // 2 - 1 and k == 1 and m == 2)
                            if b == 3:
                                ins.then_inc(unit_used, 1)
                            elif u == KD // 2 - 1:
                                ins.then_inc(SEM["bank_ready"], 1)

            def gates(st):
                groups = st["groups"]
                for g in range(groups):
                    w = [x.rearrange("p (k n) -> p k n", n=P) for x in unit_of(st, g)]
                    for k in range(KD):
                        for n, (a, c) in enumerate(PASSES):
                            ins = mm(PS[:, g, 0:S], w[c][:, k, :], XT[a][:, k, :], start=k + n == 0,
                                     stop=k == KD - 1 and n == 2)
                    ins.then_inc(unit_used, 1)
                if groups == 2:
                    pe.wait_ge(SEM["scan_ready"], at(st, "scan_ready", 1))
                    for t in range(NT):
                        tr(PS[:, 2, t * MH:(t + 1) * MH], g_r[0:MH, t * P:(t + 1) * P], ident[0:MH, 0:MH])
                        ins = tr(PS[:, 3, t * MH:(t + 1) * MH], g_floor[0:MH, t * P:(t + 1) * P], ident[0:MH, 0:MH])
                    ins.then_inc(SEM["rowsT_ready"], 1)

            def transposes(st, jobs):
                n = 0
                for src, chunks, width, _ in jobs:
                    for t in range(NT):
                        for c0 in range(0, chunks, 4):
                            if n >= 8:
                                pe.wait_ge(SEM[f"turned_taken{n % 2}"],
                                           at(st, f"turned_taken{n % 2}", (n - 8) // 2 + 1))
                            for c in range(c0, min(c0 + 4, chunks)):
                                ins = tr(PS[0:width, n % 8, (c - c0) * P:(c - c0 + 1) * P], src(t, c), ident[:, :])
                            ins.then_inc(SEM["turned"], 1)
                            n += 1

            def norm(st):
                pe.wait_ge(SEM["h_ready"], at(st, "h_ready", NT))
                dst = st["dst"]
                transposes(st, [(lambda t, c: dst(t)[:, c * P:(c + 1) * P], st["width"] // P, P, XT)])

            def mlstm(st):
                q_of = lambda h: m_conv[(h % 2) * MQK:(h % 2 + 1) * MQK, h // 2, :]
                k_of = lambda h: m_conv[(h % 2) * MQK:(h % 2 + 1) * MQK, MH // 2 + h // 2, :]

                def scores(h):
                    b = h % 2
                    if h >= 2:
                        pe.wait_ge(SEM["probs_ready"], at(st, "probs_ready", h - 1))
                    mm(PS[:, b, 0:S], ident[0:MH, h:h + 1].to_broadcast([MH, P]), g_m[0:MH, :],
                       start=True, stop=True).then_inc(SEM["decay_spread"], 1)
                    mm(PS[:, 2 + b, 0:S], k_of(h)[:, 0:P], q_of(h), start=True, stop=True)
                    mm(PS[:, 2 + b, S:S + P], k_of(h)[:, P:S], q_of(h)[:, P:S], start=True, stop=True
                       ).then_inc(SEM["scores_ready"], 1)

                scores(0)
                for h in range(MH):
                    if h + 1 < MH:
                        scores(h + 1)
                    b = h % 2
                    pe.wait_ge(SEM["probs_ready"], at(st, "probs_ready", h + 1))
                    if h >= 2:
                        pe.wait_ge(SEM["pv_taken"], at(st, "pv_taken", h - 1))
                    mm(PS[:, 4 + b, 0:MV + 1], m_p[:, b, 0:P], m_v[:, 0, h, :], start=True, stop=True)
                    mm(PS[:, 4 + b, 256:256 + MV + 1], m_p[:, b, P:S], m_v[:, 0, h, :], start=True, stop=False)
                    mm(PS[:, 4 + b, 256:256 + MV + 1], m_p[:, b, S:S + P], m_v[:, 1, h, :], start=False, stop=True
                       ).then_inc(SEM["pv_ready"], 1)

            def subkeys(st):
                w = [x[:, 0:2 * PK].rearrange("p (k n) -> p k n", n=PK) for x in unit_of(st, 0)]
                for t in range(NT):
                    for b in range(16):
                        for n, (a, c) in enumerate(PASSES):
                            ins = mm(PS[:, t * 4 + b // 4, (b % 4) * P:(b % 4 + 1) * P],
                                     QUERY[a][:, b, t * P:(t + 1) * P], w[c][:, b % 2, :], start=n == 0, stop=n == 2)
                        if b % 4 == 3:
                            ins.then_inc(unit_used if t * 4 + b // 4 == 7 else SEM["bank_ready"], 1)

            def gather(st):
                for b in range(4):
                    mm(PS[:, b, :], zrow[:, 0:P], zrow[:, :], start=True, stop=False, skip_group_check=True)
                m0 = st["gather0"] * NT * PSLOTS
                for t in range(NT):
                    with pe.Fori(0, PH) as i:
                        for ab in range(2):
                            for q in range(BATCH):
                                n = t * PSLOTS + ab * BATCH + q
                                pe.wait_ge(v_loaded[q], 16 * ((m0 + n) // BATCH + 1) + 32 * i)
                                pe.wait_ge(SEM["diag_ready"], at(st, "diag_ready", n + 1) + PTOP * i)
                                for c in range(2):
                                    ins = mm(PS[:, 2 * t + c, :], DIAG[:, q, :], VROWS[:, q, c * TW:(c + 1) * TW],
                                             start=False, stop=False, skip_group_check=True)
                                ins.then_inc(SEM["mix_free"], 1)
                for b in range(4):
                    ins = mm(PS[:, b, :], zrow[:, 0:P], zrow[:, :], start=False, stop=True, skip_group_check=True)
                ins.then_inc(SEM["mixed"], 1)

            def stick(st):
                qT, kT, v = st["qT"], st["kT"], st["v"]
                for g in range(SH // HG):
                    for h in range(HG):
                        hh = g * HG + h
                        mm(PS[:, h // 2, (h % 2) * S:(h % 2 + 1) * S], kT[0:SD, hh, 0:P], qT[0:SD, hh, :],
                           start=True, stop=True)
                        ins = mm(PS[:, 2, h * P:(h + 1) * P], kT[0:SD, hh, P:S], qT[0:SD, hh, P:S],
                                 start=True, stop=True)
                    ins.then_inc(SEM["scores_ready"], 1)
                    pe.wait_ge(SEM["log_in"], at(st, "log_in", g + 1))
                    lost = k_lost
                    for n in range(2):
                        mm(PS[:, 3 + n, :], after[:, :], lost[:, n * TW:(n + 1) * TW], start=True, stop=False)
                        mm(PS[:, 3 + n, :].rearrange("p (h t) -> p h t", t=S)[:, :, P:S], ones[:, :],
                           lost[:, 2 * TW + 2 * n * P:2 * TW + (2 * n + 2) * P].rearrange("p (h t) -> p h t", t=P),
                           start=False, stop=True)
                    mm(PS[:, 5, :], after[:, :], lost[:, 2 * TW:3 * TW], start=True, stop=True
                       ).then_inc(SEM["between_ready"], 1)
                    pe.wait_ge(SEM["probs_ready"], at(st, "probs_ready", g + 1))
                    if g:
                        pe.wait_ge(SEM["pv_taken"], at(st, "pv_taken", g))
                    for h in range(HG):
                        hh = g * HG + h
                        o = lambda t: PS[:, 6, t * 256 + h * SD:t * 256 + (h + 1) * SD]
                        mm(o(0), k_att[:, h * S:h * S + P], v(0, hh), start=True, stop=True)
                        mm(o(1), k_att[:, h * S + P:(h + 1) * S], v(0, hh), start=True, stop=False)
                        ins = mm(o(1), k_att[:, 2 * TW + h * P:2 * TW + (h + 1) * P], v(1, hh), start=False, stop=True)
                    ins.then_inc(SEM["pv_ready"], 1)

            def softmax(st):
                qT, kT, v, dk = st["qT"], st["kT"], st["v"], st["dk"]
                prob, probT = soft_bufs(st)
                for g in range(AH // HG):
                    for h in range(HG):
                        hh = g * HG + h
                        for t, (bank, at_, n) in enumerate(((0, h * P, P), (1 + h // 2, (h % 2) * S, S))):
                            o = PS[:, bank, at_:at_ + n]
                            ins = mm(o, qT[0:dk, hh, t * P:(t + 1) * P], kT[0:dk, hh, 0:n],
                                     start=True, stop=not st["decay"])
                            if st["decay"]:
                                ins = mm(o, ident[0:AH, hh:hh + 1].to_broadcast([AH, P]), f_c[0:AH, 0:n],
                                         start=False, stop=True)
                    ins.then_inc(SEM["scores_ready"], 1)
                    pe.wait_ge(SEM["exp_ready"], at(st, "exp_ready", g + 1))
                    for n in range(3):
                        for c in range(4):
                            ins = tr(PS[:, 3 + n, c * P:(c + 1) * P], prob[:, (4 * n + c) * P:(4 * n + c + 1) * P],
                                     ident[:, :])
                        ins.then_inc(SEM["probsT_ready"], 1)
                    pe.wait_ge(SEM["probsT_taken0"], at(st, "probsT_taken0", 2 * g + 2))
                    pe.wait_ge(SEM["probsT_taken1"], at(st, "probsT_taken1", g + 1))
                    if g:
                        pe.wait_ge(SEM["pv_taken"], at(st, "pv_taken", g))
                    for h in range(HG):
                        hh = g * HG + h
                        o = lambda t: PS[:, 6, t * 256 + h * AV:t * 256 + (h + 1) * AV]
                        mm(o(0), probT[:, h * P:(h + 1) * P], v(0, hh), start=True, stop=True)
                        late = 4 * P + h * S
                        mm(o(1), probT[:, late:late + P], v(0, hh), start=True, stop=False)
                        ins = mm(o(1), probT[:, late + P:late + S], v(1, hh), start=False, stop=True)
                    ins.then_inc(SEM["pv_ready"], 1)

            def ffn(st):
                for b in range(4):
                    mm(PS[:, 4 + b, :], zrow[:, 0:P], zrow[:, :], start=True, stop=False, skip_group_check=True)

                def gate_up(q, f, turn, lap):
                    for a in range(2):
                        w = [x.rearrange("p (k n) -> p k n", n=P) for x in unit_of(st, q + a, turn)]
                        for k in range(KD):
                            for n, (x, c) in enumerate(PASSES):
                                ins = mm(PS[:, f % 2, a * S:(a + 1) * S], w[c][:, k, :], XT[x][:, k, :],
                                         start=k + n == 0, stop=k == KD - 1 and n == 2)
                        ins.then_inc(unit_used, 1)

                def down(q, f, turn, lap):
                    pe.wait_ge(SEM["hidden_ready"], at(st, "hidden_ready", f + 1) + lap)
                    w = unit_of(st, q, turn)
                    for t in range(NT):
                        for n, (x, c) in enumerate(PASSES):
                            for half in range(2):
                                ins = mm(PS[:, 4 + 2 * t + half, :], f_hidden[x][:, f % 2, t * P:(t + 1) * P],
                                         w[c][:, half * TW:(half + 1) * TW], start=False, stop=False,
                                         skip_group_check=True)
                    ins.then_inc(unit_used, 1)

                gate_up(0, 0, 0, 0)
                with pe.Fori(0, (FB - 2) // 2) as i:
                    for b in range(2):
                        gate_up(2 + 3 * b, b + 1, i, i * 2)
                        down(4 + 3 * b, b, i, i * 2)
                gate_up(3 * FB - 4, FB - 1, 0, 0)
                down(3 * FB - 2, FB - 2, 0, 0)
                down(3 * FB - 1, FB - 1, 0, 0)
                for b in range(4):
                    ins = mm(PS[:, 4 + b, :], zrow[:, 0:P], zrow[:, :], start=False, stop=True, skip_group_check=True)
                ins.then_inc(SEM["mixed"], 1)

            parts = dict(ada=ada, norm=norm, linear=linear, linearT=linearT, gates=gates, mlstm=mlstm,
                         turn=lambda st: transposes(st, st["jobs"]), subkeys=subkeys, gather=gather, stick=stick,
                         softmax=softmax, ffn=ffn)
            for st in STAGES:
                enter(pe, st)
                if st["kind"] in parts:
                    parts[st["kind"]](st)
                leave(pe)

        @block.scalar
        def _(act):
            f = nc.scalar.activation

            def load_gain(n):
                name, width = gains[n]
                act.dma_start(GAIN[:, n % 2, 0:width], d[name].partition_broadcast(P)).then_inc(gain_loaded[n % 2], 16)

            act.dma_start(ccol[:, :], d["c"]).then_inc(bias_loaded, 16)
            act.dma_start(bias8[0:MH, :], d["ma_b_if"]).then_inc(inputs_loaded, 16)
            act.dma_start(bias16[:, :], d["fox_b_f"]).then_inc(inputs_loaded, 16)
            act.dma_start(m_cw, d["conv_w"]).then_inc(inputs_loaded, 16)
            act.dma_start(posi[:, :], d["positions"]).then_inc(inputs_loaded, 16)
            act.dma_start(r_freq, d["rope_freq"].partition_broadcast(P)).then_inc(rope_loaded, 16)
            load_gain(0)
            act.wait_ge(bias_loaded, 16)
            f(ccol[:, :], ccol[:, :], ACT.Silu).then_inc(SEM["sines_ready"], 1)
            act.drain().then_inc(SEM["diag_ready"], 1)

            def linear(st):
                per = st["kc"] // 2
                for q in range(per):
                    split_hi(act, st, q)
                for j in range(st["tiles"]):
                    for q in range((j + 1) * per, min((j + 2) * per, st["units"])):
                        split_hi(act, st, q)
                    for t in range(NT):
                        what, dst, *_ = st["out"](t, j)
                        if what in ("sigmoid", "copy by ACT") or (what == "copy" and t == 0):
                            if t == 0:
                                act.wait_ge(SEM["bank_ready"], at(st, "bank_ready", j + 1))
                            else:
                                act.wait_ge(unit_used, used(st["unit0"] + (j + 1) * per - 1))
                            src = PS[:, 2 * (j % PAIRS) + t, 0:st["width"]]
                            if len(dst.shape) == 3:
                                src = src.rearrange("p (a b) -> p a b", b=dst.shape[2])
                            f(dst, src, ACT.Sigmoid if what == "sigmoid" else ACT.Copy
                              ).then_inc(SEM[f"bank_free{t}"], 1)

            def linearT(st):
                parts_ = isinstance(st["dst"], tuple)
                for q in range(4):
                    split_hi(act, st, q)
                for j in range(st["tiles"]):
                    for q in range(4 * j + 4, min(4 * j + 8, st["units"])):
                        split_hi(act, st, q)
                    for b in range(0, 4, 1 if parts_ else 2):
                        n = 4 * j + b
                        if b == 3:
                            act.wait_ge(unit_used, used(st["unit0"] + 4 * j + 3))
                        else:
                            act.wait_ge(SEM["bank_ready"], at(st, "bank_ready", 3 * j + b + 1))
                        f((st["dst"][0] if parts_ else st["dst"])[:, n, :], PS[:, n % 8, 0:S], ACT.Copy
                          ).then_inc(SEM["turned_taken0"], 1)

            def log_sigmoid_in(m, pre, a, e):
                f(a[0:m, :], pre[0:m, :], ACT.Abs)
                act.drain()
                f(e[0:m, :], a[0:m, :], ACT.Exp, scale=-1.0)
                act.drain()
                f(e[0:m, :], e[0:m, :], ACT.Ln, bias=1.0).then_inc(SEM["log_out"], 1)

            def gates(st):
                act.wait_ge(inputs_loaded, 16 * 5)
                for g in range(st["groups"]):
                    split_hi(act, st, g)
                act.wait_ge(unit_used, used(st["unit0"] + st["groups"] - 1))
                if st["groups"] == 2:
                    f(g_i[0:MH, :], PS[0:MH, 0, 0:S], ACT.Identity, bias=bias8[0:MH, 0:1])
                    f(g_f[0:MH, :], PS[0:MH, 1, 0:S], ACT.Identity, bias=bias8[0:MH, 1:2])
                    act.drain().then_inc(SEM["gates_in"], 1)
                    log_sigmoid_in(MH, g_f, g_t, g_e)
                    act.wait_ge(SEM["rowsT_ready"], at(st, "rowsT_ready", 1))
                    f(m_floor, PS[:, 3, 0:NT * MH].rearrange("p (a b) -> p a b", b=MH), ACT.Exp
                      ).then_inc(SEM["floor_ready"], 1)
                else:
                    f(fx, PS[0:AH, 0, 0:S], ACT.Identity, bias=bias16[:, 0:1])
                    act.drain().then_inc(SEM["gates_in"], 1)
                    log_sigmoid_in(AH, fx, f_l, f_e)

            def taken(st, jobs):
                n = 0
                for _, chunks, width, dst in jobs:
                    for t in range(NT):
                        for c0 in range(0, chunks, 4):
                            if n % 2 == 0 or isinstance(dst, tuple):
                                c1 = min(c0 + 4, chunks)
                                act.wait_ge(SEM["turned"], at(st, "turned", n + 1))
                                f((dst[0] if isinstance(dst, tuple) else dst)[0:width, c0:c1, t * P:(t + 1) * P],
                                  PS[0:width, n % 8, 0:(c1 - c0) * P].rearrange("p (a b) -> p a b", b=P),
                                  ACT.Copy).then_inc(SEM["turned_taken0"], 1)
                            n += 1

            def norm(st):
                if st["gain"] + 1 < len(gains):
                    load_gain(st["gain"] + 1)
                if st["n"] == 1:
                    act.wait_ge(inputs_loaded, 16 * 5)
                w = st["width"]
                for t in range(NT):
                    f(st["dst"](t), st["src"](t), ACT.Square, accum_out=ss[:, t:t + 1])
                act.drain()
                f(rms[:, 0:NT], ss[:, 0:NT], ACT.Sqrt, scale=1.0 / w, bias=eps[:, 0:1]
                  ).then_inc(SEM["rms_ready"], 1)
                taken(st, [(None, w // P, P, XT)])

            def headnorm(st):
                if st["gain"] + 1 < len(gains):
                    load_gain(st["gain"] + 1)
                n = st["heads"] * st["hd"]
                sq = head_square(st)
                for t in range(NT):
                    f(sq[:, t, 0:n], heads_of(st["src"], t, n), ACT.Square)
                act.drain().then_inc(SEM["sq_ready"], 1)
                act.wait_ge(SEM["sum_ready"], at(st, "sum_ready", 1))
                m = NT * st["heads"]
                f(rms[:, 0:m], ss[:, 0:m], ACT.Sqrt, scale=1.0 / st["hd"], bias=eps[:, 0:1]
                  ).then_inc(SEM["rms_ready"], 1)

            def conv(st):
                for b in range(8):
                    act.wait_ge(SEM["conv_ready"], at(st, "conv_ready", b + 1))
                    f(m_conv[:, b, :], m_conv[:, b, :], ACT.Silu)

            def mlstm(st):
                for h in range(MH):
                    act.wait_ge(SEM["exponent_ready"], at(st, "exponent_ready", h + 1))
                    f(m_w[:, h % 2, :], m_w[:, h % 2, :], ACT.Exp).then_inc(SEM["exp_ready"], 1)

            def subkeys(st):
                split_hi(act, st, 0)
                for t in range(NT):
                    for b in range(0, 4, 2):
                        n = t * 4 + b
                        act.wait_ge(SEM["bank_ready"], at(st, "bank_ready", n + 1))
                        f(SCORE[:, t, 4 * b:4 * b + 4, :], PS[:, n, :].rearrange("p (a b) -> p a b", b=P), ACT.Copy)

            def topk(st):
                act.wait_ge(SEM["top_shifted"], at(st, "top_shifted", 1))
                f(BESTV[:, :, :, :], BESTV[:, :, :, :], ACT.Exp).then_inc(SEM["top_exp"], 1)

            def gather(st):
                for t in range(NT):
                    with act.Fori(0, PH) as i:
                        for ab in range(2):
                            n = t * PSLOTS + ab * BATCH
                            act.wait_ge(SEM["dots_ready"], at(st, "dots_ready", n // BATCH + 1) + 2 * i)
                            f(GELU[:, ab, :], DOTS[:, ab, :], ACT.Gelu).then_inc(SEM["gelu_ready"], 1)
                            act.wait_ge(SEM["weights_ready"], at(st, "weights_ready", n // BATCH + 1) + 2 * i)
                            for q in range(BATCH):
                                act.wait_ge(SEM["mix_free"], at(st, "mix_free", n + q + 1) + PTOP * i)
                                f(DIAG[:, q, :], ident[:, :], ACT.Copy, scale=WEIGHTS[:, ab, q:q + 1]
                                  ).then_inc(SEM["diag_ready"], 1)

            def stick(st):
                for g in range(SH // HG):
                    act.wait_ge(SEM["scores_ready"], at(st, "scores_ready", g + 1))
                    z = PS[:, 0:3, :]
                    view = lambda b: b.rearrange("p (a b) -> p a b", b=TW)
                    if g:
                        act.wait_ge(SEM["probs_ready"], at(st, "probs_ready", g))
                    f(view(k_log), z, ACT.Abs)
                    act.drain()
                    f(k_log, k_log, ACT.Exp, scale=-1.0)
                    act.drain()
                    f(k_log, k_log, ACT.Ln, bias=1.0).then_inc(SEM["soft_ready"], 1)
                    act.wait_ge(SEM["exponent_ready"], at(st, "exponent_ready", g + 1))
                    f(k_att, k_exp, ACT.Exp).then_inc(SEM["exp_ready"], 1)

            def softmax(st):
                prob, probT = soft_bufs(st)
                sums, nmax, rsum = soft_small(st)
                for g in range(AH // HG):
                    act.wait_ge(SEM["max_ready"], at(st, "max_ready", g + 1))
                    for t in range(NT):
                        for h in range(HG):
                            a0, n = (h * P, P) if t == 0 else (4 * P + h * S, S)
                            f(prob[:, a0:a0 + n], prob[:, a0:a0 + n], ACT.Exp, bias=nmax[:, t * HG + h:t * HG + h + 1],
                              accum_out=sums[:, t * HG + h:t * HG + h + 1])
                    act.drain().then_inc(SEM["exp_ready"], 1)
                    for n in (0, 2):
                        act.wait_ge(SEM["probsT_ready"], at(st, "probsT_ready", 3 * g + n + 1))
                        f(probT[:, n * TW:(n + 1) * TW], PS[:, 3 + n, :], ACT.Copy).then_inc(SEM["probsT_taken0"], 1)

            def ffn(st):
                def hidden(fb, i):
                    b = fb % 2
                    act.wait_ge(unit_used, used(st["unit0"] + (1 if fb == 0 else 3 * fb), i))
                    f(f_gate[:, b, :], PS[:, b, 0:S], ACT.Silu).then_inc(SEM["hidden_silu"], 1)
                    act.wait_ge(SEM["hidden_raw"], at(st, "hidden_raw", fb + 1) + 2 * i)
                    f(f_hidden[0][:, b, :], f_raw[:, b, :], ACT.Copy).then_inc(SEM["hidden_hi"], 1)

                ffn_schedule(act, lambda q, i: split_hi(act, st, q, i), hidden)

            def rope(st):
                act.wait_ge(SEM["angles_ready"], at(st, "angles_ready", 1))
                f(r_cs, r_ang, ACT.Sin).then_inc(SEM["sines_ready"], 1)

            def ada(st):
                act.dma_start(st["dst"][:, 0:st["tiles"] * TW], d[st["bias"]].partition_broadcast(P)
                              ).then_inc(bias_loaded, 16)
                units = st["units"]
                looped = units // (2 * RING) if units >= 4 * RING else 0
                if looped:
                    with act.Fori(0, looped) as i:
                        for q in range(2 * RING):
                            split_hi(act, st, q, i * 2)
                for q in range(looped * 2 * RING, units):
                    split_hi(act, st, q)

            def fetch(st):
                act.dma_start(st["dst"], d[st["name"]]).then_inc(fetched, 16)
                act.wait_ge(fetched, 16 * (st["fetch0"] + 1))

            parts = dict(ada=ada, norm=norm, linear=linear, linearT=linearT, gates=gates, conv=conv, mlstm=mlstm,
                         headnorm=headnorm, turn=lambda st: taken(st, st["jobs"]), subkeys=subkeys, topk=topk,
                         gather=gather, stick=stick, softmax=softmax, ffn=ffn, rope=rope, fetch=fetch)
            for st in STAGES:
                enter(act, st)
                if st["kind"] in parts:
                    parts[st["kind"]](st)
                leave(act)

        @block.vector
        def _(dve):
            v = nc.vector
            tt, ts, stt, cp = v.tensor_tensor, v.tensor_scalar, v.scalar_tensor_tensor, v.tensor_copy

            dve.drain().then_inc(SEM["expert_free"], BATCH)
            dve.drain().then_inc(SEM["mix_free"], BATCH)
            dve.wait_ge(consts_ready, 1)
            dve.wait_ge(SEM["sines_ready"], 1)
            spread = part(0, KD, P)
            for k in range(KD):
                ts(spread[:, k, :], ones[:, :], ccol[:, k:k + 1], None, ALU.mult)
            dve.drain()
            cp(CB[0][:, :, :], spread)
            dve.drain()
            tt(CB[1][:, :, :], spread, CB[0][:, :, :].bitcast(F32), ALU.subtract)
            dve.drain().then_inc(SEM["angles_ready"], 1)

            def ada(st):
                tiles, dst = st["tiles"], st["dst"]
                dve.wait_ge(bias_loaded, 16 * (st["ada0"] + 2))

                def split(j, turn):
                    for q in range(4):
                        split_lo(dve, st, 4 * j + q, turn)

                def take(j, turn, lap):
                    dve.wait_ge(unit_used, used(st["unit0"] + 4 * j + 3, turn))
                    o = dst[:, j * TW:(j + 1) * TW] if isinstance(lap, int) else \
                        dst[:, bass.ds(lap * (PAIRS * TW) + j * TW, TW)]
                    tt(o, o, PS[:, 2 * (j % PAIRS), :], ALU.add).then_inc(SEM["bank_free0"], 1)

                split(0, 0)
                looped = tiles // PAIRS - 1 if tiles >= 2 * PAIRS else 0
                if looped:
                    with dve.Fori(0, looped) as i:
                        for j in range(PAIRS):
                            split(j + 1, i * 2)
                            take(j, i * 2, i)
                for j in range(looped * PAIRS, tiles):
                    if j + 1 < tiles:
                        split(j + 1, 0)
                    take(j, 0, 0)
                dve.drain()
                for s in st["scales"]:
                    ts(dst[:, s * D:(s + 1) * D], dst[:, s * D:(s + 1) * D], 1.0, None, ALU.add)

            def linear(st):
                per = st["kc"] // 2
                for q in range(per):
                    split_lo(dve, st, q)
                for j in range(st["tiles"]):
                    for q in range((j + 1) * per, min((j + 2) * per, st["units"])):
                        split_lo(dve, st, q)
                    for t in range(NT):
                        what, dst, *gate = st["out"](t, j)
                        if what == "residual" or (what == "copy" and t == 1):
                            if t == 0:
                                dve.wait_ge(SEM["bank_ready"], at(st, "bank_ready", j + 1))
                            else:
                                dve.wait_ge(unit_used, used(st["unit0"] + (j + 1) * per - 1))
                            src = PS[:, 2 * (j % PAIRS) + t, 0:st["width"]]
                            if what == "copy":
                                if len(dst.shape) == 3:
                                    src = src.rearrange("p (a b) -> p a b", b=dst.shape[2])
                                cp(dst, src).then_inc(SEM[f"bank_free{t}"], 1)
                            elif gate[0] is None:
                                tt(dst, dst, src, ALU.add).then_inc(SEM[f"bank_free{t}"], 1)
                            else:
                                tmp = H[:, t, j * TW:(j + 1) * TW]
                                tt(tmp, gate[0], src, ALU.mult).then_inc(SEM[f"bank_free{t}"], 1)
                                dve.drain()
                                tt(dst, dst, tmp, ALU.add)

            def linearT(st):
                parts_ = isinstance(st["dst"], tuple)
                for q in range(4):
                    split_lo(dve, st, q)
                for j in range(st["tiles"]):
                    for q in range(4 * j + 4, min(4 * j + 8, st["units"])):
                        split_lo(dve, st, q)
                    for b in range(4) if parts_ else (1, 3):
                        n = 4 * j + b
                        if parts_:
                            dve.wait_ge(SEM["turned_taken0"], at(st, "turned_taken0", n + 1))
                            tt(st["dst"][1][:, n, :], PS[:, n % 8, 0:S], st["dst"][0][:, n, :].bitcast(F32),
                               ALU.subtract).then_inc(SEM["turned_taken1"], 1)
                            continue
                        if b == 3:
                            dve.wait_ge(unit_used, used(st["unit0"] + 4 * j + 3))
                        else:
                            dve.wait_ge(SEM["bank_ready"], at(st, "bank_ready", 3 * j + b + 1))
                        cp(st["dst"][:, n, :], PS[:, n % 8, 0:S]).then_inc(SEM["turned_taken1"], 1)

            def log_sigmoid_cumsum(st, m, pre, e, t_, out):
                dve.wait_ge(SEM["gates_in"], at(st, "gates_in", 1))
                dve.wait_ge(SEM["log_out"], at(st, "log_out", 1))
                stt(t_[0:m, :], pre[0:m, :], 0.0, e[0:m, :], ALU.min, ALU.subtract)
                dve.drain()
                v.tensor_tensor_scan(out=out[0:m, :], data0=t_[0:m, :], data1=zrow[0:m, 0:S], initial=0.0,
                                     op0=ALU.add, op1=ALU.add)
                dve.drain().then_inc(SEM["log_in"], 1)

            def gates(st):
                for g in range(st["groups"]):
                    split_lo(dve, st, g)
                if st["groups"] == 2:
                    log_sigmoid_cumsum(st, MH, g_f, g_e, g_t, g_b)
                    tt(g_r[0:MH, :], g_i[0:MH, :], g_b[0:MH, :], ALU.subtract)
                    dve.drain()
                    v.tensor_tensor_scan(out=g_m[0:MH, :], data0=g_r[0:MH, :], data1=g_r[0:MH, :], initial=0.0,
                                         op0=ALU.max, op1=ALU.max)
                    dve.drain()
                    stt(g_floor[0:MH, :], g_b[0:MH, :], -1.0, g_m[0:MH, :], ALU.mult, ALU.subtract)
                    dve.drain().then_inc(SEM["scan_ready"], 1)
                    dve.wait_ge(SEM["rowsT_ready"], at(st, "rowsT_ready", 1))
                    cp(m_rT, PS[:, 2, 0:NT * MH].rearrange("p (a b) -> p a b", b=MH)).then_inc(SEM["rows_taken"], 1)
                else:
                    log_sigmoid_cumsum(st, AH, fx, f_e, f_l, f_c)
                    ts(f_c[0:AH, :], f_c[0:AH, :], -1.0, None, ALU.mult)

            def taken(st, jobs):
                n = 0
                for _, chunks, width, dst in jobs:
                    for t in range(NT):
                        for c0 in range(0, chunks, 4):
                            c1 = min(c0 + 4, chunks)
                            if isinstance(dst, tuple):
                                dve.wait_ge(SEM["turned_taken0"], at(st, "turned_taken0", n + 1))
                                hi, lo = (x[0:width, c0:c1, t * P:(t + 1) * P] for x in dst)
                                tt(lo, PS[0:width, n % 8, 0:(c1 - c0) * P].rearrange("p (a b) -> p a b", b=P),
                                   hi.bitcast(F32), ALU.subtract).then_inc(SEM["turned_taken1"], 1)
                            elif n % 2 == 1:
                                dve.wait_ge(SEM["turned"], at(st, "turned", n + 1))
                                cp(dst[0:width, c0:c1, t * P:(t + 1) * P],
                                   PS[0:width, n % 8, 0:(c1 - c0) * P].rearrange("p (a b) -> p a b", b=P)
                                   ).then_inc(SEM["turned_taken1"], 1)
                            n += 1

            def gain_wait(st):
                n = st["gain"]
                dve.wait_ge(gain_loaded[n % 2], 16 * (n // 2 + 1))

            def norm(st):
                w, n = st["width"], st["gain"]
                gain_wait(st)
                g = GAIN[:, n % 2, 0:w]
                if st["scale"] is not None:
                    tt(g, g, st["scale"], ALU.mult)
                dve.wait_ge(SEM["rms_ready"], at(st, "rms_ready", 1))
                v.reciprocal(rs[:, 0:NT], rms[:, 0:NT])
                dve.drain()
                for t in range(NT):
                    ins = stt(st["dst"](t), st["src"](t), rs[:, t:t + 1], g, ALU.mult, ALU.mult)
                    if st["shift"] is not None:
                        dve.drain()
                        ins = tt(st["dst"](t), st["dst"](t), st["shift"], ALU.add)
                    ins.then_inc(SEM["h_ready"], 1)
                taken(st, [(None, w // P, P, XT)])

            def headnorm(st):
                heads, hd, src = st["heads"], st["hd"], st["src"]
                n = heads * hd
                sq = head_square(st)
                gain_wait(st)
                dve.wait_ge(SEM["sq_ready"], at(st, "sq_ready", 1))
                for t in range(NT):
                    v.tensor_reduce(out=ss[:, t * heads:(t + 1) * heads],
                                    in_=sq[:, t, 0:n].rearrange("p (h e) -> p h e", e=hd), axis=AX.X, op=ALU.add)
                dve.drain().then_inc(SEM["sum_ready"], 1)
                dve.wait_ge(SEM["rms_ready"], at(st, "rms_ready", 1))
                m = NT * heads
                v.reciprocal(rs[:, 0:m], rms[:, 0:m])
                dve.drain()
                if st["factor"] != 1.0:
                    ts(rs[:, 0:m], rs[:, 0:m], st["factor"], None, ALU.mult)
                    dve.drain()
                gain = GAIN[:, st["gain"] % 2, :]
                for t in range(NT):
                    x = heads_of(src, t, n).rearrange("p (h e) -> p h e", e=hd)
                    tt(x, x, rs[:, t * heads:(t + 1) * heads].unsqueeze(2).to_broadcast([P, heads, hd]), ALU.mult)
                dve.drain()
                for t in range(NT):
                    x = heads_of(src, t, n).rearrange("p (h e) -> p h e", e=hd)
                    if st["times"] is None:
                        tt(x, x, gain[:, 0:hd].unsqueeze(1).to_broadcast([P, heads, hd]), ALU.mult)
                    else:
                        tt(heads_of(src, t, n), heads_of(src, t, n), gain[:, 0:n], ALU.mult)
                if st["times"] is not None:
                    dve.drain()
                    for t in range(NT):
                        tt(heads_of(src, t, n), heads_of(src, t, n), st["times"][:, t, :], ALU.mult)

            def conv(st):
                dve.wait_ge(inputs_loaded, 16 * 5)
                for b in range(8):
                    ts(m_conv[:, b, :], m_qk[:, b, :], m_cw[:, b, 3:4], None, ALU.mult)
                    for back in (1, 2, 3):
                        dve.drain()
                        ins = stt(m_conv[:, b, back:S], m_qk[:, b, 0:S - back], m_cw[:, b, 3 - back:4 - back],
                                  m_conv[:, b, back:S], ALU.mult, ALU.add)
                    ins.then_inc(SEM["conv_ready"], 1)

            def mlstm(st):
                def exponent(h):
                    b = h % 2
                    dve.wait_ge(SEM["decay_spread"], at(st, "decay_spread", h + 1))
                    for s in range(2):
                        cols = slice(0, S) if s == 0 else slice(S, S + P)
                        src = PS[:, b, 0:S] if s == 0 else PS[:, b, P:S]
                        stt(m_w[:, b, cols], src, -1.0,
                            m_rT[:, s, h:h + 1].to_broadcast([P, S if s == 0 else P]), ALU.mult, ALU.add)
                    dve.drain()
                    ts(m_w[:, b, :], m_w[:, b, :], 0.0, None, ALU.min).then_inc(SEM["exponent_ready"], 1)

                exponent(0)
                for h in range(MH):
                    b = h % 2
                    if h + 1 < MH:
                        exponent(h + 1)
                    dve.wait_ge(SEM["exp_ready"], at(st, "exp_ready", h + 1))
                    diag = m_w[:, b, :].rearrange("p (a b) -> p a b", b=P)[:, 0:3:2, :]
                    tt(diag, diag, upto[:, :].unsqueeze(1).to_broadcast([P, 2, P]), ALU.mult)
                    dve.drain()
                    dve.wait_ge(SEM["scores_ready"], at(st, "scores_ready", h + 1))
                    if h >= 2:
                        dve.wait_ge(SEM["pv_ready"], at(st, "pv_ready", h - 1))
                    stt(m_p[:, b, :], PS[:, 2 + b, 0:3 * P], MQK ** -0.5, m_w[:, b, :], ALU.mult, ALU.mult
                        ).then_inc(SEM["probs_ready"], 1)
                    dve.wait_ge(SEM["pv_ready"], at(st, "pv_ready", h + 1))
                    num = PS[:, 4 + b, :].rearrange("p (t n) -> p t n", t=2)
                    den = m_den.rearrange("p (a b) -> p a b", a=4)
                    cp(den[:, 0, 0:2].unsqueeze(2), num[:, :, MV:MV + 1])
                    dve.drain()
                    stt(den[:, 1, 0:2], den[:, 0, 0:2], -1.0, den[:, 0, 0:2], ALU.mult, ALU.max)
                    dve.drain()
                    tt(den[:, 2, 0:2].unsqueeze(2), den[:, 1, 0:2].unsqueeze(2), m_floor[:, :, h:h + 1], ALU.max)
                    dve.drain()
                    v.reciprocal(den[:, 3, 0:2], den[:, 2, 0:2])
                    dve.drain()
                    for t in range(NT):
                        ts(m_h[:, t, h * MV:(h + 1) * MV], num[:, t, 0:MV], den[:, 3, t:t + 1], None, ALU.mult)
                    dve.drain().then_inc(SEM["pv_taken"], 1)

            def subkeys(st):
                split_lo(dve, st, 0)
                for t in range(NT):
                    for b in range(1, 4, 2):
                        n = t * 4 + b
                        if n == 7:
                            dve.wait_ge(unit_used, used(st["unit0"]))
                        else:
                            dve.wait_ge(SEM["bank_ready"], at(st, "bank_ready", n + 1))
                        cp(SCORE[:, t, 4 * b:4 * b + 4, :], PS[:, n, :].rearrange("p (a b) -> p a b", b=P))

            def best16(rows, vals, idx):
                for r, x, i in zip(rows, vals, idx):
                    v.max(x[:, 0:8], r)
                dve.drain()
                for r, x, i in zip(rows, vals, idx):
                    v.max_index(i[:, 0:8], x[:, 0:8], r)
                dve.drain()
                for r, x, i in zip(rows, vals, idx):
                    v.match_replace(out=r, in_to_replace=x[:, 0:8], in_values=r, imm_value=-HUGE)
                dve.drain()
                for r, x, i in zip(rows, vals, idx):
                    v.max(x[:, 8:16], r)
                dve.drain()
                for r, x, i in zip(rows, vals, idx):
                    v.max_index(i[:, 8:16], x[:, 8:16], r)
                dve.drain()

            def topk(st):
                every = [(t, h, p) for t in range(NT) for h in range(PH) for p in range(2)]
                best16([SCORE[:, t, 2 * h + p, :] for t, h, p in every], [TOPV[:, t, h, p, :] for t, h, p in every],
                       [TOPI[:, t, h, p, :] for t, h, p in every])
                cp(TOPIF[:, :, :, :, :].rearrange("p a b c e -> p (a b c e)"),
                   TOPI[:, :, :, :, :].rearrange("p a b c e -> p (a b c e)"))
                full = [P, PH, PTOP, PTOP]
                for t in range(NT):
                    tt(CAND[:, t, :, :].rearrange("p h (a b) -> p h a b", b=PTOP),
                       TOPV[:, t, :, 0, :].unsqueeze(3).to_broadcast(full),
                       TOPV[:, t, :, 1, :].unsqueeze(2).to_broadcast(full), ALU.add)
                dve.drain()
                both = [(t, h) for t in range(NT) for h in range(PH)]
                best16([CAND[:, t, h, :] for t, h in both], [BESTV[:, t, h, :] for t, h in both],
                       [BESTI[:, t, h * PTOP:(h + 1) * PTOP] for t, h in both])
                shape = [P, NT, PH, PTOP]
                cp(PSUMS.rearrange("p (a b) -> p a b", b=PH), BESTV[:, :, :, 0])
                ts(BROW, BESTI, 4, None, ALU.logical_shift_right)
                ts(BCOL, BESTI, PTOP - 1, None, ALU.bitwise_and)
                dve.drain()
                tt(BESTV, BESTV, PSUMS.rearrange("p (a b) -> p a b", b=PH).unsqueeze(3).to_broadcast(shape),
                   ALU.subtract).then_inc(SEM["top_shifted"], 1)
                cp(BROWF, BROW)
                cp(BCOLF, BCOL)
                dve.drain()
                for t in range(NT):
                    for place, half, out in ((BROWF, 0, EXPROW), (BCOLF, 1, EXPCOL)):
                        tt(HOT, place[:, t, :].rearrange("p (h k) -> p h k", k=PTOP).unsqueeze(3).to_broadcast(full),
                           iota16[:, :].unsqueeze(1).unsqueeze(1).to_broadcast(full), ALU.is_equal)
                        dve.drain()
                        tt(HOT, HOT, TOPIF[:, t, :, half, :].unsqueeze(2).to_broadcast(full), ALU.mult)
                        dve.drain()
                        v.tensor_reduce(out=out[:, t, :].rearrange("p (h k) -> p h k", k=PTOP), in_=HOT,
                                        axis=AX.X, op=ALU.add)
                        dve.drain()
                stt(EXPERT, EXPROW, float(PK), EXPCOL, ALU.mult, ALU.add)
                dve.wait_ge(SEM["top_exp"], at(st, "top_exp", 1))
                v.tensor_reduce(out=PSUMS.rearrange("p (a b) -> p a b", b=PH), in_=BESTV, axis=AX.X, op=ALU.add)
                dve.drain()
                v.reciprocal(PSUMS, PSUMS)
                dve.drain()
                tt(GATE.rearrange("p t (h k) -> p t h k", k=PTOP), BESTV,
                   PSUMS.rearrange("p (a b) -> p a b", b=PH).unsqueeze(3).to_broadcast(shape), ALU.mult)

            def gather(st):
                m0 = st["gather0"] * NT * PSLOTS
                for t in range(NT):
                    with dve.Fori(0, PH) as i:
                        for ab in range(2):
                            n = t * PSLOTS + ab * BATCH
                            for q in range(BATCH):
                                dve.wait_ge(u_loaded[q], 16 * ((m0 + n) // BATCH + 1) + 32 * i)
                                v.tensor_tensor_reduce(out=UROWS[:, q, :], in0=UROWS[:, q, :], in1=H[:, t, :], scale=1.0,
                                                       scalar=0.0, op0=ALU.mult, op1=ALU.add,
                                                       accum_out=DOTS[:, ab, q:q + 1]
                                                       ).then_inc(SEM["expert_free"], 1)
                            dve.drain().then_inc(SEM["dots_ready"], 1)
                            dve.wait_ge(SEM["gelu_ready"], at(st, "gelu_ready", n // BATCH + 1) + 2 * i)
                            dve.wait_ge(SEM["diag_ready"], at(st, "diag_ready", t * PSLOTS) + PTOP * i)
                            tt(WEIGHTS[:, ab, :], GELU[:, ab, :], GATE[:, t, bass.ds(i * PTOP + ab * BATCH, BATCH)],
                               ALU.mult).then_inc(SEM["weights_ready"], 1)
                dve.wait_ge(SEM["mixed"], at(st, "mixed", 1))

            def mix_in(st):
                for t in range(NT):
                    tt(H[:, t, :], PS[:, 2 * t:2 * t + 2, :].rearrange("p a b -> p (a b)"), mod(5), ALU.mult)
                dve.drain()
                for t in range(NT):
                    tt(X[:, t, :], X[:, t, :], H[:, t, :], ALU.add)

            def stick(st):
                view = lambda b: b.rearrange("p (a b) -> p a b", b=TW)

                def masked(b):
                    for x in (b[:, 0:2 * TW].rearrange("p (h t) -> p h t", t=S)[:, :, 0:P],
                              b[:, 2 * TW:3 * TW].rearrange("p (h t) -> p h t", t=P)):
                        ins = tt(x, x, before[:, :].unsqueeze(1).to_broadcast([P, HG, P]), ALU.mult)
                    return ins

                for g in range(SH // HG):
                    dve.wait_ge(SEM["soft_ready"], at(st, "soft_ready", g + 1))
                    z = PS[:, 0:3, :]
                    stt(view(k_lost), z, 0.0, view(k_log), ALU.max, ALU.add)
                    stt(view(k_exp), z, 0.0, view(k_log), ALU.min, ALU.subtract)
                    dve.drain()
                    masked(k_lost)
                    dve.drain().then_inc(SEM["log_in"], 1)
                    dve.wait_ge(SEM["between_ready"], at(st, "between_ready", g + 1))
                    tt(view(k_exp), view(k_exp), PS[:, 3:6, :], ALU.subtract)
                    dve.drain()
                    ts(k_exp, k_exp, 0.0, None, ALU.min).then_inc(SEM["exponent_ready"], 1)
                    dve.wait_ge(SEM["exp_ready"], at(st, "exp_ready", g + 1))
                    masked(k_att)
                    dve.drain().then_inc(SEM["probs_ready"], 1)
                    dve.wait_ge(SEM["pv_ready"], at(st, "pv_ready", g + 1))
                    cp(H[:, :, g * 256:(g + 1) * 256], PS[:, 6, :].rearrange("p (t n) -> p t n", t=2)
                       ).then_inc(SEM["pv_taken"], 1)

            def softmax(st):
                prob, probT = soft_bufs(st)
                sums, nmax, rsum = soft_small(st)
                for g in range(AH // HG):
                    dve.wait_ge(SEM["scores_ready"], at(st, "scores_ready", g + 1))
                    early = prob[:, 0:TW].rearrange("p (h n) -> p h n", n=P)
                    late = prob[:, TW:3 * TW].rearrange("p (h n) -> p h n", n=S)
                    tt(early, PS[:, 0, :].rearrange("p (h n) -> p h n", n=P),
                       causal[:, P:S].unsqueeze(1).to_broadcast([P, HG, P]), ALU.add)
                    tt(late, PS[:, 1:3, :].rearrange("p a (h n) -> p (a h) n", n=S),
                       causal[:, :].unsqueeze(1).to_broadcast([P, HG, S]), ALU.add)
                    dve.drain()
                    v.tensor_reduce(out=nmax[:, 0:HG], in_=early, axis=AX.X, op=ALU.max, negate=True)
                    v.tensor_reduce(out=nmax[:, HG:2 * HG], in_=late, axis=AX.X, op=ALU.max, negate=True)
                    dve.drain().then_inc(SEM["max_ready"], 1)
                    dve.wait_ge(SEM["probsT_ready"], at(st, "probsT_ready", 3 * g + 2))
                    cp(probT[:, TW:2 * TW], PS[:, 4, :]).then_inc(SEM["probsT_taken1"], 1)
                    dve.wait_ge(SEM["exp_ready"], at(st, "exp_ready", g + 1))
                    v.reciprocal(rsum, sums)
                    dve.drain()
                    dve.wait_ge(SEM["pv_ready"], at(st, "pv_ready", g + 1))
                    for t in range(NT):
                        ins = tt(H[:, t, g * 256:(g + 1) * 256].rearrange("p (h n) -> p h n", n=AV),
                                 PS[:, 6, t * 256:(t + 1) * 256].rearrange("p (h n) -> p h n", n=AV),
                                 rsum[:, t * HG:(t + 1) * HG].unsqueeze(2).to_broadcast([P, HG, AV]), ALU.mult)
                    dve.drain().then_inc(SEM["pv_taken"], 1)

            def mla_keys(st):
                for t in range(NT):
                    k = st["k"][:, t, :].rearrange("p (h e) -> p h e", e=MLA_D)
                    cp(k[:, :, 0:NOPE], st["kv"][:, t, :].rearrange("p (h e) -> p h e", e=2 * AV)[:, :, 0:NOPE])
                    cp(k[:, :, NOPE:MLA_D],
                       st["z"][:, t, MLA_Q + MLA_KV:800].unsqueeze(1).to_broadcast([P, AH, ROPE]))

            def rope(st):
                half = ROPE // 2
                dve.wait_ge(inputs_loaded, 16 * 5)
                dve.wait_ge(rope_loaded, 16)
                cp(r_pos, posi[:, :])
                dve.drain()
                ang = r_ang.rearrange("p (c t n) -> p c t n", c=2, n=half)
                turns = r_turn.rearrange("p (c t n) -> p c t n", c=2, n=half)
                for t in range(NT):
                    ts(ang[:, 1, t, :], r_freq, r_pos[:, t:t + 1], None, ALU.mult)
                dve.drain()
                ts(turns[:, 1, :, :], ang[:, 1, :, :], 1.0 / (2 * math.pi), None, ALU.mult)
                dve.drain()
                cp(r_int, r_turn[:, 32:64])
                dve.drain()
                cp(r_turn[:, 32:64], r_int)
                dve.drain()
                big = 6.28125
                stt(ang[:, 1], turns[:, 1], -big, ang[:, 1], ALU.mult, ALU.add)
                dve.drain()
                stt(ang[:, 1], turns[:, 1], -(2 * math.pi - big), ang[:, 1], ALU.mult, ALU.add)
                dve.drain()
                ts(ang[:, 0], ang[:, 1], math.pi / 2, None, ALU.add)
                dve.drain()
                for above, sign in ((ALU.is_gt, -1.0), (ALU.is_lt, 1.0)):
                    ts(r_turn, r_ang, -sign * math.pi, sign * 2 * math.pi, above, ALU.mult)
                    dve.drain()
                    tt(r_ang, r_ang, r_turn, ALU.add)
                    dve.drain()
                ts(r_ang, r_ang, 3.1415925, -3.1415925, ALU.min, ALU.max).then_inc(SEM["angles_ready"], 1)
                dve.wait_ge(SEM["sines_ready"], at(st, "sines_ready", 1))
                cs = r_cs.rearrange("p (c t n) -> p c t n", c=2, n=half)
                tmp = r_tmp.rearrange("p (c h n) -> p c h n", c=4, n=half)
                for x in st["parts"]:
                    for t in range(NT):
                        y = x[:, t, :].rearrange("p (h e) -> p h e", e=MLA_D)
                        x1, x2 = y[:, :, NOPE:NOPE + half], y[:, :, NOPE + half:MLA_D]
                        cos, sin = (cs[:, c, t, :].unsqueeze(1).to_broadcast([P, AH, half]) for c in range(2))
                        for n, (a, b) in enumerate(((x1, cos), (x2, sin), (x1, sin), (x2, cos))):
                            tt(tmp[:, n], a, b, ALU.mult)
                        dve.drain()
                        tt(x1, tmp[:, 0], tmp[:, 1], ALU.subtract)
                        tt(x2, tmp[:, 2], tmp[:, 3], ALU.add)
                        dve.drain()

            def ffn(st):
                def hidden(fb, i):
                    b = fb % 2
                    dve.wait_ge(SEM["hidden_silu"], at(st, "hidden_silu", fb + 1) + 2 * i)
                    tt(f_raw[:, b, :], f_gate[:, b, :], PS[:, b, S:2 * S], ALU.mult
                       ).then_inc(SEM["hidden_raw"], 1)
                    dve.wait_ge(SEM["hidden_hi"], at(st, "hidden_hi", fb + 1) + 2 * i)
                    tt(f_hidden[1][:, b, :], f_raw[:, b, :], f_hidden[0][:, b, :].bitcast(F32), ALU.subtract
                       ).then_inc(SEM["hidden_ready"], 1)

                ffn_schedule(dve, lambda q, i: split_lo(dve, st, q, i), hidden)
                dve.wait_ge(SEM["mixed"], at(st, "mixed", 1))
                for t in range(NT):
                    stt(X[:, t, :], PS[:, 4 + 2 * t:6 + 2 * t, :].rearrange("p a b -> p (a b)"), 0.5, X[:, t, :],
                        ALU.mult, ALU.add)

            parts = dict(ada=ada, norm=norm, linear=linear, linearT=linearT, gates=gates, conv=conv, mlstm=mlstm,
                         headnorm=headnorm, turn=lambda st: taken(st, st["jobs"]), subkeys=subkeys, topk=topk,
                         gather=gather, mix_in=mix_in, stick=stick, softmax=softmax, mla_keys=mla_keys, rope=rope,
                         ffn=ffn)
            for st in STAGES:
                enter(dve, st)
                if st["kind"] in parts:
                    parts[st["kind"]](st)
                leave(dve)


def kernel(**inputs):
    from concourse import bacc
    from concourse.bass_utils import run_bass_kernel_spmd

    a = {k: np.asarray(v) for k, v in inputs.items()}

    def tiles(w, width):
        k, n = w.shape
        w = w.reshape(k // (2 * P), 2, P, n // width, width).transpose(3, 0, 2, 1, 4)
        return np.ascontiguousarray(w.reshape(-1, P, 2 * width))

    def blocks(w):
        return w.reshape(KD, P, -1, P).transpose(2, 1, 0, 3).reshape(-1, P, UNIT)

    def padded(w):
        return blocks(np.pad(w, ((0, 0), (0, P - w.shape[1]))))

    def swiglu(w_in, w_out):
        g, u, down = blocks(w_in[:, :FF]), blocks(w_in[:, FF:]), w_out.reshape(FB, P, D)
        order = [g[0], u[0]]
        for f in range(1, FB):
            order += [g[f], u[f], down[f - 1]]
        return np.stack(order + [down[FB - 1]])

    def tokens(x):
        return np.ascontiguousarray(x.reshape(NT, P, -1).transpose(1, 0, 2))

    def columns(x):
        return np.ascontiguousarray(x.reshape(-1, P).T)

    t = {"x": tokens(a["x"][0]), "c": columns(a["c"][0])}
    for i in range(2):
        t[f"ada_w{i}"] = tiles(a["ada_w"][i], TW)
        t[f"ada_b{i}"] = a["ada_b"][i]
        t[f"norm_mix_g{i}"] = a["norm_mix_g"][i]
        t[f"norm_ffn_g{i}"] = a["norm_ffn_g"][i]
        t[f"peer_w_q{i}"] = tiles(a["peer_w_q"][i], TW)
        t[f"sub_keys{i}"] = a["peer_sub_keys"][i].transpose(2, 0, 1).reshape(1, P, 2 * PK)
        t[f"peer_u{i}"] = a["peer_u"][i]
        t[f"peer_v{i}"] = a["peer_v"][i]
        t[f"ffn1_{i}"] = swiglu(a["ffn1_w_in_2"][i], a["ffn1_w_out_2"][i])
        t[f"ffn2_{i}"] = swiglu(a["ffn2_w_in_2"][i], a["ffn2_w_out_2"][i])
        t[f"ple_gate{i}"] = tiles(a["ple_w_gate_2"][i], TW)
        t[f"ple_proj{i}"] = tiles(a["ple_w_proj_2"][i], TW)
        t[f"p{i}"] = tokens(a["p_2"][i, 0])
        t[f"g_ffn1_{i}"] = a["g_ffn1_2"][i]
        t[f"g_mix_{i}"] = a["g_mix_2"][i]
        t[f"g_ffn2_{i}"] = a["g_ffn2_2"][i]
        t[f"g_ple{i}"] = a["g_ple_2"][i]
    w = a["ma_w_in"][0]
    t["ma_w_qk"] = tiles(w[:, :D], TW)
    t["ma_w_vo"] = tiles(w[:, D:3 * D], TW)
    t["ma_w_g"] = np.concatenate([padded(w[:, 3 * D:3 * D + MH]), padded(w[:, 3 * D + MH:])])
    t["ma_b_if"] = a["ma_b_if"][0].reshape(2, MH).T
    t["conv_w"] = a["ma_conv_w"][0].reshape(4, 8, P).transpose(2, 1, 0)
    t["ma_hnorm_g"] = a["ma_hnorm_g"][0].reshape(-1)
    t["ma_w_out"] = tiles(a["ma_w_out"][0], TW)
    t["kv_ada_w"] = tiles(a["kv_ada_w"], TW)
    t["kv_ada_b"] = a["kv_ada_b"]
    t["kv_norm_g"] = a["kv_norm_g"]
    t["kv_w"] = tiles(a["kv_w"], TW)
    t["k_norm_g"] = a["k_norm_g"]
    t["sb_w_q"] = tiles(a["sb_w_q"][0], TW)
    t["sb_q_norm_g"] = a["sb_q_norm_g"][0]
    t["sb_w_out"] = tiles(a["sb_w_out"][0], TW)
    t["mla_w_in"] = tiles(a["mla_w_in_2"][0], 400)
    t["mla_g_q_lat"] = a["mla_g_q_lat_2"][0]
    t["mla_w_uq"] = tiles(a["mla_w_uq_2"][0], TW)
    t["mla_g_kv_lat"] = a["mla_g_kv_lat_2"][0]
    t["mla_w_ukv"] = tiles(a["mla_w_ukv_2"][0], TW)
    t["mla_g_qn"] = a["mla_g_qn_2"][0]
    t["mla_g_kn"] = a["mla_g_kn_2"][0]
    t["mla_w_o"] = tiles(a["mla_w_o_2"][0], TW)
    w = a["fox_w_in_2"][0]
    t["fox_w_in"] = tiles(w[:, :3 * D], TW)
    t["fox_w_g"] = padded(w[:, 3 * D:])
    t["fox_b_f"] = a["fox_b_f_2"][0].reshape(AH, 1)
    t["fox_g_qn"] = a["fox_g_qn_2"][0]
    t["fox_g_kn"] = a["fox_g_kn_2"][0]
    t["fox_w_o"] = tiles(a["fox_w_o_2"][0], TW)
    t["positions"] = a["positions_2"][0].reshape(NT, P).T
    t["rope_freq"] = (10000.0 ** (-np.arange(0, ROPE, 2, dtype=np.float32) / ROPE)).astype(np.float32)

    nc = bacc.Bacc("TRN2", target_bir_lowering=False, num_devices=1)
    arrays, d = {}, {}
    for name, x in t.items():
        x = np.ascontiguousarray(x)
        arrays["in_" + name] = x
        d[name] = nc.dram_tensor("in_" + name, x.shape, mybir.dt.from_np(x.dtype), kind="ExternalInput").ap()
    d["out"] = nc.dram_tensor("out_0", (P, NT, D), F32, kind="ExternalOutput").ap()
    build(nc, d)
    r = run_bass_kernel_spmd(nc, [arrays], core_ids=[0])
    out = np.asarray(r.results[0]["out_0"])
    return np.ascontiguousarray(out.transpose(1, 0, 2)).reshape(1, S, D)
```

```python
import math
from contextlib import ExitStack

import numpy as np

import concourse.bass as bass
from concourse import mybir

F32 = mybir.dt.float32
F32R = mybir.dt.float32r
I32 = mybir.dt.int32
U32 = mybir.dt.uint32
ALU = mybir.AluOpType
ACT = mybir.ActivationFunctionType
AX = mybir.AxisListType

P = 128
S = 256
NT = S // P
D = 1024
KD = D // P
TW = 512
EPS = 1e-6
HUGE = 3.0e38

MH, MQK, MV = 8, 64, 128
SH, SD = 16, 64
PH, PK, PTOP = 8, 128, 16
PSLOTS = PH * PTOP
FF = 2816
FB = FF // P
AH = 16
MLA_Q, MLA_KV, NOPE, ROPE, AV = 512, 256, 64, 32, 64
MLA_D = NOPE + ROPE
FOX_D = 64
HG = 4
RING = 6
UNIT = 2 * TW
PAIRS = 3
LATE = (2, 4, 6)
AHEAD = 1
BATCH = 8


def build(nc, d):
    ctx = ExitStack()
    with ctx:
        def sb(name, shape, dt=F32):
            return ctx.enter_context(nc.sbuf_tensor("sb_" + name, shape, dt))

        def sem(name):
            return ctx.enter_context(nc.semaphore(name))

        X = sb("x", [P, NT, D])
        H = sb("h", [P, NT, D])
        xt_at = nc.sbuf_base
        XT = (sb("xT_hi", [P, KD, S], F32R), sb("xT_lo", [P, KD, S], F32R))
        XTF = nc.alloc_sbuf_tensor_at("sb_xT_whole", [P, 2 * KD * S], F32, offset=xt_at)
        MOD = sb("mod", [P, 6 * D])
        GAIN = sb("gain", [P, 2, D])
        w_at = nc.sbuf_base
        W = sb("w", [P, RING, UNIT])
        WL = nc.alloc_sbuf_tensor_at("sb_w_lo", [P, RING, UNIT], F32R, offset=w_at)
        wh_at = nc.sbuf_base
        WH = sb("w_hi", [P, RING, UNIT], F32R)
        WHF = nc.alloc_sbuf_tensor_at("sb_w_hi_whole", [P, RING * UNIT], F32, offset=wh_at)
        OUTGOING = WHF[:, 0:PAIRS * TW].rearrange("p (a b) -> p a b", b=TW)
        CB = (sb("cb_hi", [P, KD, P], F32R), sb("cb_lo", [P, KD, P], F32R))
        ident = sb("ident", [P, P])
        ones = sb("ones", [P, P])
        after = sb("after", [P, P])
        before = sb("before", [P, P])
        upto = sb("upto", [P, P])
        causal = sb("causal", [P, S])
        zrow = sb("zrow", [P, TW])
        iota16 = sb("iota16", [P, 16])
        eps = sb("eps", [P, 1])
        ccol = sb("ccol", [P, KD])
        ss = sb("ss", [P, 64])
        rms = sb("rms", [P, 64])
        rs = sb("rs", [P, 64])
        unread = sb("unread", [P, 1])
        small = sb("small", [P, 256])
        bias8 = sb("bias8", [16, 2])
        bias16 = sb("bias16", [16, 1])
        posi = sb("posi", [P, NT], I32)
        rope_int = sb("rope_int", [P, NT * ROPE // 2], I32)
        r_freq_own = sb("rope_freq", [P, ROPE // 2])
        ARENA = 18432
        arena_at = nc.sbuf_base
        A = sb("arena", [P, ARENA])
        AR = nc.alloc_sbuf_tensor_at("sb_arena_r", [P, ARENA], F32R, offset=arena_at)
        PS = ctx.enter_context(nc.psum_tensor("ps", [P, 8, TW], F32))

        def part(start, *shape, of=None):
            n = int(np.prod(shape))
            assert start + n <= ARENA, (start, shape)
            v = (A if of is None else of)[:, start:start + n]
            if len(shape) == 2:
                v = v.rearrange("p (a b) -> p a b", b=shape[1])
            elif len(shape) == 3:
                v = v.rearrange("p (a b c) -> p a b c", b=shape[1], c=shape[2])
            elif len(shape) == 4:
                v = v.rearrange("p (a b c e) -> p a b c e", b=shape[1], c=shape[2], e=shape[3])
            return v

        GATE0 = XTF[:, 0:D]
        KVMOD = XTF[:, KD * S:KD * S + 2 * D]

        STAGES = []

        def stage(kind, **kw):
            kw["kind"] = kind
            kw["n"] = len(STAGES)
            STAGES.append(kw)

        gains = []

        def norm(src, width, gain, shift=None, scale=None, dst=None):
            gains.append((gain, width))
            stage("norm", src=src, width=width, gain=len(gains) - 1, shift=shift, scale=scale,
                  dst=dst or (lambda t: H[:, t, 0:width]))

        def turn(jobs, decay=False, fetched=0):
            stage("turn", jobs=jobs, decay=decay, fetched=fetched)

        def linear(name, kc, tiles, width, out, fetch=None):
            stage("linear", weights=name, kc=kc, tiles=tiles, width=width, out=out, fetch=fetch)

        def headnorm(heads, hd, *sides, times=None):
            stage("headnorm", heads=heads, hd=hd, sides=sides, gain=len(gains), times=times)
            gains.extend((gain, heads * hd if times is not None else hd) for _, gain, _ in sides)

        def model_norm(gain, shift=None, scale=None):
            norm(lambda t: X[:, t, :], D, gain, shift, scale)

        def mod(i):
            return MOD[:, i * D:(i + 1) * D]

        def copy_to(dst, width=TW):
            return lambda t, j: ("copy", dst[:, t, j * width:(j + 1) * width])

        def residual(gate):
            return lambda t, j: ("residual", X[:, t, j * TW:(j + 1) * TW],
                                 None if gate is None else gate[:, j * TW:(j + 1) * TW])

        def peer(layer):
            model_norm(f"norm_ffn_g{layer}", mod(3), mod(4))
            stage("linearT", weights=f"peer_w_q{layer}", tiles=4,
                  dst=(part(0, 16, S, of=AR), part(4096, 16, S, of=AR)))
            stage("subkeys", layer=layer, weights=f"sub_keys{layer}")
            if layer == 0:
                stage("topk", layer=0, weights="ada_w1", bias="ada_b1", tiles=16)
            else:
                stage("topk", layer=1)
            stage("gather", layer=layer)
            stage("mix_in", gate=GATE0 if layer == 0 else mod(5))

        def ffn(name, gain):
            model_norm(gain)
            stage("ffn", weights=name)

        stage("ada", weights="ada_w0", bias="ada_b0", tiles=12, dst=MOD, scales=(1, 4))
        model_norm("norm_mix_g0", mod(0), mod(1))
        m_qk, m_conv = part(0, 8, S), part(2048, 8, S)
        m_v = part(4096, NT, MH, MV + 1)
        m_o = part(6160, NT, D)
        m_h = part(8208, NT, D)
        stage("linearT", weights="ma_w_qk", tiles=2, dst=m_qk)
        stage("linear", weights="ma_w_vo", kc=KD, tiles=4, width=TW,
              out=lambda t, j: ("copy by ACT", m_v[:, t, 4 * j:4 * j + 4, 0:MV]) if j < 2
              else ("sigmoid", m_o[:, t, (j - 2) * TW:(j - 1) * TW]))
        stage("gates", weights="ma_w_g", groups=2, m=MH)
        stage("conv")
        stage("mlstm")
        headnorm(MH, MV, (m_h, "ma_hnorm_g", 1.0), times=m_o)
        turn([(lambda t, k: m_h[:, t, k * P:(k + 1) * P], KD, P, XT)])
        linear("ma_w_out", KD, 2, TW, residual(mod(2)))
        peer(0)

        s_kv = part(0, NT, 2 * D)
        s_q = part(4096, NT, D)
        s_qT, s_kT = part(6144, SH, S), part(10240, SH, S)
        model_norm("kv_norm_g", KVMOD[:, 0:D], KVMOD[:, D:2 * D])
        linear("kv_w", KD, 4, TW, copy_to(s_kv))
        model_norm("norm_mix_g1", mod(0), mod(1))
        linear("sb_w_q", KD, 2, TW, copy_to(s_q))
        headnorm(SH, SD, (s_kv[:, :, 0:D], "k_norm_g", 1.0), (s_q, "sb_q_norm_g", SD ** -0.5))
        turn([(lambda t, h: s_q[:, t, h * SD:(h + 1) * SD], SH, SD, s_qT),
              (lambda t, h: s_kv[:, t, h * SD:(h + 1) * SD], SH, SD, s_kT)])
        stage("stick", qT=s_qT, kT=s_kT, v=lambda s, h: s_kv[:, s, D + h * SD:D + (h + 1) * SD])
        turn([(lambda t, k: H[:, t, k * P:(k + 1) * P], KD, P, XT)])
        linear("sb_w_out", KD, 2, TW, residual(mod(2)))
        peer(1)

        def embed(i):
            model_norm(f"g_ple{i}")
            e_g, e_p = part(0, NT, D), part(2048, NT, 256)
            linear(f"ple_gate{i}", KD, 2, TW, lambda t, j: ("sigmoid", e_g[:, t, j * TW:(j + 1) * TW]),
                   fetch=(f"p{i}", e_p))
            turn([(lambda t, k: e_p[:, t, k * P:(k + 1) * P], 2, P, XT)], fetched=i + 1)
            linear(f"ple_proj{i}", 2, 2, TW,
                   lambda t, j: ("residual", X[:, t, j * TW:(j + 1) * TW], e_g[:, t, j * TW:(j + 1) * TW]))

        ffn("ffn1_0", "g_ffn1_0")
        model_norm("g_mix_0")
        a_z = part(0, NT, 800)
        a_kv = MOD[:, 0:NT * 2 * D].rearrange("p (t n) -> p t n", t=NT)
        a_q = part(1600, NT, AH * MLA_D)
        a_k = part(4672, NT, AH * MLA_D)
        a_qT, a_kT = part(7744, AH, S), part(11840, AH, S)
        linear("mla_w_in", KD, 2, 400, copy_to(a_z, 400))
        norm(lambda t: a_z[:, t, 0:MLA_Q], MLA_Q, "mla_g_q_lat")
        linear("mla_w_uq", MLA_Q // P, 3, TW, copy_to(a_q))
        norm(lambda t: a_z[:, t, MLA_Q:MLA_Q + MLA_KV], MLA_KV, "mla_g_kv_lat")
        linear("mla_w_ukv", MLA_KV // P, 4, TW, copy_to(a_kv))
        stage("mla_keys", z=a_z, kv=a_kv, k=a_k)
        headnorm(AH, MLA_D, (a_q, "mla_g_qn", MLA_D ** -0.5), (a_k, "mla_g_kn", 1.0))
        stage("rope", parts=(a_q, a_k))
        turn([(lambda t, h: a_q[:, t, h * MLA_D:(h + 1) * MLA_D], AH, MLA_D, a_qT),
              (lambda t, h: a_k[:, t, h * MLA_D:(h + 1) * MLA_D], AH, MLA_D, a_kT)])
        stage("softmax", qT=a_qT, kT=a_kT, dk=MLA_D, decay=False, work=1600, work2=4672,
              v=lambda s, h: a_kv[:, s, h * 2 * AV + AV:(h + 1) * 2 * AV])
        turn([(lambda t, k: H[:, t, k * P:(k + 1) * P], KD, P, XT)])
        linear("mla_w_o", KD, 2, TW, residual(None))
        ffn("ffn2_0", "g_ffn2_0")
        embed(0)

        ffn("ffn1_1", "g_ffn1_1")
        model_norm("g_mix_1")
        f_z = part(0, NT, 3 * D)
        f_qT, f_kT = part(6144, AH, S), part(10240, AH, S)
        linear("fox_w_in", KD, 6, TW, copy_to(f_z))
        stage("gates", weights="fox_w_g", groups=1, m=AH)
        headnorm(AH, FOX_D, (f_z[:, :, 0:D], "fox_g_qn", FOX_D ** -0.5), (f_z[:, :, D:2 * D], "fox_g_kn", 1.0))
        turn([(lambda t, h: f_z[:, t, h * FOX_D:(h + 1) * FOX_D], AH, FOX_D, f_qT),
              (lambda t, h: f_z[:, t, D + h * FOX_D:D + (h + 1) * FOX_D], AH, FOX_D, f_kT)], decay=True)
        stage("softmax", qT=f_qT, kT=f_kT, dk=FOX_D, decay=True, work=14336, work2=0,
              v=lambda s, h: f_z[:, s, 2 * D + h * FOX_D:2 * D + (h + 1) * FOX_D])
        turn([(lambda t, k: H[:, t, k * P:(k + 1) * P], KD, P, XT)])
        linear("fox_w_o", KD, 2, TW, residual(None))
        ffn("ffn2_1", "g_ffn2_1")
        embed(1)

        stage_done = sem("stage_done")
        consts_ready = sem("consts_ready")
        inputs_loaded = sem("inputs_loaded")
        gain_loaded = [sem("gain_loaded0"), sem("gain_loaded1")]
        bias_loaded = sem("bias_loaded")
        fetched = sem("fetched")
        decay_moved = sem("decay_moved")
        stored = sem("stored")
        w_loaded = [sem(f"w_loaded{q}") for q in range(RING)]
        unit_used = sem("unit_used")
        hi_ready = sem("hi_ready")
        lo_ready = sem("lo_ready")
        names = ["bank_ready", "bank_free0", "bank_free1", "rms_ready", "h_ready", "sq_ready", "sum_ready", "scaled_ready",
                 "turned", "turned_taken0", "turned_taken1",
                 "gates_in", "log_in", "log_out", "scan_ready", "rowsT_ready", "rows_taken", "floor_ready",
                 "decay_spread", "exponent_ready", "exp_ready", "scores_ready", "scores_taken", "probs_ready", "pv_ready",
                 "pv_taken", "soft_ready", "between_ready", "max_ready", "probsT_ready",
                 "probsT_taken0", "probsT_taken1", "conv_ready",
                 "hidden_silu", "hidden_raw", "hidden_hi", "hidden_ready", 
                 "angles_ready", "sines_ready", "top_shifted", "top_exp", "picked",
                 "expert_free", "mix_free", "dots_ready", "gelu_ready", "weights_ready", "diag_ready",
                 "claimed", "outgoing_free", "indices_staged", "mixed"]
        SEM = {n: sem(n) for n in names}
        u_loaded = [sem(f"u_loaded{q}") for q in range(BATCH)]
        v_loaded = [sem(f"v_loaded{q}") for q in range(BATCH)]

        def counts(st):
            k = st["kind"]
            c = {}
            if k == "ada":
                c = dict(bank_free0=st["tiles"])
            elif k == "linear":
                c = dict(bank_ready=st["tiles"], bank_free0=st["tiles"], bank_free1=st["tiles"])
            elif k == "linearT":
                n = (4 if isinstance(st["dst"], tuple) else 2) * st["tiles"]
                c = dict(bank_ready=3 * st["tiles"], turned_taken0=n, turned_taken1=n)
            elif k == "gates":
                c = dict(gates_in=1, log_in=1, log_out=1)
                if st["groups"] == 2:
                    c.update(scan_ready=1, rowsT_ready=1, rows_taken=1, floor_ready=1)
            elif k == "norm":
                g = NT * -(-st["width"] // (4 * P))
                c = dict(rms_ready=NT, h_ready=NT, turned=g, turned_taken0=g, turned_taken1=g)
            elif k == "turn":
                g = sum(NT * -(-j[1] // 4) for j in st["jobs"])
                n = g if isinstance(st["jobs"][0][3], tuple) else g // 2
                c = dict(turned=g, turned_taken0=n, turned_taken1=n)
            elif k == "headnorm":
                n = len(st["sides"])
                c = dict(sq_ready=NT * n, sum_ready=NT * n, rms_ready=n, scaled_ready=n - 1)
            elif k == "conv":
                c = dict(conv_ready=8)
            elif k == "mlstm":
                c = dict(decay_spread=MH, exponent_ready=MH, exp_ready=MH, scores_ready=MH, probs_ready=MH,
                         pv_ready=MH, pv_taken=MH)
            elif k == "subkeys":
                c = dict(bank_ready=7)
            elif k == "topk":
                c = dict(top_shifted=1, top_exp=1, bank_free0=st.get("tiles", 0),
                         outgoing_free=st.get("tiles", 0))
            elif k == "gather":
                n = NT * PSLOTS
                c = dict(expert_free=n, mix_free=n, dots_ready=n // BATCH, gelu_ready=n // BATCH,
                         weights_ready=n // BATCH, diag_ready=n, indices_staged=NT * PH, mixed=1)
                if st["layer"] == 1:
                    c.update(top_shifted=1, top_exp=1, picked=1)
            elif k == "stick":
                n = SH // HG
                c = dict(scores_ready=n, scores_taken=n, soft_ready=n, log_in=n, between_ready=n, exponent_ready=n, exp_ready=n,
                         probs_ready=n, pv_ready=n, pv_taken=n)
            elif k == "softmax":
                n = AH // HG
                c = dict(scores_ready=n, scores_taken=n, max_ready=n, exp_ready=n, probsT_ready=3 * n, probsT_taken0=2 * n,
                         probsT_taken1=n, pv_ready=n, pv_taken=n)
            elif k == "ffn":
                c = dict(hidden_silu=FB, hidden_raw=FB, hidden_hi=FB, hidden_ready=FB, mixed=1)
            elif k == "rope":
                c = dict(angles_ready=1, sines_ready=1)
            return c

        base = []
        running = {n: 0 for n in names}
        running.update(sines_ready=1, angles_ready=1, diag_ready=1, outgoing_free=PAIRS)
        units_before = 0
        gathers_before = 0
        norms_before = 0
        split_before = 0
        for st in STAGES:
            base.append(dict(running))
            for n_, v_ in counts(st).items():
                running[n_] += v_
            st["unit0"] = units_before
            st["units"] = {"ada": st.get("tiles", 0) * KD // 2, "topk": st.get("tiles", 0) * KD // 2, "linear": st.get("tiles", 0) * st.get("kc", 0) // 2,
                           "linearT": st.get("tiles", 0) * KD // 2, "gates": st.get("groups", 0), "subkeys": 1,
                           "ffn": 3 * FB}.get(st["kind"], 0)
            st["floats"] = {"linear": 2 * st.get("width", 0), "subkeys": 2 * PK}.get(st["kind"], UNIT)
            units_before += st["units"]
            st["gather0"] = gathers_before
            gathers_before += st["kind"] == "gather"
            st["split0"] = split_before
            split_before += 0 if st["kind"] == "topk" else st["units"]

        for st, after_ in zip(STAGES, STAGES[1:] + [{}]):
            st["next"] = after_ if st["kind"] in ("norm", "turn") and after_.get("units") else None
            if st["next"]:
                after_["split_before"] = min(AHEAD, after_["units"])

        def at(st, name, n=0):
            return base[st["n"]][name] + n

        def enter(eng, st):
            if st["n"]:
                eng.wait_ge(stage_done, 4 * st["n"])

        def leave(eng):
            eng.drain().then_inc(stage_done, 1)


        QUERY = (part(0, 16, S, of=AR), part(4096, 16, S, of=AR))

        def picking(tiles, score, cand, hot, rest):
            n, at_ = len(tiles), [0]

            def more(*shape):
                size = n * int(np.prod(shape))
                x = rest[:, at_[0]:at_[0] + size]
                at_[0] += size
                if len(shape) == 1:
                    return x.rearrange("p (t a) -> p t a", t=n)
                if len(shape) == 2:
                    return x.rearrange("p (t a b) -> p t a b", t=n, b=shape[1])
                return x.rearrange("p (t a b c) -> p t a b c", t=n, b=shape[1], c=shape[2])

            return dict(tiles=tiles, score=score, cand=cand, hot=hot,
                        top=more(PH, 2, PTOP), top_at=more(PH, 2, PTOP).bitcast(U32), top_atf=more(PH, 2, PTOP),
                        best=more(PH, PTOP), best_at=more(PH * PTOP).bitcast(U32),
                        row=more(PH * PTOP).bitcast(U32), col=more(PH * PTOP).bitcast(U32),
                        rowf=more(PH * PTOP), colf=more(PH * PTOP),
                        exp_row=more(PH * PTOP), exp_col=more(PH * PTOP), sums=more(PH))

        def four(x, b, c):
            return x.rearrange("p (t b c) -> p t b c", b=b, c=c)

        SCORE = part(8192, NT, 16, PK)
        CAND = part(0, NT, PH, PTOP * PTOP)
        HOT = part(4096, PH, PTOP, PTOP)
        PICK_BOTH = picking((0, 1), SCORE, CAND, HOT, A[:, 12288:16384])
        PICK_FIRST = picking((0,), SCORE[:, 0:1], CAND[:, 0:1], HOT, A[:, 12288:16384])
        PICK_LATE = picking((1,), four(XTF[:, 0:2048], 16, PK), four(XTF[:, 2048:4096], PH, PTOP * PTOP),
                            WHF[:, 0:2048].rearrange("p (h a b) -> p h a b", a=PTOP, b=PTOP), WHF[:, 2048:4096])

        def score_of(st, t):
            return PICK_LATE["score"][:, 0] if st["layer"] == 1 and t == 1 else SCORE[:, t]
        GATE = part(18176, NT, PSLOTS)
        EXPERT = part(17920, NT, PSLOTS).bitcast(I32)
        UROWS = part(0, BATCH, D)
        VROWS = part(8192, BATCH, D)
        DIAG = part(16384, BATCH, P)
        PEER_SMALL = part(17408, 256)
        DOTS = PEER_SMALL[:, 0:16].rearrange("p (a b) -> p a b", a=2)
        GELU = PEER_SMALL[:, 16:32].rearrange("p (a b) -> p a b", a=2)
        WEIGHTS = PEER_SMALL[:, 32:48].rearrange("p (a b) -> p a b", a=2)
        STAGED = part(17696, 2, PTOP).bitcast(I32)

        R0 = 10256
        g_i = A[0:16, R0:R0 + S]
        g_f = A[0:16, R0 + S:R0 + 2 * S]
        g_t = A[0:16, R0 + 2 * S:R0 + 3 * S]
        g_e = A[0:16, R0 + 3 * S:R0 + 4 * S]
        g_b = A[0:16, R0 + 4 * S:R0 + 5 * S]
        g_r = A[0:16, R0 + 5 * S:R0 + 6 * S]
        g_m = A[0:16, R0 + 6 * S:R0 + 7 * S]
        g_floor = A[0:16, R0 + 7 * S:R0 + 8 * S]
        m_rT = part(R0 + 8 * S, NT, MH)
        m_floor = part(R0 + 8 * S + 16, NT, MH)
        m_den = part(R0 + 8 * S + 32, 8)
        m_w = part(R0 + 8 * S + 64, 2, 3 * P)
        m_p = part(R0 + 8 * S + 64 + 6 * P, 2, 3 * P)
        m_cw = part(R0 + 8 * S + 64 + 12 * P, 8, 4)
        fx = small[0:16, :]
        f_l, f_e, f_c = (MOD[0:16, n * S:(n + 1) * S] for n in range(3))


        k_log = part(4096, 3 * TW)
        k_lost = part(14336, 3 * TW)
        k_exp = part(15872, 3 * TW)
        k_exp = [k_exp, XTF[:, 0:3 * TW]]
        k_att = [MOD[:, 0:3 * TW], XTF[:, 3 * TW:6 * TW]]

        def soft_bufs(st):
            w = st["work"]
            return [A[:, x:x + 3 * TW] for x in (w, st["work2"])], A[:, w + 3 * TW:w + 6 * TW]

        def soft_small(st):
            return [[small[:, 64 * b + n:64 * b + n + 2 * HG] for b in range(2)] for n in (0, 16, 32)]

        def head_square(st):
            n = st["heads"] * st["hd"]
            return H[:, :, :] if n <= D else part(7744, NT, n)

        def heads_of(src, t, n):
            return src[:, t, 0:n]

        f_gate = part(0, 2, S)
        f_raw = part(2 * S, 2, S)
        f_hidden = (part(4 * S, 2, S, of=AR), part(6 * S, 2, S, of=AR))

        r_freq = r_freq_own[:, :]
        r_pos = small[:, 0:NT]
        r_ang = small[:, 64:128]
        r_turn = small[:, 128:192]
        r_cs = small[:, 192:256]
        r_int = rope_int[:, :]
        r_tmp = part(16128, 4 * AH * (ROPE // 2))
        rope_loaded = sem("rope_loaded")

        def used(pos, turn=0):
            return RING + pos + 1 + turn * RING

        def split_hi(act, st, q, turn=0):
            if isinstance(q, int) and q < st.get("split_before", 0):
                return
            upper_part(act, st, q, turn)

        def upper_part(act, st, q, turn=0):
            pos, n = st["unit0"] + q, st["floats"]
            act.wait_ge(w_loaded[pos % RING], (turn + pos // RING + 1) * 16)
            nc.scalar.activation(WH[:, pos % RING, 0:n], W[:, pos % RING, 0:n], ACT.Copy).then_inc(hi_ready, 1)

        def split_lo(dve, st, q, turn=0):
            if isinstance(q, int) and q < st.get("split_before", 0):
                return
            lower_part(dve, nc.vector, st, q, turn)

        def lower_part(eng, e, st, q, turn=0):
            pos, n = st["unit0"] + q, st["floats"]
            eng.wait_ge(hi_ready, st["split0"] + q + 1 + turn * RING)
            e.tensor_tensor(WL[:, pos % RING, 0:n], W[:, pos % RING, 0:n],
                            WH[:, pos % RING, 0:n].bitcast(F32), ALU.subtract).then_inc(lo_ready, 1)

        block = ctx.enter_context(nc.Block())

        @block.sync
        def _(sp):
            sp.dma_start(X[:, :, :], d["x"]).then_inc(inputs_loaded, 16)

            def load(st, n, pos, turn):
                sp.wait_ge(unit_used, turn * RING + pos + 1)
                src = d[st["weights"]][n] if isinstance(n, int) else \
                    d[st["weights"]][bass.ds(n, 1)].rearrange("a p n -> (a p) n")
                sp.dma_start(W[:, pos % RING, 0:st["floats"]], src).then_inc(w_loaded[pos % RING], 16)

            for st in STAGES:
                units, pos = st["units"], st["unit0"]
                turns = units // RING if units >= 2 * RING else 0
                if turns:
                    with sp.Fori(0, turns) as i:
                        for q in range(RING):
                            load(st, i * RING + q, pos + q, i)
                for q in range(turns * RING, units):
                    load(st, q, pos + q, 0)
            sp.wait_ge(stage_done, 4 * len(STAGES))
            sp.dma_start(d["out"], X[:, :, :]).then_inc(stored, 16)
            sp.wait_ge(stored, 16)

        @block.gpsimd
        def _(pool):
            pool.memset(ident[:, :], 0.0)
            pool.memset(ones[:, :], 1.0)
            pool.memset(causal[:, :], 0.0)
            pool.memset(zrow[:, :], 0.0)
            pool.memset(eps[:, :], EPS)
            pool.memset(m_v[:, :, :, MV:MV + 1], 1.0)
            pool.iota(iota16[:, :], pattern=[[1, 16]], base=0, channel_multiplier=0,
                      allow_small_or_imprecise_dtypes=True)
            pool.drain()
            pool.affine_select(out=ident[:, :], in_=ident[:, :], compare_op=ALU.not_equal, fill=1.0,
                               base=0, pattern=[[-1, P]], channel_multiplier=1)
            pool.affine_select(out=after[:, :], in_=ones[:, :], compare_op=ALU.is_gt, fill=0.0,
                               base=0, pattern=[[-1, P]], channel_multiplier=1)
            pool.affine_select(out=before[:, :], in_=ones[:, :], compare_op=ALU.is_gt, fill=0.0,
                               base=0, pattern=[[1, P]], channel_multiplier=-1)
            pool.affine_select(out=upto[:, :], in_=ones[:, :], compare_op=ALU.is_ge, fill=0.0,
                               base=0, pattern=[[1, P]], channel_multiplier=-1)
            pool.affine_select(out=causal[:, :], in_=causal[:, :], compare_op=ALU.is_ge, fill=-HUGE,
                               base=P, pattern=[[-1, S]], channel_multiplier=1)
            pool.drain().then_inc(consts_ready, 1)
            pool.drain().then_inc(SEM["outgoing_free"], PAIRS)

            def gather(st):
                u_dram, v_dram = d[f"peer_u{st['layer']}"], d[f"peer_v{st['layer']}"]
                n0 = st["gather0"] * NT * PSLOTS

                def claim(name, count):
                    pool.wait_ge(SEM[name], count)
                    pool.sem_inc(SEM["claimed"], 1)

                def fetch(t, i, e):
                    m = n0 + t * PSLOTS + i * PTOP
                    pool.tensor_copy(STAGED[:, e, :], EXPERT[:, t, bass.ds(i * PTOP, PTOP)]
                                     ).then_inc(SEM["indices_staged"], 1)
                    claim("indices_staged", at(st, "indices_staged", t * PH + 1) + i)
                    for ab in range(2):
                        for ring, table, free, loaded in ((UROWS, u_dram, "expert_free", u_loaded),
                                                          (VROWS, v_dram, "mix_free", v_loaded)):
                            for q in range(BATCH):
                                claim(free, m + ab * BATCH + q + 1)
                                pool.indirect_dma_start(
                                    ring[:, q, :], None, table,
                                    bass.IndirectOffsetOnAxis(ap=STAGED[:, e, ab * BATCH + q:ab * BATCH + q + 1],
                                                              axis=0)).then_inc(loaded[q], 16)

                for t in range(NT):
                    if t == 1 and st["layer"] == 1:
                        pool.wait_ge(SEM["picked"], at(st, "picked", 1))
                    with pool.Fori(0, PH // 2) as i:
                        for e in range(2):
                            fetch(t, i * 2 + e, e)

            def headnorm(st):
                k, hd, heads = st["gain"], st["hd"], st["heads"]
                pool.wait_ge(gain_loaded[k % 2], 16 * (k // 2 + 1))
                pool.wait_ge(SEM["scaled_ready"], at(st, "scaled_ready", 1))
                for t in range(NT):
                    x = heads_of(st["sides"][0][0], t, heads * hd).rearrange("p (h e) -> p h e", e=hd)
                    pool.tensor_tensor(x, x, GAIN[:, k % 2, 0:hd].unsqueeze(1).to_broadcast([P, heads, hd]), ALU.mult)

            def topk(st):
                def take(j, lap, dst):
                    pool.wait_ge(SEM["bank_free0"], at(st, "bank_free0", j + 1) + lap)
                    pool.tensor_tensor(dst, dst, OUTGOING[:, j % PAIRS, :], ALU.add
                                       ).then_inc(SEM["outgoing_free"], 1)

                own = 6 * D // TW
                pool.wait_ge(bias_loaded, 16 * 4)
                with pool.Fori(0, own // PAIRS) as i:
                    for j in range(PAIRS):
                        take(j, i * PAIRS, MOD[:, bass.ds(i * (PAIRS * TW) + j * TW, TW)])
                for j in range(own, st["tiles"]):
                    take(j, 0, KVMOD[:, (j - own) * TW:(j - own + 1) * TW])

            for st in STAGES:
                enter(pool, st)
                if st["kind"] == "gather":
                    gather(st)
                elif st["kind"] == "topk" and "tiles" in st:
                    topk(st)
                elif st["kind"] == "headnorm" and len(st["sides"]) == 2:
                    headnorm(st)
                elif st.get("decay") and st["kind"] == "turn":
                    pool.memset(f_qT[FOX_D:FOX_D + 1, :, :], 1.0)
                elif st.get("next"):
                    for q in range(st["next"]["split_before"]):
                        lower_part(pool, nc.gpsimd, st["next"], q)
                leave(pool)


        def ffn_schedule(eng, unit, hidden):
            for q in range(5):
                unit(q, 0)
            hidden(0, 0)
            with eng.Fori(0, (FB - 2) // 2) as i:
                for b in range(2):
                    for q in range(3):
                        unit(5 + 3 * b + q, i)
                    hidden(b + 1, i)
            unit(3 * FB - 1, 0)
            hidden(FB - 1, 0)

        @block.tensor
        def _(pe):
            mm, tr = nc.tensor.matmul, nc.tensor.transpose
            pe.wait_ge(consts_ready, 1)
            pe.drain().then_inc(unit_used, RING)

            PASSES = ((0, 0), (0, 1), (1, 0))

            def keep_warm(products, bank=7):
                for _ in range(products):
                    mm(PS[:, bank, :], CB[0][:, 0, :], CB[0][:, 0:4, :].rearrange("p a b -> p (a b)"),
                       start=True, stop=True)

            def unit_of(st, q, turn=0):
                pos = st["unit0"] + q
                pe.wait_ge(lo_ready, st["split0"] + q + 1 + turn * RING)
                return WH[:, pos % RING, :], WL[:, pos % RING, :]

            def moving(st, q, turn, lhs, kc, width, halves, free):
                per = kc // 2
                for u in range(per):
                    w = [x[:, 0:2 * width].rearrange("p (k n) -> p k n", n=width)
                         for x in unit_of(st, q * per + u, turn)]
                    for t in range(halves):
                        if u == 0 and free is not None:
                            pe.wait_ge(SEM[f"bank_free{t}"], at(st, f"bank_free{t}", q - PAIRS + 1) + free)
                        for k in range(2):
                            for n, (a, b) in enumerate(PASSES):
                                ins = mm(PS[:, 2 * (q % PAIRS) + t, 0:width], lhs(a, 2 * u + k, t), w[b][:, k, :],
                                         start=u + k + n == 0, stop=u == per - 1 and k == 1 and n == 2)
                        if t == halves - 1:
                            ins.then_inc(unit_used, 1)
                        elif u == per - 1:
                            ins.then_inc(SEM["bank_ready"], 1)

            def linear(st):
                for j in range(st["tiles"]):
                    moving(st, j, 0, lambda a, k, t: XT[a][:, k, t * P:(t + 1) * P], st["kc"], st["width"], NT,
                           0 if j >= PAIRS else None)

            def ada(st):
                if st["n"] == 0:
                    pe.wait_ge(SEM["angles_ready"], 1)
                tiles = st["tiles"]

                def one(j, turn, free):
                    moving(st, j, turn, lambda a, k, t: CB[a][:, k, :], KD, TW, 1, free)

                looped = tiles // PAIRS if tiles >= 2 * PAIRS else 0
                if looped:
                    for j in range(PAIRS):
                        one(j, 0, None)
                    with pe.Fori(1, looped) as i:
                        for j in range(PAIRS):
                            one(j, i * 2, i * PAIRS)
                for j in range(looped * PAIRS, tiles):
                    one(j, 0, 0 if j >= PAIRS else None)

            def topk(st):
                def one(j, turn, free):
                    for u in range(KD // 2):
                        pos = st["unit0"] + 4 * j + u
                        pe.wait_ge(w_loaded[pos % RING], (turn + pos // RING + 1) * 16)
                        w = W[:, pos % RING, :].rearrange("p (k n) -> p k n", n=TW)
                        if u == 0 and free is not None:
                            pe.wait_ge(SEM["bank_free0"], at(st, "bank_free0", j - PAIRS + 1) + free)
                        for k in range(2):
                            ins = mm(PS[:, 2 * (j % PAIRS), :], ccol[:, 2 * u + k:2 * u + k + 1].to_broadcast([P, P]),
                                     w[:, k, :], start=u + k == 0, stop=u == KD // 2 - 1 and k == 1)
                        ins.then_inc(unit_used, 1)

                tiles = st.get("tiles", 0)
                if tiles:
                    for j in range(PAIRS):
                        one(j, 0, None)
                    with pe.Fori(1, tiles // PAIRS) as i:
                        for j in range(PAIRS):
                            one(j, i * 2, i * PAIRS)
                    for j in range(tiles // PAIRS * PAIRS, tiles):
                        one(j, 0, 0)

            def linearT(st):
                for j in range(st["tiles"]):
                    for u in range(KD // 2):
                        w = [x.rearrange("p (k n) -> p k n", n=TW) for x in unit_of(st, j * KD // 2 + u)]
                        for b in range(4):
                            n = 4 * j + b
                            if u == 0 and n >= 8:
                                if isinstance(st["dst"], tuple):
                                    pe.wait_ge(SEM["turned_taken1"], at(st, "turned_taken1", n - 7))
                                else:
                                    pe.wait_ge(SEM[f"turned_taken{n % 2}"],
                                               at(st, f"turned_taken{n % 2}", (n - 8) // 2 + 1))
                            for k in range(2):
                                for m, (a, c) in enumerate(PASSES):
                                    ins = mm(PS[:, n % 8, 0:S], w[c][:, k, b * P:(b + 1) * P], XT[a][:, 2 * u + k, :],
                                             start=u + k + m == 0, stop=u == KD // 2 - 1 and k == 1 and m == 2)
                            if b == 3:
                                ins.then_inc(unit_used, 1)
                            elif u == KD // 2 - 1:
                                ins.then_inc(SEM["bank_ready"], 1)

            def gates(st):
                groups = st["groups"]
                for g in range(groups):
                    w = [x.rearrange("p (k n) -> p k n", n=P) for x in unit_of(st, g)]
                    for k in range(KD):
                        for n, (a, c) in enumerate(PASSES):
                            ins = mm(PS[:, g, 0:S], w[c][:, k, :], XT[a][:, k, :], start=k + n == 0,
                                     stop=k == KD - 1 and n == 2)
                    ins.then_inc(unit_used, 1)
                if groups == 2:
                    pe.wait_ge(SEM["scan_ready"], at(st, "scan_ready", 1))
                    for t in range(NT):
                        tr(PS[:, 2, t * MH:(t + 1) * MH], g_r[0:MH, t * P:(t + 1) * P], ident[0:MH, 0:MH])
                        ins = tr(PS[:, 3, t * MH:(t + 1) * MH], g_floor[0:MH, t * P:(t + 1) * P], ident[0:MH, 0:MH])
                    ins.then_inc(SEM["rowsT_ready"], 1)

            def transposes(st, jobs):
                n = 0
                for src, chunks, width, _ in jobs:
                    for t in range(NT):
                        if st["kind"] == "norm":
                            pe.wait_ge(SEM["h_ready"], at(st, "h_ready", t + 1))
                        for c0 in range(0, chunks, 4):
                            if n >= 8:
                                pe.wait_ge(SEM[f"turned_taken{n % 2}"],
                                           at(st, f"turned_taken{n % 2}", (n - 8) // 2 + 1))
                            for c in range(c0, min(c0 + 4, chunks)):
                                ins = tr(PS[0:width, n % 8, (c - c0) * P:(c - c0 + 1) * P], src(t, c), ident[:, :])
                            ins.then_inc(SEM["turned"], 1)
                            n += 1

            def headnorm(st):
                keep_warm(st["heads"] * st["hd"] * (30 if len(st["sides"]) == 1 else 58) // D)

            def turn(st):
                if st["fetched"]:
                    pe.wait_ge(fetched, 16 * st["fetched"])
                transposes(st, st["jobs"])

            def norm(st):
                dst = st["dst"]
                keep_warm(12)
                transposes(st, [(lambda t, c: dst(t)[:, c * P:(c + 1) * P], st["width"] // P, P, XT)])
                keep_warm(4)

            def mlstm(st):
                q_of = lambda h: m_conv[(h % 2) * MQK:(h % 2 + 1) * MQK, h // 2, :]
                k_of = lambda h: m_conv[(h % 2) * MQK:(h % 2 + 1) * MQK, MH // 2 + h // 2, :]

                def scores(h):
                    b = h % 2
                    if h >= 2:
                        pe.wait_ge(SEM["probs_ready"], at(st, "probs_ready", h - 1))
                    mm(PS[:, b, 0:S], ident[0:MH, h:h + 1].to_broadcast([MH, P]), g_m[0:MH, :],
                       start=True, stop=True).then_inc(SEM["decay_spread"], 1)
                    mm(PS[:, 2 + b, 0:S], k_of(h)[:, 0:P], q_of(h), start=True, stop=True)
                    mm(PS[:, 2 + b, S:S + P], k_of(h)[:, P:S], q_of(h)[:, P:S], start=True, stop=True
                       ).then_inc(SEM["scores_ready"], 1)

                scores(0)
                for h in range(MH):
                    if h + 1 < MH:
                        scores(h + 1)
                    keep_warm(6)
                    b = h % 2
                    pe.wait_ge(SEM["probs_ready"], at(st, "probs_ready", h + 1))
                    if h >= 2:
                        pe.wait_ge(SEM["pv_taken"], at(st, "pv_taken", h - 1))
                    mm(PS[:, 4 + b, 0:MV + 1], m_p[:, b, 0:P], m_v[:, 0, h, :], start=True, stop=True)
                    mm(PS[:, 4 + b, 256:256 + MV + 1], m_p[:, b, P:S], m_v[:, 0, h, :], start=True, stop=False)
                    mm(PS[:, 4 + b, 256:256 + MV + 1], m_p[:, b, S:S + P], m_v[:, 1, h, :], start=False, stop=True
                       ).then_inc(SEM["pv_ready"], 1)

            def subkeys(st):
                keep_warm(8)
                w = [x[:, 0:2 * PK].rearrange("p (k n) -> p k n", n=PK) for x in unit_of(st, 0)]
                for t in range(NT):
                    for b in range(16):
                        for n, (a, c) in enumerate(PASSES):
                            ins = mm(PS[:, t * 4 + b // 4, (b % 4) * P:(b % 4 + 1) * P],
                                     QUERY[a][:, b, t * P:(t + 1) * P], w[c][:, b % 2, :], start=n == 0, stop=n == 2)
                        if b % 4 == 3:
                            ins.then_inc(unit_used if t * 4 + b // 4 == 7 else SEM["bank_ready"], 1)

            def gather(st):
                for b in range(4):
                    mm(PS[:, b, :], zrow[:, 0:P], zrow[:, :], start=True, stop=False, skip_group_check=True)
                m0 = st["gather0"] * NT * PSLOTS
                for t in range(NT):
                    with pe.Fori(0, PH) as i:
                        for ab in range(2):
                            for q in range(BATCH):
                                n = t * PSLOTS + ab * BATCH + q
                                pe.wait_ge(v_loaded[q], 16 * ((m0 + n) // BATCH + 1) + 32 * i)
                                pe.wait_ge(SEM["diag_ready"], at(st, "diag_ready", n + 1) + PTOP * i)
                                for c in range(2):
                                    ins = mm(PS[:, 2 * t + c, :], DIAG[:, q, :], VROWS[:, q, c * TW:(c + 1) * TW],
                                             start=False, stop=False, skip_group_check=True)
                                ins.then_inc(SEM["mix_free"], 1)
                for b in range(4):
                    ins = mm(PS[:, b, :], zrow[:, 0:P], zrow[:, :], start=False, stop=True, skip_group_check=True)
                ins.then_inc(SEM["mixed"], 1)

            def stick(st):
                qT, kT, v = st["qT"], st["kT"], st["v"]

                def scores(g):
                    for h in range(HG):
                        hh = g * HG + h
                        mm(PS[:, h // 2, (h % 2) * S:(h % 2 + 1) * S], kT[0:SD, hh, 0:P], qT[0:SD, hh, :],
                           start=True, stop=True)
                        ins = mm(PS[:, 2, h * P:(h + 1) * P], kT[0:SD, hh, P:S], qT[0:SD, hh, P:S],
                                 start=True, stop=True)
                    ins.then_inc(SEM["scores_ready"], 1)

                def between(g):
                    pe.wait_ge(SEM["log_in"], at(st, "log_in", g + 1))
                    lost = k_lost
                    for n in range(2):
                        mm(PS[:, 3 + n, :], after[:, :], lost[:, n * TW:(n + 1) * TW], start=True, stop=False)
                        mm(PS[:, 3 + n, :].rearrange("p (h t) -> p h t", t=S)[:, :, P:S], ones[:, :],
                           lost[:, 2 * TW + 2 * n * P:2 * TW + (2 * n + 2) * P].rearrange("p (h t) -> p h t", t=P),
                           start=False, stop=True)
                    mm(PS[:, 5, :], after[:, :], lost[:, 2 * TW:3 * TW], start=True, stop=True
                       ).then_inc(SEM["between_ready"], 1)

                def values(g):
                    att = k_att[g % 2]
                    pe.wait_ge(SEM["probs_ready"], at(st, "probs_ready", g + 1))
                    if g:
                        pe.wait_ge(SEM["pv_taken"], at(st, "pv_taken", g))
                    for h in range(HG):
                        hh = g * HG + h
                        o = lambda t: PS[:, 6, t * 256 + h * SD:t * 256 + (h + 1) * SD]
                        mm(o(0), att[:, h * S:h * S + P], v(0, hh), start=True, stop=True)
                        mm(o(1), att[:, h * S + P:(h + 1) * S], v(0, hh), start=True, stop=False)
                        ins = mm(o(1), att[:, 2 * TW + h * P:2 * TW + (h + 1) * P], v(1, hh), start=False, stop=True)
                    ins.then_inc(SEM["pv_ready"], 1)

                scores(0)
                keep_warm(50)
                for g in range(SH // HG):
                    if g + 1 < SH // HG:
                        pe.wait_ge(SEM["scores_taken"], at(st, "scores_taken", g + 1))
                        scores(g + 1)
                    between(g)
                    if g:
                        values(g - 1)
                    keep_warm(16)
                values(SH // HG - 1)

            def softmax(st):
                qT, kT, v, dk = st["qT"], st["kT"], st["v"], st["dk"]
                probs, probT = soft_bufs(st)

                def scores(g):
                    if g:
                        pe.wait_ge(SEM["scores_taken"], at(st, "scores_taken", g))
                    for h in range(HG):
                        hh = g * HG + h
                        for t, (bank, at_, n) in enumerate(((0, h * P, P), (1 + h // 2, (h % 2) * S, S))):
                            o = PS[:, bank, at_:at_ + n]
                            ins = mm(o, qT[0:dk, hh, t * P:(t + 1) * P], kT[0:dk, hh, 0:n], start=True, stop=True)
                    ins.then_inc(SEM["scores_ready"], 1)

                if st["decay"]:
                    dk += 1
                    pe.wait_ge(decay_moved, 16)
                scores(0)
                for g in range(AH // HG):
                    prob = probs[g % 2]
                    if g + 1 < AH // HG:
                        scores(g + 1)
                    keep_warm(10)
                    pe.wait_ge(SEM["exp_ready"], at(st, "exp_ready", g + 1))
                    for n in range(3):
                        for c in range(4):
                            ins = tr(PS[:, 3 + n, c * P:(c + 1) * P], prob[:, (4 * n + c) * P:(4 * n + c + 1) * P],
                                     ident[:, :])
                        ins.then_inc(SEM["probsT_ready"], 1)
                    pe.wait_ge(SEM["probsT_taken0"], at(st, "probsT_taken0", 2 * g + 2))
                    pe.wait_ge(SEM["probsT_taken1"], at(st, "probsT_taken1", g + 1))
                    if g:
                        pe.wait_ge(SEM["pv_taken"], at(st, "pv_taken", g))
                    for h in range(HG):
                        hh = g * HG + h
                        o = lambda t: PS[:, 6, t * 256 + h * AV:t * 256 + (h + 1) * AV]
                        mm(o(0), probT[:, h * P:(h + 1) * P], v(0, hh), start=True, stop=True)
                        late = 4 * P + h * S
                        mm(o(1), probT[:, late:late + P], v(0, hh), start=True, stop=False)
                        ins = mm(o(1), probT[:, late + P:late + S], v(1, hh), start=False, stop=True)
                    ins.then_inc(SEM["pv_ready"], 1)

            def ffn(st):
                for b in range(4):
                    mm(PS[:, 4 + b, :], zrow[:, 0:P], zrow[:, :], start=True, stop=False, skip_group_check=True)

                def gate_up(q, f, turn, lap):
                    for a in range(2):
                        w = [x.rearrange("p (k n) -> p k n", n=P) for x in unit_of(st, q + a, turn)]
                        for k in range(KD):
                            for n, (x, c) in enumerate(PASSES):
                                ins = mm(PS[:, f % 2, a * S:(a + 1) * S], w[c][:, k, :], XT[x][:, k, :],
                                         start=k + n == 0, stop=k == KD - 1 and n == 2)
                        ins.then_inc(unit_used, 1)

                def down(q, f, turn, lap):
                    pe.wait_ge(SEM["hidden_ready"], at(st, "hidden_ready", f + 1) + lap)
                    w = unit_of(st, q, turn)
                    for t in range(NT):
                        for n, (x, c) in enumerate(PASSES):
                            for half in range(2):
                                ins = mm(PS[:, 4 + 2 * t + half, :], f_hidden[x][:, f % 2, t * P:(t + 1) * P],
                                         w[c][:, half * TW:(half + 1) * TW], start=False, stop=False,
                                         skip_group_check=True)
                    ins.then_inc(unit_used, 1)

                gate_up(0, 0, 0, 0)
                with pe.Fori(0, (FB - 2) // 2) as i:
                    for b in range(2):
                        gate_up(2 + 3 * b, b + 1, i, i * 2)
                        down(4 + 3 * b, b, i, i * 2)
                gate_up(3 * FB - 4, FB - 1, 0, 0)
                down(3 * FB - 2, FB - 2, 0, 0)
                down(3 * FB - 1, FB - 1, 0, 0)
                for b in range(4):
                    ins = mm(PS[:, 4 + b, :], zrow[:, 0:P], zrow[:, :], start=False, stop=True, skip_group_check=True)
                ins.then_inc(SEM["mixed"], 1)

            parts = dict(ada=ada, topk=topk, norm=norm, headnorm=headnorm, linear=linear, linearT=linearT,
                         gates=gates, mlstm=mlstm, turn=turn, subkeys=subkeys, gather=gather, stick=stick,
                         softmax=softmax, ffn=ffn)
            for st in STAGES:
                enter(pe, st)
                if st["kind"] in parts:
                    parts[st["kind"]](st)
                leave(pe)

        @block.scalar
        def _(act):
            f = nc.scalar.activation

            def load_gain(n):
                name, width = gains[n]
                act.dma_start(GAIN[:, n % 2, 0:width], d[name].partition_broadcast(P)).then_inc(gain_loaded[n % 2], 16)

            act.dma_start(ccol[:, :], d["c"]).then_inc(bias_loaded, 16)
            act.dma_start(bias8[0:MH, :], d["ma_b_if"]).then_inc(inputs_loaded, 16)
            act.dma_start(bias16[:, :], d["fox_b_f"]).then_inc(inputs_loaded, 16)
            act.dma_start(m_cw, d["conv_w"]).then_inc(inputs_loaded, 16)
            act.dma_start(posi[:, :], d["positions"]).then_inc(inputs_loaded, 16)
            act.dma_start(r_freq, d["rope_freq"].partition_broadcast(P)).then_inc(rope_loaded, 16)
            load_gain(0)
            act.wait_ge(bias_loaded, 16)
            f(ccol[:, :], ccol[:, :], ACT.Silu).then_inc(SEM["sines_ready"], 1)
            act.drain().then_inc(SEM["diag_ready"], 1)

            def load_table(func):
                f(unread[:, :], eps[:, :], func)

            def linear(st):
                per = st["kc"] // 2
                if st.get("fetch"):
                    act.dma_start(st["fetch"][1], d[st["fetch"][0]]).then_inc(fetched, 16)
                for q in range(per):
                    split_hi(act, st, q)
                for j in range(st["tiles"]):
                    for q in range((j + 1) * per, min((j + 2) * per, st["units"])):
                        split_hi(act, st, q)
                    for t in range(NT):
                        what, dst, *_ = st["out"](t, j)
                        if what in ("sigmoid", "copy by ACT") or (what == "copy" and t == 0):
                            if t == 0:
                                act.wait_ge(SEM["bank_ready"], at(st, "bank_ready", j + 1))
                            else:
                                act.wait_ge(unit_used, used(st["unit0"] + (j + 1) * per - 1))
                            src = PS[:, 2 * (j % PAIRS) + t, 0:st["width"]]
                            if len(dst.shape) == 3:
                                src = src.rearrange("p (a b) -> p a b", b=dst.shape[2])
                            f(dst, src, ACT.Sigmoid if what == "sigmoid" else ACT.Copy
                              ).then_inc(SEM[f"bank_free{t}"], 1)

            def linearT(st):
                parts_ = isinstance(st["dst"], tuple)
                for q in range(4):
                    split_hi(act, st, q)
                for j in range(st["tiles"]):
                    for q in range(4 * j + 4, min(4 * j + 8, st["units"])):
                        split_hi(act, st, q)
                    for b in range(0, 4, 1 if parts_ else 2):
                        n = 4 * j + b
                        if b == 3:
                            act.wait_ge(unit_used, used(st["unit0"] + 4 * j + 3))
                        else:
                            act.wait_ge(SEM["bank_ready"], at(st, "bank_ready", 3 * j + b + 1))
                        f((st["dst"][0] if parts_ else st["dst"])[:, n, :], PS[:, n % 8, 0:S], ACT.Copy
                          ).then_inc(SEM["turned_taken0"], 1)

            def log_sigmoid_in(m, pre, a, e):
                f(a[0:m, :], pre[0:m, :], ACT.Abs)
                act.drain()
                f(e[0:m, :], a[0:m, :], ACT.Exp, scale=-1.0)
                act.drain()
                f(e[0:m, :], e[0:m, :], ACT.Ln, bias=1.0).then_inc(SEM["log_out"], 1)

            def gates(st):
                act.wait_ge(inputs_loaded, 16 * 5)
                for g in range(st["groups"]):
                    split_hi(act, st, g)
                act.wait_ge(unit_used, used(st["unit0"] + st["groups"] - 1))
                if st["groups"] == 2:
                    f(g_i[0:MH, :], PS[0:MH, 0, 0:S], ACT.Identity, bias=bias8[0:MH, 0:1])
                    f(g_f[0:MH, :], PS[0:MH, 1, 0:S], ACT.Identity, bias=bias8[0:MH, 1:2])
                    act.drain().then_inc(SEM["gates_in"], 1)
                    log_sigmoid_in(MH, g_f, g_t, g_e)
                    act.wait_ge(SEM["rowsT_ready"], at(st, "rowsT_ready", 1))
                    f(m_floor, PS[:, 3, 0:NT * MH].rearrange("p (a b) -> p a b", b=MH), ACT.Exp
                      ).then_inc(SEM["floor_ready"], 1)
                else:
                    f(fx, PS[0:AH, 0, 0:S], ACT.Identity, bias=bias16[:, 0:1])
                    act.drain().then_inc(SEM["gates_in"], 1)
                    log_sigmoid_in(AH, fx, f_l, f_e)

            def taken(st, jobs):
                n = 0
                for _, chunks, width, dst in jobs:
                    for t in range(NT):
                        for c0 in range(0, chunks, 4):
                            if n % 2 == 0 or isinstance(dst, tuple):
                                c1 = min(c0 + 4, chunks)
                                act.wait_ge(SEM["turned"], at(st, "turned", n + 1))
                                f((dst[0] if isinstance(dst, tuple) else dst)[0:width, c0:c1, t * P:(t + 1) * P],
                                  PS[0:width, n % 8, 0:(c1 - c0) * P].rearrange("p (a b) -> p a b", b=P),
                                  ACT.Copy).then_inc(SEM["turned_taken0"], 1)
                            n += 1

            def split_ahead(st):
                if st["next"]:
                    for q in range(st["next"]["split_before"]):
                        upper_part(act, st["next"], q)

            def turn(st):
                if st["decay"]:
                    act.dma_start(f_kT[FOX_D:FOX_D + 1, :, :], f_c[0:AH, :]).then_inc(decay_moved, 16)
                split_ahead(st)
                taken(st, st["jobs"])

            def norm(st):
                if st["gain"] + 1 < len(gains):
                    load_gain(st["gain"] + 1)
                if st["n"] == 1:
                    act.wait_ge(inputs_loaded, 16 * 5)
                w = st["width"]
                for t in range(NT):
                    f(st["dst"](t), st["src"](t), ACT.Square, accum_out=ss[:, t:t + 1])
                    act.drain()
                    f(rms[:, t:t + 1], ss[:, t:t + 1], ACT.Sqrt, scale=1.0 / w, bias=eps[:, 0:1]
                      ).then_inc(SEM["rms_ready"], 1)
                split_ahead(st)
                taken(st, [(None, w // P, P, XT)])

            def headnorm(st):
                if st["gain"] + 1 < len(gains):
                    load_gain(st["gain"] + 1)
                n, m = st["heads"] * st["hd"], NT * st["heads"]
                sq = head_square(st)

                def roots(side):
                    act.wait_ge(SEM["sum_ready"], at(st, "sum_ready", NT * (side + 1)))
                    f(rms[:, side * m:(side + 1) * m], ss[:, side * m:(side + 1) * m], ACT.Sqrt,
                      scale=1.0 / st["hd"], bias=eps[:, 0:1]).then_inc(SEM["rms_ready"], 1)

                for side, (src, _, _) in enumerate(st["sides"]):
                    for t in range(NT):
                        if side:
                            act.wait_ge(SEM["sum_ready"], at(st, "sum_ready", t + 1))
                        f(sq[:, t, 0:n], heads_of(src, t, n), ACT.Square).then_inc(SEM["sq_ready"], 1)
                        if side and t == 0:
                            roots(0)
                roots(len(st["sides"]) - 1)

            def conv(st):
                for b in range(8):
                    act.wait_ge(SEM["conv_ready"], at(st, "conv_ready", b + 1))
                    f(m_conv[:, b, :], m_conv[:, b, :], ACT.Silu)

            def mlstm(st):
                load_table(ACT.Exp)
                for h in range(MH):
                    act.wait_ge(SEM["exponent_ready"], at(st, "exponent_ready", h + 1))
                    f(m_w[:, h % 2, :], m_w[:, h % 2, :], ACT.Exp).then_inc(SEM["exp_ready"], 1)

            def subkeys(st):
                split_hi(act, st, 0)
                for t in range(NT):
                    for b in range(0, 4, 2):
                        n = t * 4 + b
                        act.wait_ge(SEM["bank_ready"], at(st, "bank_ready", n + 1))
                        f(score_of(st, t)[:, 4 * b:4 * b + 4, :], PS[:, n, :].rearrange("p (a b) -> p a b", b=P), ACT.Copy)

            def topk(st):
                if "tiles" in st:
                    f(GATE0, mod(5), ACT.Copy)
                    act.drain()
                    act.dma_start(MOD[:, :], d[st["bias"]].partition_broadcast(P)).then_inc(bias_loaded, 16)
                    act.dma_start(KVMOD, d["kv_ada_b"].partition_broadcast(P)).then_inc(bias_loaded, 16)

                def one_plus(x, tiles):
                    act.wait_ge(SEM["outgoing_free"], at(st, "outgoing_free", tiles))
                    f(x, x, ACT.Copy, bias=1.0)

                def take(j, turn, lap):
                    act.wait_ge(unit_used, used(st["unit0"] + 4 * j + 3, turn))
                    act.wait_ge(SEM["outgoing_free"], at(st, "outgoing_free", j + 1 - PAIRS) + lap)
                    f(OUTGOING[:, j % PAIRS, :], PS[:, 2 * (j % PAIRS), :], ACT.Copy).then_inc(SEM["bank_free0"], 1)

                def take_laps(first, end):
                    with act.Fori(first, end) as i:
                        for j in range(PAIRS):
                            take(j, i * 2, i * PAIRS)

                if "tiles" in st:
                    take_laps(0, 3)
                    one_plus(mod(1), 4)
                act.wait_ge(SEM["top_shifted"], at(st, "top_shifted", 1))
                best = (PICK_BOTH if st["layer"] == 0 else PICK_FIRST)["best"]
                f(best, best, ACT.Exp).then_inc(SEM["top_exp"], 1)
                if "tiles" in st:
                    take_laps(3, st["tiles"] // PAIRS)
                    one_plus(mod(4), 10)
                    take(st["tiles"] - 1, 0, 0)
                    one_plus(KVMOD[:, D:2 * D], 16)

            def gather(st):
                def mix(t, first, end):
                    with act.Fori(first, end) as i:
                        for ab in range(2):
                            n = t * PSLOTS + ab * BATCH
                            act.wait_ge(SEM["dots_ready"], at(st, "dots_ready", n // BATCH + 1) + 2 * i)
                            f(GELU[:, ab, :], DOTS[:, ab, :], ACT.Gelu).then_inc(SEM["gelu_ready"], 1)
                            act.wait_ge(SEM["weights_ready"], at(st, "weights_ready", n // BATCH + 1) + 2 * i)
                            for q in range(BATCH):
                                act.wait_ge(SEM["mix_free"], at(st, "mix_free", n + q + 1) + PTOP * i)
                                f(DIAG[:, q, :], ident[:, :], ACT.Copy, scale=WEIGHTS[:, ab, q:q + 1]
                                  ).then_inc(SEM["diag_ready"], 1)

                if st["layer"] == 1:
                    mix(0, 0, LATE[2])
                    act.wait_ge(SEM["top_shifted"], at(st, "top_shifted", 1))
                    f(PICK_LATE["best"], PICK_LATE["best"], ACT.Exp).then_inc(SEM["top_exp"], 1)
                    mix(0, LATE[2], PH)
                else:
                    mix(0, 0, PH)
                mix(1, 0, PH)

            def stick(st):
                def soft(g):
                    act.wait_ge(SEM["scores_ready"], at(st, "scores_ready", g + 1))
                    z = PS[:, 0:3, :]
                    view = lambda b: b.rearrange("p (a b) -> p a b", b=TW)
                    f(view(k_log), z, ACT.Abs)
                    act.drain()
                    f(k_log, k_log, ACT.Exp, scale=-1.0)
                    act.drain()
                    f(k_log, k_log, ACT.Ln, bias=1.0).then_inc(SEM["soft_ready"], 1)

                soft(0)
                for g in range(SH // HG):
                    if g + 1 < SH // HG:
                        soft(g + 1)
                    act.wait_ge(SEM["exponent_ready"], at(st, "exponent_ready", g + 1))
                    if g >= 2:
                        act.wait_ge(SEM["pv_ready"], at(st, "pv_ready", g - 1))
                    f(k_att[g % 2], k_exp[g % 2], ACT.Exp).then_inc(SEM["exp_ready"], 1)

            def softmax(st):
                probs, probT = soft_bufs(st)
                load_table(ACT.Exp)
                for g in range(AH // HG):
                    prob = probs[g % 2]
                    sums, nmax, rsum = (x[g % 2] for x in soft_small(st))
                    act.wait_ge(SEM["max_ready"], at(st, "max_ready", g + 1))
                    for t in range(NT):
                        for h in range(HG):
                            a0, n = (h * P, P) if t == 0 else (4 * P + h * S, S)
                            f(prob[:, a0:a0 + n], prob[:, a0:a0 + n], ACT.Exp, bias=nmax[:, t * HG + h:t * HG + h + 1],
                              accum_out=sums[:, t * HG + h:t * HG + h + 1])
                    act.drain().then_inc(SEM["exp_ready"], 1)
                    for n in (0, 2):
                        act.wait_ge(SEM["probsT_ready"], at(st, "probsT_ready", 3 * g + n + 1))
                        f(probT[:, n * TW:(n + 1) * TW], PS[:, 3 + n, :], ACT.Copy).then_inc(SEM["probsT_taken0"], 1)

            def ffn(st):
                def hidden(fb, i):
                    b = fb % 2
                    act.wait_ge(unit_used, used(st["unit0"] + (1 if fb == 0 else 3 * fb), i))
                    f(f_gate[:, b, :], PS[:, b, 0:S], ACT.Silu).then_inc(SEM["hidden_silu"], 1)
                    act.wait_ge(SEM["hidden_raw"], at(st, "hidden_raw", fb + 1) + 2 * i)
                    f(f_hidden[0][:, b, :], f_raw[:, b, :], ACT.Copy).then_inc(SEM["hidden_hi"], 1)

                ffn_schedule(act, lambda q, i: split_hi(act, st, q, i), hidden)

            def rope(st):
                act.wait_ge(SEM["angles_ready"], at(st, "angles_ready", 1))
                f(r_cs, r_ang, ACT.Sin).then_inc(SEM["sines_ready"], 1)

            def ada(st):
                act.dma_start(st["dst"][:, 0:st["tiles"] * TW], d[st["bias"]].partition_broadcast(P)
                              ).then_inc(bias_loaded, 16)
                units = st["units"]
                looped = units // (2 * RING) if units >= 4 * RING else 0
                if looped:
                    with act.Fori(0, looped) as i:
                        for q in range(2 * RING):
                            split_hi(act, st, q, i * 2)
                for q in range(looped * 2 * RING, units):
                    split_hi(act, st, q)

            parts = dict(ada=ada, norm=norm, linear=linear, linearT=linearT, gates=gates, conv=conv, mlstm=mlstm,
                         headnorm=headnorm, turn=turn, subkeys=subkeys, topk=topk,
                         gather=gather, stick=stick, softmax=softmax, ffn=ffn, rope=rope)
            for st in STAGES:
                enter(act, st)
                past = STAGES[st["n"] - 1] if st["n"] else {}
                if len(past.get("sides", ())) == 2 and past["gain"] + 2 < len(gains):
                    load_gain(past["gain"] + 2)
                if st["kind"] in parts:
                    parts[st["kind"]](st)
                if st["kind"] in ("gather", "ffn", "stick", "softmax", "mlstm") or \
                        st["kind"] == "linear" and st["weights"].startswith("ple_gate"):
                    act.drain()
                    load_table(ACT.Sqrt)
                leave(act)

        @block.vector
        def _(dve):
            v = nc.vector
            tt, ts, stt, cp = v.tensor_tensor, v.tensor_scalar, v.scalar_tensor_tensor, v.tensor_copy

            dve.drain().then_inc(SEM["expert_free"], BATCH)
            dve.drain().then_inc(SEM["mix_free"], BATCH)
            dve.wait_ge(consts_ready, 1)
            dve.wait_ge(SEM["sines_ready"], 1)
            spread = part(0, KD, P)
            for k in range(KD):
                ts(spread[:, k, :], ones[:, :], ccol[:, k:k + 1], None, ALU.mult)
            dve.drain()
            cp(CB[0][:, :, :], spread)
            dve.drain()
            tt(CB[1][:, :, :], spread, CB[0][:, :, :].bitcast(F32), ALU.subtract)
            dve.drain().then_inc(SEM["angles_ready"], 1)

            def ada(st):
                tiles, dst = st["tiles"], st["dst"]
                dve.wait_ge(bias_loaded, 16 * 2)

                def split(j, turn):
                    for q in range(4):
                        split_lo(dve, st, 4 * j + q, turn)

                def take(j, turn, lap):
                    dve.wait_ge(unit_used, used(st["unit0"] + 4 * j + 3, turn))
                    o = dst[:, j * TW:(j + 1) * TW] if isinstance(lap, int) else \
                        dst[:, bass.ds(lap * (PAIRS * TW) + j * TW, TW)]
                    tt(o, o, PS[:, 2 * (j % PAIRS), :], ALU.add).then_inc(SEM["bank_free0"], 1)

                split(0, 0)
                looped = tiles // PAIRS - 1 if tiles >= 2 * PAIRS else 0
                if looped:
                    with dve.Fori(0, looped) as i:
                        for j in range(PAIRS):
                            split(j + 1, i * 2)
                            take(j, i * 2, i)
                for j in range(looped * PAIRS, tiles):
                    if j + 1 < tiles:
                        split(j + 1, 0)
                    take(j, 0, 0)
                dve.drain()
                for s in st["scales"]:
                    ts(dst[:, s * D:(s + 1) * D], dst[:, s * D:(s + 1) * D], 1.0, None, ALU.add)

            def linear(st):
                per = st["kc"] // 2
                for q in range(per):
                    split_lo(dve, st, q)
                for j in range(st["tiles"]):
                    for q in range((j + 1) * per, min((j + 2) * per, st["units"])):
                        split_lo(dve, st, q)
                    for t in range(NT):
                        what, dst, *gate = st["out"](t, j)
                        if what == "residual" or (what == "copy" and t == 1):
                            if t == 0:
                                dve.wait_ge(SEM["bank_ready"], at(st, "bank_ready", j + 1))
                            else:
                                dve.wait_ge(unit_used, used(st["unit0"] + (j + 1) * per - 1))
                            src = PS[:, 2 * (j % PAIRS) + t, 0:st["width"]]
                            if what == "copy":
                                if len(dst.shape) == 3:
                                    src = src.rearrange("p (a b) -> p a b", b=dst.shape[2])
                                cp(dst, src).then_inc(SEM[f"bank_free{t}"], 1)
                            elif gate[0] is None:
                                tt(dst, dst, src, ALU.add).then_inc(SEM[f"bank_free{t}"], 1)
                            else:
                                tmp = H[:, t, j * TW:(j + 1) * TW]
                                tt(tmp, gate[0], src, ALU.mult).then_inc(SEM[f"bank_free{t}"], 1)
                                dve.drain()
                                tt(dst, dst, tmp, ALU.add)

            def linearT(st):
                parts_ = isinstance(st["dst"], tuple)
                for q in range(4):
                    split_lo(dve, st, q)
                for j in range(st["tiles"]):
                    for q in range(4 * j + 4, min(4 * j + 8, st["units"])):
                        split_lo(dve, st, q)
                    for b in range(4) if parts_ else (1, 3):
                        n = 4 * j + b
                        if parts_:
                            dve.wait_ge(SEM["turned_taken0"], at(st, "turned_taken0", n + 1))
                            tt(st["dst"][1][:, n, :], PS[:, n % 8, 0:S], st["dst"][0][:, n, :].bitcast(F32),
                               ALU.subtract).then_inc(SEM["turned_taken1"], 1)
                            continue
                        if b == 3:
                            dve.wait_ge(unit_used, used(st["unit0"] + 4 * j + 3))
                        else:
                            dve.wait_ge(SEM["bank_ready"], at(st, "bank_ready", 3 * j + b + 1))
                        cp(st["dst"][:, n, :], PS[:, n % 8, 0:S]).then_inc(SEM["turned_taken1"], 1)

            def log_sigmoid_cumsum(st, m, pre, e, t_, out):
                dve.wait_ge(SEM["gates_in"], at(st, "gates_in", 1))
                dve.wait_ge(SEM["log_out"], at(st, "log_out", 1))
                stt(t_[0:m, :], pre[0:m, :], 0.0, e[0:m, :], ALU.min, ALU.subtract)
                dve.drain()
                v.tensor_tensor_scan(out=out[0:m, :], data0=t_[0:m, :], data1=zrow[0:m, 0:S], initial=0.0,
                                     op0=ALU.add, op1=ALU.add)
                dve.drain().then_inc(SEM["log_in"], 1)

            def gates(st):
                for g in range(st["groups"]):
                    split_lo(dve, st, g)
                if st["groups"] == 2:
                    log_sigmoid_cumsum(st, MH, g_f, g_e, g_t, g_b)
                    tt(g_r[0:MH, :], g_i[0:MH, :], g_b[0:MH, :], ALU.subtract)
                    dve.drain()
                    v.tensor_tensor_scan(out=g_m[0:MH, :], data0=g_r[0:MH, :], data1=g_r[0:MH, :], initial=0.0,
                                         op0=ALU.max, op1=ALU.max)
                    dve.drain()
                    stt(g_floor[0:MH, :], g_b[0:MH, :], -1.0, g_m[0:MH, :], ALU.mult, ALU.subtract)
                    dve.drain().then_inc(SEM["scan_ready"], 1)
                    dve.wait_ge(SEM["rowsT_ready"], at(st, "rowsT_ready", 1))
                    cp(m_rT, PS[:, 2, 0:NT * MH].rearrange("p (a b) -> p a b", b=MH)).then_inc(SEM["rows_taken"], 1)
                else:
                    log_sigmoid_cumsum(st, AH, fx, f_e, f_l, f_c)
                    ts(f_c[0:AH, :], f_c[0:AH, :], -1.0, None, ALU.mult)

            def taken(st, jobs):
                n = 0
                for _, chunks, width, dst in jobs:
                    for t in range(NT):
                        for c0 in range(0, chunks, 4):
                            c1 = min(c0 + 4, chunks)
                            if isinstance(dst, tuple):
                                dve.wait_ge(SEM["turned_taken0"], at(st, "turned_taken0", n + 1))
                                hi, lo = (x[0:width, c0:c1, t * P:(t + 1) * P] for x in dst)
                                tt(lo, PS[0:width, n % 8, 0:(c1 - c0) * P].rearrange("p (a b) -> p a b", b=P),
                                   hi.bitcast(F32), ALU.subtract).then_inc(SEM["turned_taken1"], 1)
                            elif n % 2 == 1:
                                dve.wait_ge(SEM["turned"], at(st, "turned", n + 1))
                                cp(dst[0:width, c0:c1, t * P:(t + 1) * P],
                                   PS[0:width, n % 8, 0:(c1 - c0) * P].rearrange("p (a b) -> p a b", b=P)
                                   ).then_inc(SEM["turned_taken1"], 1)
                            n += 1

            def gain_wait(st):
                n = st["gain"]
                dve.wait_ge(gain_loaded[n % 2], 16 * (n // 2 + 1))

            def norm(st):
                w, n = st["width"], st["gain"]
                gain_wait(st)
                g = GAIN[:, n % 2, 0:w]
                if st["scale"] is not None:
                    tt(g, g, st["scale"], ALU.mult)
                for t in range(NT):
                    dve.wait_ge(SEM["rms_ready"], at(st, "rms_ready", t + 1))
                    v.reciprocal(rs[:, t:t + 1], rms[:, t:t + 1])
                    dve.drain()
                    ins = stt(st["dst"](t), st["src"](t), rs[:, t:t + 1], g, ALU.mult, ALU.mult)
                    if st["shift"] is not None:
                        dve.drain()
                        ins = tt(st["dst"](t), st["dst"](t), st["shift"], ALU.add)
                    ins.then_inc(SEM["h_ready"], 1)
                if st["shift"] is not None:
                    dve.drain()
                taken(st, [(None, w // P, P, XT)])

            def headnorm(st):
                heads, hd, sides, times = st["heads"], st["hd"], st["sides"], st["times"]
                n, m = heads * hd, NT * heads
                sq = head_square(st)

                def sums(side, t):
                    dve.wait_ge(SEM["sq_ready"], at(st, "sq_ready", NT * side + t + 1))
                    v.tensor_reduce(out=ss[:, side * m + t * heads:side * m + (t + 1) * heads],
                                    in_=sq[:, t, 0:n].rearrange("p (h e) -> p h e", e=hd), axis=AX.X, op=ALU.add
                                    ).then_inc(SEM["sum_ready"], 1)

                def scaled(side):
                    src, _, factor = sides[side]
                    r = rs[:, side * m:(side + 1) * m]
                    dve.wait_ge(SEM["rms_ready"], at(st, "rms_ready", side + 1))
                    v.reciprocal(r, rms[:, side * m:(side + 1) * m])
                    dve.drain()
                    if factor != 1.0:
                        ts(r, r, factor, None, ALU.mult)
                        dve.drain()
                    for t in range(NT):
                        x = heads_of(src, t, n).rearrange("p (h e) -> p h e", e=hd)
                        tt(x, x, r[:, t * heads:(t + 1) * heads].unsqueeze(2).to_broadcast([P, heads, hd]), ALU.mult)

                sums(0, 0)
                sums(0, 1)
                if len(sides) == 2:
                    sums(1, 0)
                    sums(1, 1)
                    scaled(0)
                    dve.drain().then_inc(SEM["scaled_ready"], 1)
                last = len(sides) - 1
                scaled(last)
                dve.drain()
                k = st["gain"] + last
                dve.wait_ge(gain_loaded[k % 2], 16 * (k // 2 + 1))
                gain = GAIN[:, k % 2, :]
                for t in range(NT):
                    x = heads_of(sides[last][0], t, n)
                    if times is None:
                        x = x.rearrange("p (h e) -> p h e", e=hd)
                        tt(x, x, gain[:, 0:hd].unsqueeze(1).to_broadcast([P, heads, hd]), ALU.mult)
                    else:
                        tt(x, x, gain[:, 0:n], ALU.mult)
                if times is not None:
                    dve.drain()
                    for t in range(NT):
                        x = heads_of(sides[last][0], t, n)
                        tt(x, x, times[:, t, :], ALU.mult)

            def conv(st):
                dve.wait_ge(inputs_loaded, 16 * 5)
                for b in range(8):
                    ts(m_conv[:, b, :], m_qk[:, b, :], m_cw[:, b, 3:4], None, ALU.mult)
                    for back in (1, 2, 3):
                        dve.drain()
                        ins = stt(m_conv[:, b, back:S], m_qk[:, b, 0:S - back], m_cw[:, b, 3 - back:4 - back],
                                  m_conv[:, b, back:S], ALU.mult, ALU.add)
                    ins.then_inc(SEM["conv_ready"], 1)

            def mlstm(st):
                def exponent(h):
                    b = h % 2
                    dve.wait_ge(SEM["decay_spread"], at(st, "decay_spread", h + 1))
                    for s in range(2):
                        cols = slice(0, S) if s == 0 else slice(S, S + P)
                        src = PS[:, b, 0:S] if s == 0 else PS[:, b, P:S]
                        stt(m_w[:, b, cols], src, -1.0,
                            m_rT[:, s, h:h + 1].to_broadcast([P, S if s == 0 else P]), ALU.mult, ALU.add)
                    dve.drain()
                    ts(m_w[:, b, :], m_w[:, b, :], 0.0, None, ALU.min).then_inc(SEM["exponent_ready"], 1)

                def take(h):
                    b = h % 2
                    dve.wait_ge(SEM["pv_ready"], at(st, "pv_ready", h + 1))
                    num = PS[:, 4 + b, :].rearrange("p (t n) -> p t n", t=2)
                    den = m_den.rearrange("p (a b) -> p a b", a=4)
                    cp(den[:, 0, 0:2].unsqueeze(2), num[:, :, MV:MV + 1])
                    dve.drain()
                    stt(den[:, 1, 0:2], den[:, 0, 0:2], -1.0, den[:, 0, 0:2], ALU.mult, ALU.max)
                    dve.drain()
                    tt(den[:, 2, 0:2].unsqueeze(2), den[:, 1, 0:2].unsqueeze(2), m_floor[:, :, h:h + 1], ALU.max)
                    dve.drain()
                    v.reciprocal(den[:, 3, 0:2], den[:, 2, 0:2])
                    dve.drain()
                    for t in range(NT):
                        ts(m_h[:, t, h * MV:(h + 1) * MV], num[:, t, 0:MV], den[:, 3, t:t + 1], None, ALU.mult)
                    dve.drain().then_inc(SEM["pv_taken"], 1)

                exponent(0)
                for h in range(MH):
                    b = h % 2
                    if h + 1 < MH:
                        exponent(h + 1)
                    dve.wait_ge(SEM["exp_ready"], at(st, "exp_ready", h + 1))
                    diag = m_w[:, b, :].rearrange("p (a b) -> p a b", b=P)[:, 0:3:2, :]
                    tt(diag, diag, upto[:, :].unsqueeze(1).to_broadcast([P, 2, P]), ALU.mult)
                    dve.drain()
                    dve.wait_ge(SEM["scores_ready"], at(st, "scores_ready", h + 1))
                    if h >= 2:
                        dve.wait_ge(SEM["pv_ready"], at(st, "pv_ready", h - 1))
                    stt(m_p[:, b, :], PS[:, 2 + b, 0:3 * P], MQK ** -0.5, m_w[:, b, :], ALU.mult, ALU.mult
                        ).then_inc(SEM["probs_ready"], 1)
                    if h:
                        take(h - 1)
                take(MH - 1)

            def subkeys(st):
                split_lo(dve, st, 0)
                for t in range(NT):
                    for b in range(1, 4, 2):
                        n = t * 4 + b
                        if n == 7:
                            dve.wait_ge(unit_used, used(st["unit0"]))
                        else:
                            dve.wait_ge(SEM["bank_ready"], at(st, "bank_ready", n + 1))
                        cp(score_of(st, t)[:, 4 * b:4 * b + 4, :], PS[:, n, :].rearrange("p (a b) -> p a b", b=P))

            def best16(rows, vals, idx):
                for r, x, i in zip(rows, vals, idx):
                    v.max(x[:, 0:8], r)
                dve.drain()
                for r, x, i in zip(rows, vals, idx):
                    v.max_index(i[:, 0:8], x[:, 0:8], r)
                dve.drain()
                for r, x, i in zip(rows, vals, idx):
                    v.match_replace(out=r, in_to_replace=x[:, 0:8], in_values=r, imm_value=-HUGE)
                dve.drain()
                for r, x, i in zip(rows, vals, idx):
                    v.max(x[:, 8:16], r)
                dve.drain()
                for r, x, i in zip(rows, vals, idx):
                    v.max_index(i[:, 8:16], x[:, 8:16], r)
                dve.drain()

            full = [P, PH, PTOP, PTOP]

            def best_halves(b):
                every = [(t, h, p) for t in range(len(b["tiles"])) for h in range(PH) for p in range(2)]
                best16([b["score"][:, t, 2 * h + p, :] for t, h, p in every],
                       [b["top"][:, t, h, p, :] for t, h, p in every],
                       [b["top_at"][:, t, h, p, :] for t, h, p in every])

            def best_pairs(b):
                cp(b["top_atf"], b["top_at"])
                for t in range(len(b["tiles"])):
                    tt(b["cand"][:, t, :, :].rearrange("p h (a b) -> p h a b", b=PTOP),
                       b["top"][:, t, :, 0, :].unsqueeze(3).to_broadcast(full),
                       b["top"][:, t, :, 1, :].unsqueeze(2).to_broadcast(full), ALU.add)
                dve.drain()
                both = [(t, h) for t in range(len(b["tiles"])) for h in range(PH)]
                best16([b["cand"][:, t, h, :] for t, h in both], [b["best"][:, t, h, :] for t, h in both],
                       [b["best_at"][:, t, h * PTOP:(h + 1) * PTOP] for t, h in both])

            def chosen(st, b):
                tiles = b["tiles"]
                sums = b["sums"].unsqueeze(3).to_broadcast([P, len(tiles), PH, PTOP])
                cp(b["sums"], b["best"][:, :, :, 0])
                ts(b["row"], b["best_at"], 4, None, ALU.logical_shift_right)
                ts(b["col"], b["best_at"], PTOP - 1, None, ALU.bitwise_and)
                dve.drain()
                tt(b["best"], b["best"], sums, ALU.subtract).then_inc(SEM["top_shifted"], 1)
                cp(b["rowf"], b["row"])
                cp(b["colf"], b["col"])
                dve.drain()
                hot = b["hot"]
                for t in range(len(tiles)):
                    for place, half, out in ((b["rowf"], 0, b["exp_row"]), (b["colf"], 1, b["exp_col"])):
                        tt(hot, place[:, t, :].rearrange("p (h k) -> p h k", k=PTOP).unsqueeze(3).to_broadcast(full),
                           iota16[:, :].unsqueeze(1).unsqueeze(1).to_broadcast(full), ALU.is_equal)
                        dve.drain()
                        tt(hot, hot, b["top_atf"][:, t, :, half, :].unsqueeze(2).to_broadcast(full), ALU.mult)
                        dve.drain()
                        v.tensor_reduce(out=out[:, t, :].rearrange("p (h k) -> p h k", k=PTOP), in_=hot,
                                        axis=AX.X, op=ALU.add)
                        dve.drain()
                mine = slice(tiles[0], tiles[-1] + 1)
                stt(EXPERT[:, mine], b["exp_row"], float(PK), b["exp_col"], ALU.mult, ALU.add)
                dve.wait_ge(SEM["top_exp"], at(st, "top_exp", 1))
                v.tensor_reduce(out=b["sums"], in_=b["best"], axis=AX.X, op=ALU.add)
                dve.drain()
                v.reciprocal(b["sums"], b["sums"])
                dve.drain()
                tt(GATE[:, mine].rearrange("p t (h k) -> p t h k", k=PTOP), b["best"], sums, ALU.mult)

            def topk(st):
                b = PICK_BOTH if st["layer"] == 0 else PICK_FIRST
                best_halves(b)
                best_pairs(b)
                chosen(st, b)

            def gather(st):
                m0 = st["gather0"] * NT * PSLOTS

                def weigh(t, first, end):
                    with dve.Fori(first, end) as i:
                        for ab in range(2):
                            n = t * PSLOTS + ab * BATCH
                            for q in range(BATCH):
                                dve.wait_ge(u_loaded[q], 16 * ((m0 + n) // BATCH + 1) + 32 * i)
                                v.tensor_tensor_reduce(out=UROWS[:, q, :], in0=UROWS[:, q, :], in1=H[:, t, :], scale=1.0,
                                                       scalar=0.0, op0=ALU.mult, op1=ALU.add,
                                                       accum_out=DOTS[:, ab, q:q + 1]
                                                       ).then_inc(SEM["expert_free"], 1)
                            dve.drain().then_inc(SEM["dots_ready"], 1)
                            dve.wait_ge(SEM["gelu_ready"], at(st, "gelu_ready", n // BATCH + 1) + 2 * i)
                            dve.wait_ge(SEM["diag_ready"], at(st, "diag_ready", t * PSLOTS) + PTOP * i)
                            tt(WEIGHTS[:, ab, :], GELU[:, ab, :], GATE[:, t, bass.ds(i * PTOP + ab * BATCH, BATCH)],
                               ALU.mult).then_inc(SEM["weights_ready"], 1)

                if st["layer"] == 1:
                    weigh(0, 0, LATE[0])
                    best_halves(PICK_LATE)
                    weigh(0, LATE[0], LATE[1])
                    best_pairs(PICK_LATE)
                    weigh(0, LATE[1], LATE[2])
                    chosen(st, PICK_LATE)
                    dve.drain().then_inc(SEM["picked"], 1)
                    weigh(0, LATE[2], PH)
                else:
                    weigh(0, 0, PH)
                weigh(1, 0, PH)
                dve.wait_ge(SEM["mixed"], at(st, "mixed", 1))

            def mix_in(st):
                for t in range(NT):
                    tt(H[:, t, :], PS[:, 2 * t:2 * t + 2, :].rearrange("p a b -> p (a b)"), st["gate"], ALU.mult)
                dve.drain()
                for t in range(NT):
                    tt(X[:, t, :], X[:, t, :], H[:, t, :], ALU.add)

            def stick(st):
                view = lambda b: b.rearrange("p (a b) -> p a b", b=TW)

                def masked(b):
                    for x in (b[:, 0:2 * TW].rearrange("p (h t) -> p h t", t=S)[:, :, 0:P],
                              b[:, 2 * TW:3 * TW].rearrange("p (h t) -> p h t", t=P)):
                        ins = tt(x, x, before[:, :].unsqueeze(1).to_broadcast([P, HG, P]), ALU.mult)
                    return ins

                def take(g):
                    dve.wait_ge(SEM["pv_ready"], at(st, "pv_ready", g + 1))
                    cp(H[:, :, g * 256:(g + 1) * 256], PS[:, 6, :].rearrange("p (t n) -> p t n", t=2)
                       ).then_inc(SEM["pv_taken"], 1)

                def logs(g):
                    z = PS[:, 0:3, :]
                    dve.wait_ge(SEM["soft_ready"], at(st, "soft_ready", g + 1))
                    stt(view(k_lost), z, 0.0, view(k_log), ALU.max, ALU.add)
                    stt(view(k_exp[g % 2]), z, 0.0, view(k_log), ALU.min, ALU.subtract)
                    dve.drain().then_inc(SEM["scores_taken"], 1)
                    masked(k_lost)
                    dve.drain().then_inc(SEM["log_in"], 1)

                logs(0)
                for g in range(SH // HG):
                    x = k_exp[g % 2]
                    dve.wait_ge(SEM["between_ready"], at(st, "between_ready", g + 1))
                    tt(view(x), view(x), PS[:, 3:6, :], ALU.subtract)
                    dve.drain()
                    ts(x, x, 0.0, None, ALU.min).then_inc(SEM["exponent_ready"], 1)
                    if g + 1 < SH // HG:
                        logs(g + 1)
                    dve.wait_ge(SEM["exp_ready"], at(st, "exp_ready", g + 1))
                    masked(k_att[g % 2])
                    dve.drain().then_inc(SEM["probs_ready"], 1)
                    if g:
                        take(g - 1)
                take(SH // HG - 1)

            def softmax(st):
                probs, probT = soft_bufs(st)

                def shifted(g):
                    prob = probs[g % 2]
                    sums, nmax, rsum = (x[g % 2] for x in soft_small(st))
                    dve.wait_ge(SEM["scores_ready"], at(st, "scores_ready", g + 1))
                    early = prob[:, 0:TW].rearrange("p (h n) -> p h n", n=P)
                    late = prob[:, TW:3 * TW].rearrange("p (h n) -> p h n", n=S)
                    tt(early, PS[:, 0, :].rearrange("p (h n) -> p h n", n=P),
                       causal[:, P:S].unsqueeze(1).to_broadcast([P, HG, P]), ALU.add)
                    tt(late, PS[:, 1:3, :].rearrange("p a (h n) -> p (a h) n", n=S),
                       causal[:, :].unsqueeze(1).to_broadcast([P, HG, S]), ALU.add)
                    dve.drain().then_inc(SEM["scores_taken"], 1)
                    v.tensor_reduce(out=nmax[:, 0:HG], in_=early, axis=AX.X, op=ALU.max, negate=True)
                    v.tensor_reduce(out=nmax[:, HG:2 * HG], in_=late, axis=AX.X, op=ALU.max, negate=True)
                    dve.drain().then_inc(SEM["max_ready"], 1)

                shifted(0)
                for g in range(AH // HG):
                    sums, nmax, rsum = (x[g % 2] for x in soft_small(st))
                    if g + 1 < AH // HG:
                        shifted(g + 1)
                    dve.wait_ge(SEM["probsT_ready"], at(st, "probsT_ready", 3 * g + 2))
                    cp(probT[:, TW:2 * TW], PS[:, 4, :]).then_inc(SEM["probsT_taken1"], 1)
                    dve.wait_ge(SEM["exp_ready"], at(st, "exp_ready", g + 1))
                    v.reciprocal(rsum, sums)
                    dve.drain()
                    dve.wait_ge(SEM["pv_ready"], at(st, "pv_ready", g + 1))
                    for t in range(NT):
                        ins = tt(H[:, t, g * 256:(g + 1) * 256].rearrange("p (h n) -> p h n", n=AV),
                                 PS[:, 6, t * 256:(t + 1) * 256].rearrange("p (h n) -> p h n", n=AV),
                                 rsum[:, t * HG:(t + 1) * HG].unsqueeze(2).to_broadcast([P, HG, AV]), ALU.mult)
                    dve.drain().then_inc(SEM["pv_taken"], 1)

            def mla_keys(st):
                for t in range(NT):
                    k = st["k"][:, t, :].rearrange("p (h e) -> p h e", e=MLA_D)
                    cp(k[:, :, 0:NOPE], st["kv"][:, t, :].rearrange("p (h e) -> p h e", e=2 * AV)[:, :, 0:NOPE])
                    cp(k[:, :, NOPE:MLA_D],
                       st["z"][:, t, MLA_Q + MLA_KV:800].unsqueeze(1).to_broadcast([P, AH, ROPE]))

            def rope(st):
                half = ROPE // 2
                dve.wait_ge(inputs_loaded, 16 * 5)
                dve.wait_ge(rope_loaded, 16)
                cp(r_pos, posi[:, :])
                dve.drain()
                ang = r_ang.rearrange("p (c t n) -> p c t n", c=2, n=half)
                turns = r_turn.rearrange("p (c t n) -> p c t n", c=2, n=half)
                for t in range(NT):
                    ts(ang[:, 1, t, :], r_freq, r_pos[:, t:t + 1], None, ALU.mult)
                dve.drain()
                ts(turns[:, 1, :, :], ang[:, 1, :, :], 1.0 / (2 * math.pi), None, ALU.mult)
                dve.drain()
                cp(r_int, r_turn[:, 32:64])
                dve.drain()
                cp(r_turn[:, 32:64], r_int)
                dve.drain()
                big = 6.28125
                stt(ang[:, 1], turns[:, 1], -big, ang[:, 1], ALU.mult, ALU.add)
                dve.drain()
                stt(ang[:, 1], turns[:, 1], -(2 * math.pi - big), ang[:, 1], ALU.mult, ALU.add)
                dve.drain()
                ts(ang[:, 0], ang[:, 1], math.pi / 2, None, ALU.add)
                dve.drain()
                for above, sign in ((ALU.is_gt, -1.0), (ALU.is_lt, 1.0)):
                    ts(r_turn, r_ang, -sign * math.pi, sign * 2 * math.pi, above, ALU.mult)
                    dve.drain()
                    tt(r_ang, r_ang, r_turn, ALU.add)
                    dve.drain()
                ts(r_ang, r_ang, 3.1415925, -3.1415925, ALU.min, ALU.max).then_inc(SEM["angles_ready"], 1)
                dve.wait_ge(SEM["sines_ready"], at(st, "sines_ready", 1))
                cs = r_cs.rearrange("p (c t n) -> p c t n", c=2, n=half)
                tmp = r_tmp.rearrange("p (c h n) -> p c h n", c=4, n=half)
                for x in st["parts"]:
                    for t in range(NT):
                        y = x[:, t, :].rearrange("p (h e) -> p h e", e=MLA_D)
                        x1, x2 = y[:, :, NOPE:NOPE + half], y[:, :, NOPE + half:MLA_D]
                        cos, sin = (cs[:, c, t, :].unsqueeze(1).to_broadcast([P, AH, half]) for c in range(2))
                        for n, (a, b) in enumerate(((x1, cos), (x2, sin), (x1, sin), (x2, cos))):
                            tt(tmp[:, n], a, b, ALU.mult)
                        dve.drain()
                        tt(x1, tmp[:, 0], tmp[:, 1], ALU.subtract)
                        tt(x2, tmp[:, 2], tmp[:, 3], ALU.add)
                        dve.drain()

            def ffn(st):
                def hidden(fb, i):
                    b = fb % 2
                    dve.wait_ge(SEM["hidden_silu"], at(st, "hidden_silu", fb + 1) + 2 * i)
                    tt(f_raw[:, b, :], f_gate[:, b, :], PS[:, b, S:2 * S], ALU.mult
                       ).then_inc(SEM["hidden_raw"], 1)
                    dve.wait_ge(SEM["hidden_hi"], at(st, "hidden_hi", fb + 1) + 2 * i)
                    tt(f_hidden[1][:, b, :], f_raw[:, b, :], f_hidden[0][:, b, :].bitcast(F32), ALU.subtract
                       ).then_inc(SEM["hidden_ready"], 1)

                ffn_schedule(dve, lambda q, i: split_lo(dve, st, q, i), hidden)
                dve.wait_ge(SEM["mixed"], at(st, "mixed", 1))
                for t in range(NT):
                    stt(X[:, t, :], PS[:, 4 + 2 * t:6 + 2 * t, :].rearrange("p a b -> p (a b)"), 0.5, X[:, t, :],
                        ALU.mult, ALU.add)

            parts = dict(ada=ada, norm=norm, linear=linear, linearT=linearT, gates=gates, conv=conv, mlstm=mlstm,
                         headnorm=headnorm, turn=lambda st: taken(st, st["jobs"]), subkeys=subkeys, topk=topk,
                         gather=gather, mix_in=mix_in, stick=stick, softmax=softmax, mla_keys=mla_keys, rope=rope,
                         ffn=ffn)
            for st in STAGES:
                enter(dve, st)
                if st["kind"] in parts:
                    parts[st["kind"]](st)
                leave(dve)


def kernel(**inputs):
    from concourse import bacc
    from concourse.bass_utils import run_bass_kernel_spmd

    a = {k: np.asarray(v) for k, v in inputs.items()}

    def tiles(w, width):
        k, n = w.shape
        w = w.reshape(k // (2 * P), 2, P, n // width, width).transpose(3, 0, 2, 1, 4)
        return np.ascontiguousarray(w.reshape(-1, P, 2 * width))

    def blocks(w):
        return w.reshape(KD, P, -1, P).transpose(2, 1, 0, 3).reshape(-1, P, UNIT)

    def padded(w):
        return blocks(np.pad(w, ((0, 0), (0, P - w.shape[1]))))

    def swiglu(w_in, w_out):
        g, u, down = blocks(w_in[:, :FF]), blocks(w_in[:, FF:]), w_out.reshape(FB, P, D)
        order = [g[0], u[0]]
        for f in range(1, FB):
            order += [g[f], u[f], down[f - 1]]
        return np.stack(order + [down[FB - 1]])

    def tokens(x):
        return np.ascontiguousarray(x.reshape(NT, P, -1).transpose(1, 0, 2))

    def columns(x):
        return np.ascontiguousarray(x.reshape(-1, P).T)

    t = {"x": tokens(a["x"][0]), "c": columns(a["c"][0])}
    for i in range(2):
        t[f"ada_w{i}"] = tiles(a["ada_w"][i], TW) if i == 0 else \
            np.concatenate([tiles(a["ada_w"][i], TW), tiles(a["kv_ada_w"], TW)])
        t[f"ada_b{i}"] = a["ada_b"][i]
        t[f"norm_mix_g{i}"] = a["norm_mix_g"][i]
        t[f"norm_ffn_g{i}"] = a["norm_ffn_g"][i]
        t[f"peer_w_q{i}"] = tiles(a["peer_w_q"][i], TW)
        t[f"sub_keys{i}"] = a["peer_sub_keys"][i].transpose(2, 0, 1).reshape(1, P, 2 * PK)
        t[f"peer_u{i}"] = a["peer_u"][i]
        t[f"peer_v{i}"] = a["peer_v"][i]
        t[f"ffn1_{i}"] = swiglu(a["ffn1_w_in_2"][i], a["ffn1_w_out_2"][i])
        t[f"ffn2_{i}"] = swiglu(a["ffn2_w_in_2"][i], a["ffn2_w_out_2"][i])
        t[f"ple_gate{i}"] = tiles(a["ple_w_gate_2"][i], TW)
        t[f"ple_proj{i}"] = tiles(a["ple_w_proj_2"][i], TW)
        t[f"p{i}"] = tokens(a["p_2"][i, 0])
        t[f"g_ffn1_{i}"] = a["g_ffn1_2"][i]
        t[f"g_mix_{i}"] = a["g_mix_2"][i]
        t[f"g_ffn2_{i}"] = a["g_ffn2_2"][i]
        t[f"g_ple{i}"] = a["g_ple_2"][i]
    w = a["ma_w_in"][0]
    t["ma_w_qk"] = tiles(w[:, :D], TW)
    t["ma_w_vo"] = tiles(w[:, D:3 * D], TW)
    t["ma_w_g"] = np.concatenate([padded(w[:, 3 * D:3 * D + MH]), padded(w[:, 3 * D + MH:])])
    t["ma_b_if"] = a["ma_b_if"][0].reshape(2, MH).T
    t["conv_w"] = a["ma_conv_w"][0].reshape(4, 8, P).transpose(2, 1, 0)
    t["ma_hnorm_g"] = a["ma_hnorm_g"][0].reshape(-1)
    t["ma_w_out"] = tiles(a["ma_w_out"][0], TW)
    t["kv_ada_b"] = a["kv_ada_b"]
    t["kv_norm_g"] = a["kv_norm_g"]
    t["kv_w"] = tiles(a["kv_w"], TW)
    t["k_norm_g"] = a["k_norm_g"]
    t["sb_w_q"] = tiles(a["sb_w_q"][0], TW)
    t["sb_q_norm_g"] = a["sb_q_norm_g"][0]
    t["sb_w_out"] = tiles(a["sb_w_out"][0], TW)
    t["mla_w_in"] = tiles(a["mla_w_in_2"][0], 400)
    t["mla_g_q_lat"] = a["mla_g_q_lat_2"][0]
    t["mla_w_uq"] = tiles(a["mla_w_uq_2"][0], TW)
    t["mla_g_kv_lat"] = a["mla_g_kv_lat_2"][0]
    t["mla_w_ukv"] = tiles(a["mla_w_ukv_2"][0], TW)
    t["mla_g_qn"] = a["mla_g_qn_2"][0]
    t["mla_g_kn"] = a["mla_g_kn_2"][0]
    t["mla_w_o"] = tiles(a["mla_w_o_2"][0], TW)
    w = a["fox_w_in_2"][0]
    t["fox_w_in"] = tiles(w[:, :3 * D], TW)
    t["fox_w_g"] = padded(w[:, 3 * D:])
    t["fox_b_f"] = a["fox_b_f_2"][0].reshape(AH, 1)
    t["fox_g_qn"] = a["fox_g_qn_2"][0]
    t["fox_g_kn"] = a["fox_g_kn_2"][0]
    t["fox_w_o"] = tiles(a["fox_w_o_2"][0], TW)
    t["positions"] = a["positions_2"][0].reshape(NT, P).T
    t["rope_freq"] = (10000.0 ** (-np.arange(0, ROPE, 2, dtype=np.float32) / ROPE)).astype(np.float32)

    nc = bacc.Bacc("TRN2", target_bir_lowering=False, num_devices=1)
    arrays, d = {}, {}
    for name, x in t.items():
        x = np.ascontiguousarray(x)
        arrays["in_" + name] = x
        d[name] = nc.dram_tensor("in_" + name, x.shape, mybir.dt.from_np(x.dtype), kind="ExternalInput").ap()
    d["out"] = nc.dram_tensor("out_0", (P, NT, D), F32, kind="ExternalOutput").ap()
    build(nc, d)
    r = run_bass_kernel_spmd(nc, [arrays], core_ids=[0])
    out = np.asarray(r.results[0]["out_0"])
    return np.ascontiguousarray(out.transpose(1, 0, 2)).reshape(1, S, D)
```
